# Optimizing a Trainium2 kernel written in Bass

```python
import jax, jax.numpy as jnp
from jax import lax
import numpy as np

D_MODEL = 1024
BATCH = 1
SEQ = 256
DEPTH = 2
DEC_BATCH = 8
DEC_SEQ = 1
PAST_LEN = 2048
PAGE_SIZE = 128

POOL_WIDTH = D_MODEL // 2
POOL_WINDOWS = (2, 4, 8, 16)
POOL_GROUPS = len(POOL_WINDOWS)
POOL_GROUP_DIM = POOL_WIDTH // POOL_GROUPS
POOL_BUF = max(POOL_WINDOWS) - 1
RET_HEADS = 8
RET_HEAD_DIM = 64
RET_WIDTH = RET_HEADS * RET_HEAD_DIM
RET_CHUNK = 128
ROPE_THETA = 10000.0
MIX_WIDTH = POOL_WIDTH + RET_WIDTH
IN_WIDTH = POOL_WIDTH + 4 * RET_WIDTH
D_FF = 2816
N_EXPERTS = 8
TOP_K = 2
D_FF_EXPERT = 1408
N_DENSE = (DEPTH + 1) // 2
N_MOE = DEPTH // 2
PLE_DIM = 256
NORM_EPS = 1e-6

kernel_name = "hymba_pool_retention_moe_step"

def rmsnorm(x, g):
    xf = x.astype(jnp.float32)
    y = xf * lax.rsqrt(jnp.mean(xf * xf, axis=-1, keepdims=True) + NORM_EPS)
    return (y * g.astype(jnp.float32)).astype(x.dtype)

def rope(x, pos):
    half = RET_HEAD_DIM // 2
    inv = ROPE_THETA ** (-jnp.arange(half, dtype=jnp.float32) / half)
    ang = pos.astype(jnp.float32)[:, None] * inv[None, :]
    cos = jnp.cos(ang)[None, :, None, :]
    sin = jnp.sin(ang)[None, :, None, :]
    xf = x.astype(jnp.float32)
    x1, x2 = xf[..., :half], xf[..., half:]
    return jnp.concatenate([x1 * cos - x2 * sin, x1 * sin + x2 * cos], axis=-1)

def pool_mixer(u, buf, pos0, w_pool, scale):
    B, L, _ = u.shape
    xp = jnp.concatenate([buf.astype(u.dtype), u], axis=1)
    c = jnp.cumsum(xp.astype(jnp.float32), axis=1)
    c = jnp.pad(c, ((0, 0), (1, 0), (0, 0)))
    end = c[:, POOL_BUF + 1:POOL_BUF + 1 + L]
    pos = pos0 + jnp.arange(L)
    means = []
    for g, w in enumerate(POOL_WINDOWS):
        sl = slice(g * POOL_GROUP_DIM, (g + 1) * POOL_GROUP_DIM)
        s = end[:, :, sl] - c[:, POOL_BUF + 1 - w:POOL_BUF + 1 - w + L, sl]
        cnt = jnp.minimum(pos + 1, w).astype(jnp.float32)[None, :, None]
        means.append(s / cnt)
    mean = jnp.concatenate(means, axis=-1)
    d = (mean - u.astype(jnp.float32)).reshape(B, L, POOL_GROUPS, POOL_GROUP_DIM)
    y = jnp.einsum('blgc,gcd->blgd', d, w_pool.astype(jnp.float32)).reshape(B, L, POOL_WIDTH)
    y = y * scale.astype(jnp.float32)
    return y, xp[:, -POOL_BUF:]

def retention(q, k, v, S0):
    B, L, H, D = q.shape
    C = RET_CHUNK if L % RET_CHUNK == 0 else L
    n = L // C
    log_g = jnp.log1p(-jnp.power(2.0, -5.0 - jnp.arange(H, dtype=jnp.float32)))
    idx = jnp.arange(C, dtype=jnp.float32)
    rel = idx[:, None] - idx[None, :]
    dmask = jnp.where(rel >= 0, jnp.exp(log_g[:, None, None] * jnp.maximum(rel, 0.0)), 0.0)
    xi = jnp.exp(log_g[None, :] * (idx[:, None] + 1.0))
    zeta = jnp.exp(log_g[None, :] * (C - 1.0 - idx)[:, None])
    g_c = jnp.exp(log_g * C)

    def to_chunks(t):
        return t.reshape(B, n, C, H, D).swapaxes(0, 1)

    def step(S, qkv):
        qc, kc, vc = qkv
        sc = jnp.einsum('bnhd,bmhd->bhnm', qc, kc) * dmask[None]
        inner = jnp.einsum('bhnm,bmhe->bnhe', sc, vc)
        cross = jnp.einsum('bnhd,bhde->bnhe', qc, S) * xi[None, :, :, None]
        S = S * g_c[None, :, None, None] + jnp.einsum('bmhd,bmhe->bhde', kc * zeta[None, :, :, None], vc)
        return S, inner + cross

    S, o = lax.scan(step, S0.astype(jnp.float32), (to_chunks(q), to_chunks(k), to_chunks(v)))
    return o.swapaxes(0, 1).reshape(B, L, H, D), S

def mixer(hn, buf, S, pos0, w_in, w_pool, pool_scale, w_o):
    B, L, _ = hn.shape
    z = jnp.einsum('bld,de->ble', hn, w_in)
    u = z[..., :POOL_WIDTH]
    q, k, v, g = jnp.split(z[..., POOL_WIDTH:], 4, axis=-1)
    pos = pos0 + jnp.arange(L)
    q = rope(q.reshape(B, L, RET_HEADS, RET_HEAD_DIM), pos)
    k = rope(k.reshape(B, L, RET_HEADS, RET_HEAD_DIM), pos) * (RET_HEAD_DIM ** -0.5)
    v = v.reshape(B, L, RET_HEADS, RET_HEAD_DIM).astype(jnp.float32)
    o, S_new = retention(q, k, v, S)
    mu = jnp.mean(o, axis=-1, keepdims=True)
    var = jnp.mean(jnp.square(o - mu), axis=-1, keepdims=True)
    o = ((o - mu) * lax.rsqrt(var + NORM_EPS)).reshape(B, L, RET_WIDTH)
    o = o * jax.nn.silu(g.astype(jnp.float32))
    pool_out, buf_new = pool_mixer(u, buf, pos0, w_pool, pool_scale)
    mix = jnp.concatenate([pool_out, o], axis=-1).astype(hn.dtype)
    return jnp.einsum('ble,ed->bld', mix, w_o), buf_new, S_new.astype(S.dtype)

def swiglu(x, wg, wu, wd):
    h = jax.nn.silu(jnp.einsum('bld,df->blf', x, wg)) * jnp.einsum('bld,df->blf', x, wu)
    return jnp.einsum('blf,fd->bld', h, wd)

def moe(x, w_router, wg, wu, wd):
    logits = jnp.einsum('bld,de->ble', x.astype(jnp.float32), w_router.astype(jnp.float32))
    vals, idx = lax.top_k(logits, TOP_K)
    wts = jax.nn.softmax(vals, axis=-1)
    gates = jnp.sum(jax.nn.one_hot(idx, N_EXPERTS, dtype=jnp.float32) * wts[..., None], axis=-2)
    y = jnp.zeros(x.shape, jnp.float32)
    for e in range(N_EXPERTS):
        y = y + gates[..., e:e + 1] * swiglu(x, wg[e], wu[e], wd[e]).astype(jnp.float32)
    return y.astype(x.dtype)

def layer(i, h, p_l, buf, S, pos0, norm1, w_in, w_pool, pool_scale, w_o, norm2,
          ffn_w_gate, ffn_w_up, ffn_w_down, moe_router, moe_w_gate, moe_w_up, moe_w_down,
          w_ple, w_ple_gate):
    mix, buf_new, S_new = mixer(rmsnorm(h, norm1[i]), buf, S, pos0, w_in[i], w_pool[i], pool_scale[i], w_o[i])
    h = h + mix
    hn = rmsnorm(h, norm2[i])
    j = i // 2
    if i % 2 == 0:
        f = swiglu(hn, ffn_w_gate[j], ffn_w_up[j], ffn_w_down[j])
    else:
        f = moe(hn, moe_router[j], moe_w_gate[j], moe_w_up[j], moe_w_down[j])
    h = h + f
    gate = jax.nn.sigmoid(jnp.einsum('bld,de->ble', h, w_ple_gate[i]).astype(jnp.float32))
    e = jnp.einsum('blp,pd->bld', p_l, w_ple[i]).astype(jnp.float32)
    h = h + (gate * e).astype(h.dtype)
    return h, buf_new, S_new

def setup_inputs(seed: int = 0) -> dict:
    key = jax.random.key(seed)
    ks = jax.random.split(key, 24)
    f32 = jnp.float32
    nrm = lambda k, s, sc: jax.random.normal(k, s, f32) * sc
    return {
        "x_prompt": nrm(ks[0], (BATCH, SEQ, D_MODEL), 1.0),
        "x_sample": nrm(ks[1], (DEC_BATCH, DEC_SEQ, D_MODEL), 1.0),
        "state_pool": nrm(ks[2], (DEPTH, DEC_BATCH, POOL_BUF, POOL_WIDTH), 1.0),
        "state_ret": nrm(ks[3], (DEPTH, DEC_BATCH, RET_HEADS, RET_HEAD_DIM, RET_HEAD_DIM), 0.5),
        "p_prompt": nrm(ks[4], (DEPTH, BATCH, SEQ, PLE_DIM), 1.0),
        "p_sample": nrm(ks[5], (DEPTH, DEC_BATCH, DEC_SEQ, PLE_DIM), 1.0),
        "norm1": 1.0 + nrm(ks[6], (DEPTH, D_MODEL), 0.05),
        "w_in": nrm(ks[7], (DEPTH, D_MODEL, IN_WIDTH), D_MODEL ** -0.5),
        "w_pool": nrm(ks[8], (DEPTH, POOL_GROUPS, POOL_GROUP_DIM, POOL_GROUP_DIM), POOL_GROUP_DIM ** -0.5),
        "pool_scale": 1.0 + nrm(ks[9], (DEPTH, POOL_WIDTH), 0.1),
        "w_o": nrm(ks[10], (DEPTH, MIX_WIDTH, D_MODEL), MIX_WIDTH ** -0.5),
        "norm2": 1.0 + nrm(ks[11], (DEPTH, D_MODEL), 0.05),
        "ffn_w_gate": nrm(ks[12], (N_DENSE, D_MODEL, D_FF), D_MODEL ** -0.5),
        "ffn_w_up": nrm(ks[13], (N_DENSE, D_MODEL, D_FF), D_MODEL ** -0.5),
        "ffn_w_down": nrm(ks[14], (N_DENSE, D_FF, D_MODEL), D_FF ** -0.5),
        "moe_router": nrm(ks[15], (N_MOE, D_MODEL, N_EXPERTS), D_MODEL ** -0.5),
        "moe_w_gate": nrm(ks[16], (N_MOE, N_EXPERTS, D_MODEL, D_FF_EXPERT), D_MODEL ** -0.5),
        "moe_w_up": nrm(ks[17], (N_MOE, N_EXPERTS, D_MODEL, D_FF_EXPERT), D_MODEL ** -0.5),
        "moe_w_down": nrm(ks[18], (N_MOE, N_EXPERTS, D_FF_EXPERT, D_MODEL), D_FF_EXPERT ** -0.5),
        "w_ple": nrm(ks[19], (DEPTH, PLE_DIM, D_MODEL), PLE_DIM ** -0.5),
        "w_ple_gate": nrm(ks[20], (DEPTH, D_MODEL, D_MODEL), D_MODEL ** -0.5),
        "final_norm": 1.0 + nrm(ks[21], (D_MODEL,), 0.05),
    }

def reference(x_prompt, x_sample, state_pool, state_ret, p_prompt, p_sample, norm1, w_in, w_pool,
              pool_scale, w_o, norm2, ffn_w_gate, ffn_w_up, ffn_w_down, moe_router, moe_w_gate,
              moe_w_up, moe_w_down, w_ple, w_ple_gate, final_norm):
    hp, hs = x_prompt, x_sample
    Bp = x_prompt.shape[0]
    pool_p, ret_p, pool_s, ret_s = [], [], [], []
    for i in range(DEPTH):
        buf0 = jnp.zeros((Bp, POOL_BUF, POOL_WIDTH), x_prompt.dtype)
        S0 = jnp.zeros((Bp, RET_HEADS, RET_HEAD_DIM, RET_HEAD_DIM), x_prompt.dtype)
        hp, bp, sp = layer(i, hp, p_prompt[i], buf0, S0, 0, norm1, w_in, w_pool, pool_scale, w_o, norm2,
                           ffn_w_gate, ffn_w_up, ffn_w_down, moe_router, moe_w_gate, moe_w_up, moe_w_down,
                           w_ple, w_ple_gate)
        hs, bs, ss = layer(i, hs, p_sample[i], state_pool[i], state_ret[i], PAST_LEN, norm1, w_in, w_pool,
                           pool_scale, w_o, norm2, ffn_w_gate, ffn_w_up, ffn_w_down, moe_router, moe_w_gate,
                           moe_w_up, moe_w_down, w_ple, w_ple_gate)
        pool_p.append(bp); ret_p.append(sp); pool_s.append(bs); ret_s.append(ss)
    y_prompt = rmsnorm(hp, final_norm)
    y_sample = rmsnorm(hs, final_norm)
    return (y_prompt, y_sample, jnp.stack(pool_p), jnp.stack(ret_p), jnp.stack(pool_s), jnp.stack(ret_s))


_drawn_inputs = setup_inputs


def setup_inputs(seed=0):
    import zlib

    import numpy as np

    out = dict(_drawn_inputs(seed))
    spreads = {}
    factors = {}
    for name, (base, spread) in spreads.items():
        noise = np.random.default_rng([zlib.crc32(name.encode()), seed]).standard_normal(out[name].shape)
        drawn = base * np.exp(spread * noise) if base else spread * noise
        out[name] = __import__('jax').numpy.asarray(drawn.astype(out[name].dtype))
    for name, factor in factors.items():
        out[name] = (out[name] * factor).astype(out[name].dtype)
    return out
```

```python
from contextlib import ExitStack

import numpy as np

import concourse.bass as bass
from concourse import mybir

F32 = mybir.dt.float32
F32R = mybir.dt.float32r
I32 = mybir.dt.int32
ALU = mybir.AluOpType
ACT = mybir.ActivationFunctionType
AX_X = mybir.AxisListType.X

P = 128
D = 1024
DC = D // P
NP = 256
NS = 8
T = NP + NS
DEPTH = 2
POOL_W = 512
PC = POOL_W // P
WINDOWS = (2, 4, 8, 16)
BUF = 15
HEADS, HD = 8, 64
RC = 512 // P
IN_W = POOL_W + 4 * 512
FF = 2816
NE = 8
FE = 1408
PLE = 256
EPS = 1e-6
PAST = 2048
CH = 128
PAD = 16

RAW = 4
SPL = 4
UNIT = 2048
AHEAD = 2

CONST = {}
_at = 0
for _name, _n in (("ident", P), ("rot", P), ("mean", P), ("hmean", P),
                  ("cos", T), ("sin", T), ("decay", 2 * RC * CH), ("xi", RC * CH), ("zeta", HEADS),
                  ("gchunk", RC), ("gamma", RC), ("early", PC * PAD), ("wsel", PC * NS),
                  ("tie", NE), ("eps", 1)):
    CONST[_name] = (_at, _n)
    _at += _n
NCONST = _at


def constants():
    f = np.float32
    c = np.zeros((P, NCONST), f)

    def put(name, v):
        a, n = CONST[name]
        c[:v.shape[0], a:a + n] = v.reshape(v.shape[0], n)

    p = np.arange(P)
    put("ident", np.eye(P, dtype=f))
    rot = np.zeros((P, P), f)
    for m in range(P):
        if m % HD < HD // 2:
            rot[m + HD // 2, m] = -1.0
        else:
            rot[m - HD // 2, m] = 1.0
    put("rot", rot)
    put("mean", np.full((P, P), 1.0 / D, f))
    put("hmean", np.where(p[:, None] // HD == p[None, :] // HD, f(1.0 / HD), f(0)))
    half = HD // 2
    inv = f(10000.0) ** (-np.arange(half, dtype=f) / f(half))
    pos = np.concatenate([np.arange(NP), np.full(NS, PAST)]).astype(f)
    ang = (pos[None, :] * inv[p % half][:, None]).astype(f)
    put("cos", np.cos(ang).astype(f))
    put("sin", np.sin(ang).astype(f))
    log_g = np.log1p(-np.power(f(2), -5 - np.arange(HEADS, dtype=f))).astype(f)
    i = np.arange(CH, dtype=f)
    rel = i[None, :] - i[:, None]
    dec = np.zeros((P, 2, RC, CH), f)
    for h in range(HEADS):
        dec[:, h % 2, h // 2] = np.where(rel >= 0, np.exp(log_g[h] * np.maximum(rel, 0)), 0)
    put("decay", dec)
    own = 2 * np.arange(RC)[None, :] + (p[:, None] // HD)
    put("xi", np.exp(log_g[own][:, :, None] * (i + 1)[None, None, :]).astype(f))
    put("zeta", np.exp(log_g[None, :] * (CH - 1 - i)[:, None]).astype(f))
    put("gchunk", np.exp(log_g[own] * CH).astype(f))
    put("gamma", np.exp(log_g[own]).astype(f))
    early = np.ones((P, PC, PAD), f)
    for g, w in enumerate(WINDOWS):
        early[:, g] = w / np.minimum(np.arange(PAD) + 1, w)
    put("early", early)
    wsel = np.zeros((NS * BUF, PC, NS), f)
    for g, w in enumerate(WINDOWS):
        for b in range(NS):
            wsel[b * BUF + BUF - (w - 1):(b + 1) * BUF, g, b] = 1
    put("wsel", wsel)
    put("tie", np.broadcast_to(NE - np.arange(NE, dtype=f), (P, NE)))
    put("eps", np.full((P, 1), EPS, f))
    return c


def sample_rows():
    z = np.zeros((64, NS, P), np.float32)
    for b in range(NS):
        z[b, b, 0:HD] = 1
        z[32 + b, b, HD:P] = 1
    return z


Z_ORDER = ((512, "q"), (1024, "k"), (1536, "v"), (0, "u"), (2048, "g"))
W_IN = [("w_in", 0, DC, at + 256 * j, 256) for at, _ in Z_ORDER for j in range(2)]
W_O = [("w_o", 0, DC, 256 * j, 256) for j in range(4)]
PLEU = [("w_ple", 0, 2, 0, D)] + [("w_ple_gate", 0, DC, 256 * j, 256) for j in range(4)]

EC = FE // P
GROUPS = (EC + 1) // 2


def part_units():
    out, chunks, full = [], 0, 0
    for i in range(GROUPS):
        w = min(2, EC - 2 * i)
        for kind in ("gate", "up"):
            out.append((kind, 2 * i, w, chunks, full))
            chunks += w
            full += w - 1
    for m in range(DC):
        out.append(("down", m, 1, chunks, full))
        chunks += 1
    return out, chunks, full


PART, PART_CHUNKS, PART_FULL = part_units()
PART_UNITS = len(PART)
STEP_UNITS, STEP_CHUNKS, STEP_FULL = 2 * PART_UNITS, 2 * PART_CHUNKS, 2 * PART_FULL
assert STEP_UNITS % RAW == 0 and STEP_UNITS % SPL == 0 and STEP_CHUNKS % 4 == 0
assert FF == 2 * FE
FF_STEPS = (1, NE // 2)

PLE_FULL = DC - 1 + 4
U_MIX, A_MIX, F_MIX = [0], [0], [0]
U_WO, U_FF, U_PLE, A_WO, A_FF, A_PLE, F_FF = [], [], [], [], [], [], []
for _l in range(DEPTH):
    U_WO.append(U_MIX[_l] + len(W_IN))
    U_FF.append(U_WO[_l] + len(W_O))
    U_PLE.append(U_FF[_l] + STEP_UNITS * FF_STEPS[_l])
    U_MIX.append(U_PLE[_l] + len(PLEU))
    A_WO.append(A_MIX[_l] + 2 * len(W_IN))
    A_FF.append(A_WO[_l] + 2 * len(W_O))
    A_PLE.append(A_FF[_l] + STEP_CHUNKS * FF_STEPS[_l])
    A_MIX.append(A_PLE[_l] + 2 * DC)
    F_FF.append(F_MIX[_l] + len(W_IN) + len(W_O))
    F_MIX.append(F_FF[_l] + STEP_FULL * FF_STEPS[_l] + PLE_FULL)
N_UNITS = U_MIX[DEPTH]


def chunk_table():
    table, count = {}, 0

    def unit(u, chunks):
        nonlocal count
        for n in chunks[:-1]:
            count += 1
            table[n] = (False, count)
        table[chunks[-1]] = (True, u + 1)

    for l in range(DEPTH):
        for j in range(len(W_IN)):
            unit(U_MIX[l] + j, [A_MIX[l] + 2 * j, A_MIX[l] + 2 * j + 1])
        for j in range(len(W_O)):
            unit(U_WO[l] + j, [A_WO[l] + 2 * j, A_WO[l] + 2 * j + 1])
        assert count == F_FF[l]
        count += STEP_FULL * FF_STEPS[l]
        unit(U_PLE[l], [A_PLE[l] + m for m in range(DC)])
        for j in range(4):
            unit(U_PLE[l] + 1 + j, [A_PLE[l] + 8 + 2 * j, A_PLE[l] + 9 + 2 * j])
    return table


CHUNK_FULL = chunk_table()

PARTS_AT = {0: 0, 1: 8, 2: 16, 3: 24, 4: 32, 5: 40}
SQUARES_AT = {0: 0, 1: 8, 3: 16, 4: 24, 6: 32}
GAIN = {0: 0, 1: 2, 3: 1, 4: 3}
NORM_STAGE = {(0, "norm1"): 0, (0, "norm2"): 1, (1, "norm1"): 3, (1, "norm2"): 4, (2, "norm1"): 6}
NORM_ORDER = {k: i for i, k in enumerate(NORM_STAGE)}

AFTER = [["norm1"], [], [f"rq{c}" for c in range(RC)], [], [f"rk{c}" for c in range(RC)], [],
         ["kt0", "kt1", "vt0", "vt1"], ["vs", "sc00", "sc01", "o0", "win"],
         ["sc10", "sc11", "S1", "S2", "bc0", "bc1"],
         ["bc2", "bc3", "o1", "qS", "tail", "wp0", "wp1", "wp2", "wp3"],
         [f"mu{c}" for c in range(RC)] + [f"va{c}" for c in range(RC)]]
LAST = (["norm2"], ["norm2", "rt", "lg"] + [f"gb{e}" for e in range(NE)])
SIDE = {}
_at = 0
for _l in range(DEPTH):
    for _group in AFTER + [LAST[_l]]:
        for _s in _group:
            SIDE[_l, _s] = _at
            _at += 1
SIDE[DEPTH, "norm1"] = _at


def program(nc, t):
    with ExitStack() as ctx:
        at = [16512]

        def place(name, shape, dt=F32, offset=None):
            n = 4 * int(np.prod(shape[1:]))
            if offset is None:
                offset = at[0]
                at[0] += (n + 31) // 32 * 32
            return nc.alloc_sbuf_tensor_at(name, list(shape), dt, offset=offset)

        def sem(name):
            return ctx.enter_context(nc.semaphore(name))

        const = place("const", [P, NCONST])
        raw = [place(f"raw{i}", [P, UNIT]) for i in range(RAW)]
        whi = [place(f"whi{i}", [P, UNIT], F32R) for i in range(SPL)]
        wlo = [place(f"wlo{i}", [P, UNIT], F32R) for i in range(SPL)]
        h = place("h", [P, DC, T])
        x_at, ple_at = at[0], at[0] + 8 * DC * T
        xh = place("xh", [P, DC, T], F32R)
        xl = place("xl", [P, DC, T], F32R)
        ph = place("ph", [P, 2, T], F32R)
        pl = place("pl", [P, 2, T], F32R)
        selb = place("selb", [64, NS, P], F32, ple_at)
        gains = place("gains", [P, 5, DC])
        pscale = place("pscale", [P, DEPTH, PC])
        ssum = place("ssum", [P, T])
        sq = place("sq", [P, 2, T])
        std = place("std", [P, T])
        rstd = place("rstd", [P, T])
        rstd8 = place("rstd8", [P, T])
        wr = place("wr", [P, DC, NE])
        r = {n: place("r_" + n, [P, 3, NE]) for n in ("lg", "eq", "key", "one", "two", "lg2", "gate", "t2")}
        rs = place("rs", [P, 3])
        m1, m2, kx, dm, w1, w2 = (place(n, [P, 3]) for n in ("m1", "m2", "kx", "dm", "w1", "w2"))
        arena = at[0]
        qk = place("qk", [P, 2, RC, T])
        wsum_at = at[0]
        wsum = place("wsum", [P, PC, PAD + T])
        v = place("v", [P, RC, T], F32, wsum_at)
        sg = place("sg", [P, RC, T])
        upad = place("upad", [P, PC, PAD + T])
        sbd = place("sbd", [P, RC, P])
        o = place("o", [P, RC, T])
        S = place("S", [P, NS, RC, HD])
        kv_at = at[0]
        kv = place("kv", [P, 2, 2, RC, HD])
        rt = place("rt", [P, 2, T], F32, kv_at)
        buf = place("buf", [NS * BUF, POOL_W])
        utail = place("utail", [BUF + NS, POOL_W], F32, kv_at)
        s2 = place("s2", [P, RC, HD])
        vs2 = place("vs2", [64, RC, HD])
        qm = place("qm", [P, NS, RC, 2])
        wpool = place("wpool", [P, PC, P])
        pin = place("pin", [P, 2, T])
        mix_at = at[0]
        mh = place("mh", [P, DC, T], F32R)
        ml = place("ml", [P, DC, T], F32R)
        assert at[0] <= 229344, at[0]
        kz = place("kz", [P, 2, 512], F32, mix_at)
        vpad = place("vpad", [P, 2, RC, 3, HD], F32, mix_at + 4096)
        sc = place("sc", [P, 2, RC, CH], F32, mix_at + 4096 + 6144)
        qxi = place("qxi", [P, RC, CH], F32, mix_at + 4096 + 6144 + 4096)
        oc = place("oc", [P, RC, T], F32, x_at)
        osq = place("osq", [P, RC, T], F32, x_at + 4 * RC * T)
        og = place("og", [P, RC, T], F32, x_at + 8 * RC * T)
        stdv = place("stdv", [P, 2, T], F32, x_at + 12 * RC * T)
        fh = place("fh", [P, EC, T], F32R, arena)
        fl = place("fl", [P, EC, T], F32R, arena + 4 * EC * T)
        rg = place("rg", [P, NE, T], F32, arena + 8 * EC * T)
        rge = place("rge", [P, 2, T], F32, arena + 4 * (2 * EC + NE) * T)
        assert arena + 4 * (2 * EC + NE + 2) * T <= mix_at
        tg = place("tg", [P, 2, T], F32, mix_at)
        hv = place("hv", [P, 2, T], F32, mix_at + 8 * T)
        esb = place("esb", [P, DC, T], F32, arena)
        sgp = place("sgp", [P, 2, T], F32, arena + 4 * DC * T)
        bank = [ctx.enter_context(nc.psum_tensor(f"bank{i}", [P, 512], F32)) for i in range(8)]

        raw_landed = [sem(f"raw_landed{i}") for i in range(RAW)]
        hi_ready, lo_ready, unit_used = sem("hi_ready"), sem("lo_ready"), sem("unit_used")
        base_in, layer_in = sem("base_in"), sem("layer_in")
        pool_kept, state_out, y_out = sem("pool_kept"), sem("state_out"), sem("y_out")
        acc_full, acc_free = sem("acc_full"), sem("acc_free")
        side_full, side_free = sem("side_full"), sem("side_free")
        part_hi, part_lo, sq_ready, ss_added = sem("part_hi"), sem("part_lo"), sem("sq_ready"), sem("ss_added")
        std_ready = sem("std_ready")
        zeroed, cosed, roped, silu_g = sem("zeroed"), sem("cosed"), sem("roped"), sem("silu_g")
        s_decayed, s_ready, qm_ready = sem("s_decayed"), sem("s_ready"), sem("qm_ready")
        qxi_ready, wsummed, d_ready = sem("qxi_ready"), sem("wsummed"), sem("d_ready")
        osq_ready, og_ready, stdv_ready = sem("osq_ready"), sem("og_ready"), sem("stdv_ready")
        s2_ready = sem("s2_ready")
        on_ready, mix_hi, mix_lo = sem("on_ready"), sem("mix_hi"), sem("mix_lo")
        silu_f, scaled_f, f_hi, f_lo = sem("silu_f"), sem("scaled_f"), sem("f_hi"), sem("f_lo")
        ple_hi, ple_lo, gate_ready, ge_ready = sem("ple_hi"), sem("ple_lo"), sem("gate_ready"), sem("ge_ready")
        moe_zeroed, wr_ready, rowstd = sem("moe_zeroed"), sem("wr_ready"), sem("rowstd")
        dm_ready, sig_ready, routed, y_ready = sem("dm_ready"), sem("sig_ready"), sem("routed"), sem("y_ready")
        rge_ready = sem("rge_ready")
        dve_step, pool_step = sem("dve_step"), sem("pool_step")

        def C(name, rows=P):
            a, n = CONST[name]
            return const[0:rows, a:a + n]

        ident, rot, mean = C("ident"), C("rot"), C("mean")
        decay = C("decay").rearrange("p (a c n) -> p a c n", a=2, c=RC)
        xi = C("xi").rearrange("p (c n) -> p c n", c=RC)
        wsel = C("wsel", NS * BUF).rearrange("p (g b) -> p g b", g=PC)
        BLK = ((0, P), (1, P), (2, NS))

        def chunk_full(eng, n):
            by_unit, count = CHUNK_FULL[n]
            eng.wait_ge(unit_used if by_unit else acc_full, count)

        def h_final(eng, stage, m):
            if stage == 0:
                eng.wait_ge(base_in, 80)
            else:
                first = {1: A_WO[0], 2: A_PLE[0] - DC, 3: A_PLE[0] + DC, 4: A_WO[1], 5: A_PLE[1] - DC,
                         6: A_PLE[1] + DC}[stage]
                eng.wait_ge(acc_free, first + m + 1)

        part_cols = [(DC if kind != "down" else EC) * w * P for kind, _, w, _, _ in PART]
        cols = {}
        for l in range(DEPTH):
            for first, specs in ((U_MIX[l], W_IN), (U_WO[l], W_O), (U_PLE[l], PLEU)):
                cols |= {first + j: x[2] * x[4] for j, x in enumerate(specs)}
            cols |= {U_FF[l] + j: part_cols[j] for j in range(AHEAD)}
            assert all(cols[U_PLE[l] + j] == part_cols[j] for j in range(AHEAD))

        class Count:

            def __init__(self, l, p, half):
                steps = sum(FF_STEPS[:l])
                self.p = p
                self.unit_at = U_FF[l] + half * PART_UNITS
                self.chunk_at = A_FF[l] + half * PART_CHUNKS
                self.unit = p * STEP_UNITS + self.unit_at
                self.chunk = p * STEP_CHUNKS + self.chunk_at
                self.full = p * STEP_FULL + (F_FF[l] + half * PART_FULL)
                self.hidden = p * (2 * EC) + (2 * EC * steps + half * EC)

        block = ctx.enter_context(nc.Block())

        @block.sync
        def _(sp):
            def load(slot, vector_through, src, n, w):
                if vector_through is not None:
                    sp.wait_ge(lo_ready, vector_through)
                dst = raw[slot][:, 0:n * w].rearrange("p (k w) -> p k w", k=n)
                sp.dma_start(dst, src.rearrange("(k p) w -> p k w", p=P)).then_inc(raw_landed[slot], 16)

            def dense(layer, first, specs):
                for j, (name, k0, n, c0, w) in enumerate(specs):
                    u = first + j
                    m = t[name][layer]
                    load(u % RAW, u - RAW + 1 if u >= RAW else None, m[k0 * P:(k0 + n) * P, c0:c0 + w], n, w)

            def feed_forward(l, p):
                for half in range(2):
                    n = Count(l, p, half)
                    if l:
                        e = p * 2 + half
                        gate, up, down = (t[name][0][bass.ds(e, 1)].rearrange("a k w -> (a k) w")
                                          for name in ("moe_w_gate", "moe_w_up", "moe_w_down"))
                    else:
                        own = slice(half * FE, (half + 1) * FE)
                        gate, up, down = t["ffn_w_gate"][0][:, own], t["ffn_w_up"][0][:, own], t["ffn_w_down"][0][own, :]
                    for i, (kind, c, w, _, _) in enumerate(PART):
                        src = {"gate": gate, "up": up, "down": down}[kind]
                        load((n.unit_at + i) % RAW, n.unit + (i - RAW + 1), src[:, c * P:(c + w) * P],
                             EC if kind == "down" else DC, w * P)

            sp.dma_start(h[:, :, :], t["x"]).then_inc(base_in, 16)
            sp.dma_start(gains[:, :, :], t["gains"]).then_inc(base_in, 16)
            sp.dma_start(const[:, :], t["const"]).then_inc(base_in, 16)
            sp.dma_start(pscale[:, :, :], t["pscale"]).then_inc(base_in, 16)
            sp.dma_start(wr[:, :, :], t["moe_router"][0].rearrange("(c p) e -> p c e", p=P)).then_inc(base_in, 16)
            dense(0, U_MIX[0], W_IN)
            dense(0, U_WO[0], W_O)
            feed_forward(0, 0)
            dense(0, U_PLE[0], PLEU)
            dense(1, U_MIX[1], W_IN)
            dense(1, U_WO[1], W_O)
            with sp.Fori(0, FF_STEPS[1]) as p:
                feed_forward(1, p)
            dense(1, U_PLE[1], PLEU)
            for j in range(4):
                sp.wait_ge(y_ready, 2 * j + 2)
                sp.dma_start(t["y"][:, 2 * j:2 * j + 2, :], h[:, 2 * j:2 * j + 2, :]).then_inc(y_out, 16)
            sp.wait_ge(y_out, 64)

        @block.tensor
        def _(pe):
            def weights_first(out, w_hi, w_lo, x_hi, x_lo, start, stop):
                pe.matmul(out, w_hi, x_hi, start=start, stop=False)
                pe.matmul(out, w_hi, x_lo, start=False, stop=False)
                return pe.matmul(out, w_lo, x_hi, start=False, stop=stop)

            def chunk(at, n, u, k, w, m, xhi, xlo, row_ready=None):
                if at >= 4:
                    pe.wait_ge(acc_free, n - 3)
                out = bank[at % 4][:, 0:T]
                H = whi[u % SPL][:, 0:k * w].rearrange("p (k w) -> p k w", k=k)
                L = wlo[u % SPL][:, 0:k * w].rearrange("p (k w) -> p k w", k=k)
                for kc in range(k):
                    if row_ready is not None:
                        pe.wait_ge(f_lo, row_ready + (kc + 1))
                    mm = weights_first(out, H[:, kc, m * P:(m + 1) * P], L[:, kc, m * P:(m + 1) * P],
                                       xhi[:, kc, :], xlo[:, kc, :], kc == 0, kc == k - 1)
                return mm

            def pair(u, n, xhi, xlo):
                pe.wait_ge(lo_ready, u + 1)
                chunk(n, n, u, DC, 256, 0, xhi, xlo).then_inc(acc_full, 1)
                chunk(n + 1, n + 1, u, DC, 256, 1, xhi, xlo).then_inc(unit_used, 1)

            def feed_forward(l, p):
                for half in range(2):
                    n = Count(l, p, half)
                    for i, (kind, _, w, a, _) in enumerate(PART):
                        pe.wait_ge(lo_ready, n.unit + (i + 1))
                        for m in range(w):
                            down = kind == "down"
                            mm = chunk(n.chunk_at + a + m, n.chunk + (a + m), n.unit_at + i, EC if down else DC, w * P, m,
                                       fh if down else xh, fl if down else xl,
                                       n.hidden if i == 2 * GROUPS else None)
                            mm.then_inc(acc_full if m < w - 1 else unit_used, 1)

            def side_step(l, name):
                i = SIDE[l, name]
                if i >= 4:
                    pe.wait_ge(side_free, i - 3)
                b = bank[4 + i % 4]
                if name in ("norm1", "norm2"):
                    pe.wait_ge(ss_added, SQUARES_AT[NORM_STAGE[l, name]] + DC)
                    mm = pe.matmul(b[:, 0:T], mean, ssum[:, :], start=True, stop=True)
                elif name[:2] in ("rq", "rk"):
                    a, c = int(name[1] == "k"), int(name[2])
                    pe.wait_ge(acc_free, A_MIX[l] + 4 * a + c + 1)
                    mm = pe.matmul(b[:, 0:T], rot, qk[:, a, c, :], start=True, stop=True)
                elif name[:2] in ("kt", "vt"):
                    blk = int(name[2])
                    if name[0] == "k":
                        pe.wait_ge(roped, 8 * (l + 1))
                    else:
                        pe.wait_ge(acc_free, A_MIX[l] + 12)
                    for c in range(RC):
                        src = qk[:, 1, c, :] if name[0] == "k" else v[:, c, :]
                        mm = pe.transpose(b[:, c * P:(c + 1) * P], src[:, blk * CH:(blk + 1) * CH], ident)
                elif name == "vs":
                    for c in range(RC):
                        mm = pe.transpose(b[0:NS, c * P:(c + 1) * P], v[:, c, NP:T], ident)
                elif name[:2] == "sc":
                    blk, hp = int(name[2]) * CH, int(name[3])
                    rows = slice(hp * HD, (hp + 1) * HD)
                    for c in range(RC):
                        mm = pe.matmul(b[:, c * CH:(c + 1) * CH], qk[rows, 1, c, blk:blk + CH],
                                       qk[rows, 0, c, blk:blk + CH], start=True, stop=True)
                elif name == "win":
                    pe.wait_ge(layer_in, 80 * (l + 1))
                    for g in range(PC):
                        mm = pe.matmul(b[:, g * NS:(g + 1) * NS], buf[:, g * P:(g + 1) * P], wsel[:, g, :],
                                       start=True, stop=True)
                elif name in ("S1", "S2"):
                    blk = int(name == "S2")
                    pe.wait_ge(side_free, SIDE[l, "vt1"] + 1)
                    for c in range(RC):
                        mm = pe.matmul(b[:, c * P:(c + 1) * P], kz[:, blk, c * P:(c + 1) * P],
                                       vpad[:, blk, c, 0:3:2, :], start=True, stop=True)
                elif name in ("o0", "o1"):
                    blk = int(name[1])
                    pe.wait_ge(side_free, SIDE[l, f"sc{blk}1"] + 1)
                    pe.wait_ge(zeroed, 5 * (l + 1))
                    if blk:
                        pe.wait_ge(side_free, SIDE[l, "S1"] + 1)
                        pe.wait_ge(qxi_ready, l + 1)
                    for c in range(RC):
                        out = b[:, c * CH:(c + 1) * CH]
                        vc = vpad[:, blk, c, :, :].rearrange("p a e -> p (a e)")
                        pe.matmul(out, vc[:, 0:P], sc[:, 0, c, :], start=True, stop=False)
                        mm = pe.matmul(out, vc[:, HD:HD + P], sc[:, 1, c, :], start=False, stop=not blk)
                        if blk:
                            mm = pe.matmul(out, sbd[:, c, :], qxi[:, c, :], start=False, stop=True)
                elif name[:2] == "bc":
                    pe.wait_ge(side_free, SIDE[l, "vs"] + 1)
                    pe.wait_ge(layer_in, 80 * (l + 1))
                    for a in range(2):
                        mm = pe.matmul(b[:, a * 256:(a + 1) * 256], selb[:, 2 * int(name[2]) + a, :],
                                       vs2[:, :, :].rearrange("p c e -> p (c e)"), start=True, stop=True)
                elif name == "qS":
                    pe.wait_ge(s_ready, 4 * (l + 1))
                    pe.wait_ge(qm_ready, 2 * (l + 1))
                    for s in range(NS):
                        for c in range(RC):
                            a = 2 * (s * RC + c)
                            mm = pe.matmul(b[0:HD, a:a + 2], S[:, s, c, :], qm[:, s, c, :], start=True, stop=True)
                elif name == "tail":
                    pe.wait_ge(acc_free, A_MIX[l] + 16)
                    for g in range(PC):
                        mm = pe.transpose(b[0:BUF + NS, g * P:(g + 1) * P], upad[:, g, PAD + NP - BUF:PAD + T], ident)
                elif name[:2] == "wp":
                    g = int(name[2])
                    pe.wait_ge(d_ready, PC * l + g + 1)
                    mm = pe.matmul(b[:, 0:T], wpool[:, g, :], wsum[:, g, PAD:PAD + T], start=True, stop=True)
                elif name[:2] == "mu":
                    pe.wait_ge(side_free, SIDE[l, "qS"] + 1)
                    mm = pe.matmul(b[:, 0:T], C("hmean"), o[:, int(name[2]), :], start=True, stop=True)
                elif name[:2] == "va":
                    pe.wait_ge(osq_ready, RC * l + int(name[2]) + 1)
                    mm = pe.matmul(b[:, 0:T], C("hmean"), osq[:, int(name[2]), :], start=True, stop=True)
                elif name == "rt":
                    pe.wait_ge(ss_added, SQUARES_AT[4] + DC)
                    for j, w in BLK:
                        mm = pe.matmul(b[0:w, j:j + 1], ssum[:, j * P:j * P + w], mean[:, 0:1], start=True, stop=True)
                elif name == "lg":
                    pe.wait_ge(wr_ready, 1)
                    for j, w in BLK:
                        for c in range(DC):
                            mm = pe.matmul(b[0:w, j * NE:(j + 1) * NE], h[:, c, j * P:j * P + w], wr[:, c, :],
                                           start=(c == 0), stop=(c == DC - 1))
                elif name[:2] == "gb":
                    pe.wait_ge(routed, 1)
                    e = int(name[2])
                    for j, w in BLK:
                        mm = pe.matmul(b[:, j * P:j * P + w], r["gate"][0:w, j, e:e + 1].to_broadcast([w, P]),
                                       ident[0:w, 0:w], start=True, stop=True)
                mm.then_inc(side_full, 1)

            pe.wait_ge(base_in, 80)
            for l in range(DEPTH):
                for j in range(10):
                    if j == 0:
                        pe.wait_ge(part_lo, PARTS_AT[3 * l] + DC)
                    pair(U_MIX[l] + j, A_MIX[l] + 2 * j, xh, xl)
                    for name in AFTER[j]:
                        side_step(l, name)
                for name in AFTER[10]:
                    side_step(l, name)
                pe.wait_ge(side_free, SIDE[l, "wp3"] + 1)
                pe.wait_ge(mix_lo, RC * (l + 1))
                for j in range(4):
                    pair(U_WO[l] + j, A_WO[l] + 2 * j, mh, ml)
                for name in LAST[l]:
                    side_step(l, name)
                pe.wait_ge(part_lo, PARTS_AT[4 if l else 1] + DC)
                if l:
                    with pe.Fori(0, FF_STEPS[1]) as p:
                        feed_forward(1, p)
                else:
                    feed_forward(0, 0)
                u = U_PLE[l]
                pe.wait_ge(lo_ready, u + 1)
                pe.wait_ge(ple_lo, l + 1)
                for m in range(DC):
                    chunk(A_PLE[l] + m, A_PLE[l] + m, u, 2, D, m, ph, pl).then_inc(acc_full if m < DC - 1 else unit_used, 1)
                pe.wait_ge(part_lo, PARTS_AT[5 if l else 2] + DC)
                for j in range(4):
                    pair(U_PLE[l] + 1 + j, A_PLE[l] + 8 + 2 * j, mh, ml)
            side_step(DEPTH, "norm1")

        @block.scalar
        def _(act):
            def hi(off, n, p=None):
                act.wait_ge(raw_landed[off % RAW], 16 * (off // RAW + 1) if p is None else
                            p * (16 * STEP_UNITS // RAW) + 16 * (off // RAW + 1))
                if off >= SPL:
                    act.wait_ge(unit_used, (off if p is None else p * STEP_UNITS + off) - (SPL - 1))
                act.activation(whi[off % SPL][:, 0:n], raw[off % RAW][:, 0:n], ACT.Copy).then_inc(hi_ready, 1)

            def ahead(u):
                if u + AHEAD < N_UNITS:
                    hi(u + AHEAD, cols[u + AHEAD])

            def finish(stage, m):
                h_final(act, stage, m)
                if stage in PARTS_AT:
                    dst = xh if stage in GAIN else mh
                    scale = gains[:, GAIN[stage], m:m + 1] if stage in GAIN else 1.0
                    act.activation(dst[:, m, :], h[:, m, :], ACT.Copy, scale=scale).then_inc(part_hi, 1)
                if stage in SQUARES_AT:
                    n = SQUARES_AT[stage] + m
                    if n >= 2:
                        act.wait_ge(ss_added, n - 1)
                    act.activation(sq[:, n % 2, :], h[:, m, :], ACT.Square).then_inc(sq_ready, 1)

            def norm(l, name):
                act.wait_ge(side_full, SIDE[l, name] + 1)
                i = SIDE[l, name] % 4
                act.activation(std[:, :], bank[4 + i][:, 0:T], ACT.Sqrt, bias=C("eps")).then_inc(std_ready, 1)

            def feed_forward(l, p):
                for half in range(2):
                    n = Count(l, p, half)
                    for i, (kind, c, w, a, _) in enumerate(PART):
                        hi(n.unit_at + i + AHEAD, part_cols[(i + AHEAD) % PART_UNITS], p)
                        for m in range(w):
                            if kind == "gate":
                                act.wait_ge(acc_free, n.chunk + (a + m + 1))
                                act.activation(tg[:, m, :], tg[:, m, :], ACT.Silu).then_inc(silu_f, 1)
                            elif kind == "up":
                                act.wait_ge(acc_free, n.chunk + (a + m + 1))
                                act.activation(fh[:, c + m, :], hv[:, m, :], ACT.Copy).then_inc(f_hi, 1)

            act.wait_ge(base_in, 80)
            for m in range(DC):
                finish(0, m)
                if m == 1:
                    hi(0, cols[0])
                if m == 4:
                    hi(1, cols[1])
            for l in range(DEPTH):
                for j in range(10):
                    ahead(U_MIX[l] + j)
                    if j == 0:
                        norm(l, "norm1")
                    if j >= 8:
                        for c in range(2 * (j - 8), 2 * (j - 8) + 2):
                            act.wait_ge(acc_free, A_MIX[l] + 16 + c + 1)
                            act.activation(sg[:, c, :], sg[:, c, :], ACT.Silu).then_inc(silu_g, 1)
                for g in range(PC):
                    i = SIDE[l, f"wp{g}"]
                    act.wait_ge(side_full, i + 1)
                    act.activation(mh[:, g, :], bank[4 + i % 4][:, 0:T], ACT.Copy,
                                   scale=pscale[:, l, g:g + 1]).then_inc(mix_hi, 1)
                for c in range(RC):
                    act.wait_ge(side_free, SIDE[l, f"mu{c}"] + 1)
                    act.activation(osq[:, c, :], oc[:, c, :], ACT.Square).then_inc(osq_ready, 1)
                for c in range(RC):
                    i = SIDE[l, f"va{c}"]
                    act.wait_ge(side_full, i + 1)
                    if c >= 2:
                        act.wait_ge(on_ready, RC * l + c - 1)
                    act.activation(stdv[:, c % 2, :], bank[4 + i % 4][:, 0:T], ACT.Sqrt,
                                   bias=C("eps")).then_inc(stdv_ready, 1)
                for c in range(RC):
                    act.wait_ge(on_ready, RC * l + c + 1)
                    act.activation(mh[:, PC + c, :], og[:, c, :], ACT.Copy).then_inc(mix_hi, 1)
                act.wait_ge(side_free, SIDE[l, "bc3"] + 1)
                act.activation(ph[:, :, :].rearrange("p a n -> p (a n)"), pin[:, :, :].rearrange("p a n -> p (a n)"),
                               ACT.Copy).then_inc(ple_hi, 1)
                for j in range(4):
                    ahead(U_WO[l] + j)
                    for m in (2 * j, 2 * j + 1):
                        finish(4 if l else 1, m)
                norm(l, "norm2")
                act.wait_ge(state_out, 64 * (l + 1))
                if l:
                    i = SIDE[1, "rt"]
                    act.wait_ge(side_full, i + 1)
                    act.wait_ge(moe_zeroed, 2)
                    act.activation(rs[:, 0:2], bank[4 + i % 4][:, 0:2], ACT.Sqrt, bias=C("eps")).then_inc(rowstd, 1)
                    act.activation(rs[0:NS, 2:3], bank[4 + i % 4][0:NS, 2:3], ACT.Sqrt,
                                   bias=C("eps", NS)).then_inc(rowstd, 1)
                    act.wait_ge(dm_ready, 1)
                    act.activation(w1[:, :], dm[:, :], ACT.Sigmoid)
                    act.activation(w2[:, :], dm[:, :], ACT.Sigmoid, scale=-1.0).then_inc(sig_ready, 1)
                    with act.Fori(0, FF_STEPS[1]) as p:
                        feed_forward(1, p)
                else:
                    feed_forward(0, 0)
                for m in range(DC):
                    finish(5 if l else 2, m)
                ahead(U_PLE[l])
                for j in range(4):
                    ahead(U_PLE[l] + 1 + j)
                    for m in (2 * j, 2 * j + 1):
                        n = A_PLE[l] + 8 + m
                        chunk_full(act, n)
                        if DC * l + m >= 2:
                            act.wait_ge(ge_ready, DC * l + m - 1)
                        act.activation(sgp[:, m % 2, :], bank[n % 4][:, 0:T], ACT.Sigmoid).then_inc(gate_ready, 1)
                    for m in (2 * j, 2 * j + 1):
                        finish(6 if l else 3, m)
            norm(DEPTH, "norm1")

        @block.vector
        def _(dve):
            steps = 0

            def step(ins):
                nonlocal steps
                steps += 1
                ins.then_inc(dve_step, 1)
                dve.wait_ge(dve_step, steps)

            def lo(off, n, u=None):
                u = off if u is None else u
                dve.wait_ge(hi_ready, u + 1)
                dve.tensor_tensor(wlo[off % SPL][:, 0:n], raw[off % RAW][:, 0:n],
                                  whi[off % SPL][:, 0:n].bitcast(F32), ALU.subtract).then_inc(lo_ready, 1)

            def ahead(u):
                if u + AHEAD < N_UNITS:
                    lo(u + AHEAD, cols[u + AHEAD])

            def finish(stage, m):
                n = PARTS_AT[stage] + m
                dve.wait_ge(part_hi, n + 1)
                if stage in GAIN:
                    dve.scalar_tensor_tensor(out=xl[:, m, :], in0=h[:, m, :], scalar=gains[:, GAIN[stage], m:m + 1],
                                             in1=xh[:, m, :].bitcast(F32), op0=ALU.mult,
                                             op1=ALU.subtract).then_inc(part_lo, 1)
                else:
                    dve.tensor_tensor(ml[:, m, :], h[:, m, :], mh[:, m, :].bitcast(F32), ALU.subtract).then_inc(part_lo, 1)

            def feed_forward(l, p):
                for half in range(2):
                    n = Count(l, p, half)
                    for i, (kind, c, w, a, full) in enumerate(PART):
                        j = i + AHEAD
                        lo(n.unit_at + j, part_cols[j % PART_UNITS], n.unit + j)
                        for m in range(w):
                            if m < w - 1:
                                dve.wait_ge(acc_full, n.full + (full + 1))
                            else:
                                dve.wait_ge(unit_used, n.unit + (i + 1))
                            b = bank[(n.chunk_at + a + m) % 4][:, 0:T]
                            if kind == "gate":
                                dve.tensor_tensor(tg[:, m, :], b, rstd[:, :], ALU.mult).then_inc(acc_free, 1)
                            elif kind == "up":
                                dve.wait_ge(scaled_f, n.hidden + (c + m + 1))
                                dve.tensor_tensor(hv[:, m, :], b, tg[:, m, :], ALU.mult).then_inc(acc_free, 1)
                            else:
                                dve.tensor_tensor(h[:, c, :], h[:, c, :], b, ALU.add).then_inc(acc_free, 1)
                        if kind == "up":
                            for m in range(w):
                                dve.wait_ge(f_hi, n.hidden + (c + m + 1))
                                dve.tensor_tensor(fl[:, c + m, :], hv[:, m, :], fh[:, c + m, :].bitcast(F32),
                                                  ALU.subtract).then_inc(f_lo, 1)

            def side(l, name):
                i = SIDE[l, name]
                dve.wait_ge(side_full, i + 1)
                return bank[4 + i % 4]

            def side_step(l, name):
                if name in ("norm1", "norm2"):
                    dve.wait_ge(std_ready, NORM_ORDER[l, name] + 1)
                    step(dve.reciprocal(rstd[:, :], std[:, :]))
                    dve.tensor_scalar(rstd8[:, :], rstd[:, :], float(HD) ** -0.5, None, ALU.mult).then_inc(side_free, 1)
                    dve.wait_ge(side_free, SIDE[l, name] + 1)
                    return
                b = side(l, name)
                if name[:2] in ("rq", "rk"):
                    a, c = int(name[1] == "k"), int(name[2])
                    i = SIDE[l, name]
                    dve.tensor_tensor(rt[:, c % 2, :], b[:, 0:T], C("sin"), ALU.mult).then_inc(side_free, 1)
                    dve.wait_ge(side_free, i + 1)
                    dve.wait_ge(cosed, 8 * l + 4 * a + c + 1)
                    dve.tensor_tensor(qk[:, a, c, :], qk[:, a, c, :], rt[:, c % 2, :], ALU.add).then_inc(roped, 1)
                    return
                if name[:2] == "kt":
                    last = dve.tensor_tensor(kz[:, int(name[2]), :].rearrange("p (a d) -> p a d", a=HEADS),
                                             b[:, :].rearrange("p (a d) -> p a d", a=HEADS),
                                             C("zeta").unsqueeze(2).to_broadcast([P, HEADS, HD]), ALU.mult)
                elif name[:2] == "vt":
                    last = dve.tensor_copy(vpad[:, int(name[2]), :, 0:3:2, :],
                                           b[:, :].rearrange("p (c a e) -> p c a e", c=RC, a=2))
                elif name == "vs":
                    dve.wait_ge(zeroed, 5 * (l + 1))
                    src = b[0:NS, :].rearrange("p (c a e) -> p c a e", c=RC, a=2)
                    dve.tensor_copy(vs2[0:NS, :, :], src[:, :, 0, :])
                    last = dve.tensor_copy(vs2[32:32 + NS, :, :], src[:, :, 1, :])
                elif name[:2] == "sc":
                    hp = int(name[3])
                    last = dve.tensor_tensor(sc[:, hp, :, :], b[:, :].rearrange("p (c n) -> p c n", c=RC),
                                             decay[:, hp, :, :], ALU.mult)
                elif name == "win":
                    last = dve.tensor_tensor(wsum[:, :, PAD + NP:], b[:, 0:PC * NS].rearrange("p (g s) -> p g s", g=PC),
                                             upad[:, :, PAD + NP:], ALU.add)
                elif name == "S1":
                    dve.wait_ge(zeroed, 5 * (l + 1))
                    for hp in range(2):
                        rows = slice(hp * HD, (hp + 1) * HD)
                        last = dve.tensor_copy(sbd[rows, :, rows], b[rows, :].rearrange("p (c n) -> p c n", c=RC)[:, :, rows])
                elif name == "S2":
                    dve.wait_ge(side_free, SIDE[l, "S1"] + 1)
                    for hp in range(2):
                        rows = slice(hp * HD, (hp + 1) * HD)
                        decay_c = C("gchunk")[rows, :].unsqueeze(2).to_broadcast([HD, RC, HD])
                        step(dve.tensor_tensor(s2[rows, :, :], sbd[rows, :, rows], decay_c, ALU.mult))
                        last = dve.tensor_tensor(s2[rows, :, :], s2[rows, :, :],
                                                 b[rows, :].rearrange("p (c n) -> p c n", c=RC)[:, :, rows], ALU.add)
                elif name in ("o0", "o1"):
                    a = int(name[1]) * CH
                    last = dve.tensor_copy(o[:, :, a:a + CH], b[:, :].rearrange("p (c n) -> p c n", c=RC))
                elif name[:2] == "bc":
                    i = int(name[2])
                    if i >= 2:
                        dve.wait_ge(s_ready, 4 * l + i - 1)
                    k = qk[:, 1, :, NP + 2 * i:NP + 2 * i + 2].rearrange("p c s -> p s c")
                    last = dve.tensor_tensor(kv[:, i % 2, :, :, :],
                                             b[:, :].rearrange("p (s c e) -> p s c e", s=2, c=RC),
                                             k.unsqueeze(3).to_broadcast([P, 2, RC, HD]), ALU.mult)
                elif name == "qS":
                    src = b[0:HD, 0:2 * NS * RC].rearrange("p (s c a) -> p a c s", s=NS, c=RC)
                    dve.tensor_copy(o[0:HD, :, NP:T], src[:, 0, :, :])
                    last = dve.tensor_copy(o[HD:P, :, NP:T], src[:, 1, :, :])
                elif name == "tail":
                    last = dve.tensor_copy(utail[:, :], b[0:BUF + NS, :])
                elif name[:2] == "wp":
                    g = int(name[2])
                    dve.wait_ge(mix_hi, 8 * l + g + 1)
                    last = dve.scalar_tensor_tensor(out=ml[:, g, :], in0=b[:, 0:T], scalar=pscale[:, l, g:g + 1],
                                                    in1=mh[:, g, :].bitcast(F32), op0=ALU.mult, op1=ALU.subtract)
                elif name[:2] == "mu":
                    c = int(name[2])
                    if c == 0:
                        dve.wait_ge(side_free, SIDE[l, "qS"] + 1)
                    last = dve.tensor_tensor(oc[:, c, :], o[:, c, :], b[:, 0:T], ALU.subtract)
                elif name[:2] == "va":
                    c = int(name[2])
                    dve.wait_ge(stdv_ready, RC * l + c + 1)
                    dve.reciprocal(stdv[:, c % 2, :], stdv[:, c % 2, :]).then_inc(side_free, 1)
                    dve.wait_ge(side_free, SIDE[l, name] + 1)
                    dve.wait_ge(og_ready, RC * l + c + 1)
                    dve.tensor_tensor(og[:, c, :], og[:, c, :], stdv[:, c % 2, :], ALU.mult).then_inc(on_ready, 1)
                    if c:
                        mix_part(l, c - 1)
                    return
                last.then_inc(side_free, 1)

            def mix_part(l, c):
                dve.wait_ge(mix_hi, 8 * l + PC + c + 1)
                dve.tensor_tensor(ml[:, PC + c, :], og[:, c, :], mh[:, PC + c, :].bitcast(F32),
                                  ALU.subtract).then_inc(mix_lo, 1)

            def z_chunk(l, c):
                n = A_MIX[l] + c
                chunk_full(dve, n)
                part, i = divmod(c, 4)
                dst = (qk[:, 0, i, :], qk[:, 1, i, :], v[:, i, :], upad[:, i, PAD:PAD + T], sg[:, i, :])[part]
                scale = rstd8 if part == 1 else rstd
                dve.tensor_tensor(dst, bank[n % 4][:, 0:T], scale[:, :], ALU.mult).then_inc(acc_free, 1)

            def pool_diff(l, g):
                dve.wait_ge(wsummed, PC * l + g + 1)
                dve.wait_ge(side_free, SIDE[l, "win"] + 1)
                early = C("early").rearrange("p (g n) -> p g n", g=PC)[:, g, :]
                step(dve.tensor_tensor(wsum[:, g, PAD:2 * PAD], wsum[:, g, PAD:2 * PAD], early, ALU.mult))
                dve.scalar_tensor_tensor(out=wsum[:, g, PAD:], in0=wsum[:, g, PAD:], scalar=1.0 / WINDOWS[g],
                                         in1=upad[:, g, PAD:], op0=ALU.mult, op1=ALU.subtract).then_inc(d_ready, 1)

            def add_h(n, m, src=None):
                if src is None:
                    chunk_full(dve, n)
                    src = bank[n % 4][:, 0:T]
                dve.tensor_tensor(h[:, m, :], h[:, m, :], src, ALU.add).then_inc(acc_free, 1)

            def route():
                def bc(x):
                    return x[:, :].unsqueeze(2).to_broadcast([P, 3, NE])

                tie = C("tie").unsqueeze(1).to_broadcast([P, 3, NE])
                b = side(1, "rt")
                dve.wait_ge(rowstd, 2)
                dve.reciprocal(rs[:, :], rs[:, :]).then_inc(side_free, 1)
                dve.wait_ge(side_free, SIDE[1, "rt"] + 1)
                b = side(1, "lg")
                for j, w in BLK:
                    last = dve.tensor_scalar(r["lg"][0:w, j, :], b[0:w, j * NE:(j + 1) * NE], rs[0:w, j:j + 1], None, ALU.mult)
                last.then_inc(side_free, 1)
                dve.wait_ge(side_free, SIDE[1, "lg"] + 1)

                def best(src, top, out):
                    step(dve.tensor_reduce(top[:, :], src[:, :, :], AX_X, ALU.max))
                    step(dve.tensor_tensor(r["eq"][:, :, :], src[:, :, :], bc(top), ALU.is_equal))
                    step(dve.tensor_tensor(r["key"][:, :, :], r["eq"][:, :, :], tie, ALU.mult))
                    step(dve.tensor_reduce(kx[:, :], r["key"][:, :, :], AX_X, ALU.max))
                    step(dve.tensor_tensor(out[:, :, :], r["key"][:, :, :], bc(kx), ALU.is_equal))

                best(r["lg"], m1, r["one"])
                step(dve.scalar_tensor_tensor(out=r["lg2"][:, :, :], in0=r["one"][:, :, :], scalar=-3.0e38,
                                              in1=r["lg"][:, :, :], op0=ALU.mult, op1=ALU.add))
                best(r["lg2"], m2, r["two"])
                dve.tensor_tensor(dm[:, :], m1[:, :], m2[:, :], ALU.subtract).then_inc(dm_ready, 1)
                dve.wait_ge(sig_ready, 1)
                step(dve.tensor_tensor(r["gate"][:, :, :], r["one"][:, :, :], bc(w1), ALU.mult))
                step(dve.tensor_tensor(r["t2"][:, :, :], r["two"][:, :, :], bc(w2), ALU.mult))
                dve.tensor_tensor(r["gate"][:, :, :], r["gate"][:, :, :], r["t2"][:, :, :], ALU.add).then_inc(routed, 1)
                for e in range(NE):
                    b = side(1, f"gb{e}")
                    last = dve.tensor_tensor(rg[:, e, :], b[:, 0:T], rstd[:, :], ALU.mult).then_inc(side_free, 1)

            dve.wait_ge(base_in, 80)
            dve.tensor_tensor(wr[:, :, :], wr[:, :, :], gains[:, 3, :].unsqueeze(2).to_broadcast([P, DC, NE]),
                              ALU.mult).then_inc(wr_ready, 1)
            for m in range(DC):
                finish(0, m)
                if m == 1:
                    lo(0, cols[0])
                if m == 4:
                    lo(1, cols[1])
            for l in range(DEPTH):
                for j in range(10):
                    ahead(U_MIX[l] + j)
                    if j == 0:
                        side_step(l, "norm1")
                    for c in (2 * j, 2 * j + 1):
                        z_chunk(l, c)
                    for name in AFTER[j]:
                        if name == "norm1":
                            continue
                        if name == "wp0":
                            for g in range(PC):
                                pool_diff(l, g)
                        side_step(l, name)
                    if j == 6:
                        dve.tensor_tensor(qxi[:, :, :], qk[:, 0, :, CH:2 * CH], xi, ALU.mult).then_inc(qxi_ready, 1)
                for name in AFTER[10]:
                    side_step(l, name)
                mix_part(l, RC - 1)
                dve.wait_ge(ple_hi, l + 1)
                dve.tensor_tensor(pl[:, :, :], pin[:, :, :], ph[:, :, :].bitcast(F32), ALU.subtract).then_inc(ple_lo, 1)
                for j in range(4):
                    ahead(U_WO[l] + j)
                    for m in (2 * j, 2 * j + 1):
                        add_h(A_WO[l] + m, m)
                    for m in (2 * j, 2 * j + 1):
                        finish(4 if l else 1, m)
                side_step(l, "norm2")
                if l:
                    route()
                    with dve.Fori(0, FF_STEPS[1]) as p:
                        feed_forward(1, p)
                else:
                    feed_forward(0, 0)
                for m in range(DC):
                    finish(5 if l else 2, m)
                ahead(U_PLE[l])
                for m in range(DC):
                    n = A_PLE[l] + m
                    chunk_full(dve, n)
                    dve.tensor_copy(esb[:, m, :], bank[n % 4][:, 0:T]).then_inc(acc_free, 1)
                for j in range(4):
                    ahead(U_PLE[l] + 1 + j)
                    for m in (2 * j, 2 * j + 1):
                        dve.wait_ge(ge_ready, DC * l + m + 1)
                        add_h(None, m, esb[:, m, :])
                    if l == 0:
                        for m in (2 * j, 2 * j + 1):
                            finish(3, m)
            side_step(DEPTH, "norm1")
            for m in range(DC):
                dve.scalar_tensor_tensor(out=h[:, m, :], in0=h[:, m, :], scalar=gains[:, 4, m:m + 1], in1=rstd[:, :],
                                         op0=ALU.mult, op1=ALU.mult).then_inc(y_ready, 1)

        @block.gpsimd
        def _(pool):
            steps = 0

            def step(ins):
                nonlocal steps
                steps += 1
                ins.then_inc(pool_step, 1)
                pool.wait_ge(pool_step, steps)

            def add_square(stage, m):
                n = SQUARES_AT[stage] + m
                pool.wait_ge(sq_ready, n + 1)
                if m == 0:
                    pool.tensor_copy(ssum[:, :], sq[:, n % 2, :]).then_inc(ss_added, 1)
                else:
                    pool.wait_ge(ss_added, n)
                    pool.tensor_tensor(ssum[:, :], ssum[:, :], sq[:, n % 2, :], ALU.add).then_inc(ss_added, 1)

            def square_sum(stage):
                for m in range(DC):
                    add_square(stage, m)

            def feed_forward(l, p):
                for half in range(2):
                    n = Count(l, p, half)
                    if l:
                        pool.tensor_copy(rge[:, half, :], rg[:, bass.ds(p * 2 + half, 1), :].rearrange("p a n -> p (a n)")).then_inc(
                            rge_ready, 1)
                        pool.wait_ge(rge_ready, p * 2 + (half + 1))
                    scale = rge[:, half, :] if l else rstd[:, :]
                    for f in range(EC):
                        pool.wait_ge(silu_f, n.hidden + (f + 1))
                        pool.tensor_tensor(tg[:, f % 2, :], tg[:, f % 2, :], scale, ALU.mult).then_inc(scaled_f, 1)

            pool.memset(rs[:, :], 1.0).then_inc(moe_zeroed, 1)
            pool.memset(r["lg"][:, :, :], 0.0).then_inc(moe_zeroed, 1)
            square_sum(0)
            for l in range(DEPTH):
                if l:
                    pool.wait_ge(acc_free, A_MIX[l])
                pool.dma_start(S[:, :, :, :], t["state_ret"][l].rearrange("s (c a) d e -> (a d) s c e", a=2)).then_inc(layer_in, 16)
                pool.dma_start(buf[:, :], t["state_pool"][l].rearrange("s r w -> (s r) w")).then_inc(layer_in, 16)
                pool.dma_start(wpool[:, :, :], t["w_pool"][l].rearrange("g c d -> c g d")).then_inc(layer_in, 16)
                pool.dma_start(selb[:, :, :], t["selb"]).then_inc(layer_in, 16)
                pool.dma_start(pin[:, :, :], t["p"][:, l, :, :]).then_inc(layer_in, 16)
                pool.dma_start(t["new_pool_sample"][l][:, 0:BUF - 1, :], t["state_pool"][l][:, 1:BUF, :]).then_inc(pool_kept, 16)
                pool.memset(upad[:, :, 0:PAD], 0.0).then_inc(zeroed, 1)
                pool.memset(sbd[:, :, :], 0.0).then_inc(zeroed, 1)
                pool.memset(vpad[:, :, :, 1, :], 0.0).then_inc(zeroed, 1)
                pool.memset(vs2[:, :, :], 0.0).then_inc(zeroed, 1)
                pool.memset(qm[:, :, :, :], 0.0).then_inc(zeroed, 1)
                pool.wait_ge(layer_in, 80 * (l + 1))
                pool.tensor_tensor(S[:, :, :, :].rearrange("p s c e -> p s c e"), S[:, :, :, :],
                                   C("gamma").unsqueeze(1).unsqueeze(3).to_broadcast([P, NS, RC, HD]),
                                   ALU.mult).then_inc(s_decayed, 1)
                for a, name in enumerate(("rq", "rk")):
                    for c in range(RC):
                        pool.wait_ge(side_full, SIDE[l, f"{name}{c}"] + 1)
                        pool.tensor_tensor(qk[:, a, c, :], qk[:, a, c, :], C("cos"), ALU.mult).then_inc(cosed, 1)
                pool.wait_ge(roped, 8 * l + 4)
                pool.wait_ge(zeroed, 5 * (l + 1))
                pool.wait_ge(cosed, 8 * (l + 1))
                for a in range(2):
                    rows = slice(a * HD, (a + 1) * HD)
                    pool.tensor_copy(qm[rows, :, :, a], qk[rows, 0, :, NP:T].rearrange("p c s -> p s c")).then_inc(qm_ready, 1)
                    pool.wait_ge(qm_ready, 2 * l + a + 1)
                pool.wait_ge(side_full, SIDE[l, "vs"] + 1)
                wtmp = sq[:, :, :].rearrange("p a n -> p (a n)")
                pool.wait_ge(acc_free, A_MIX[l] + 16)
                for g in range(PC):
                    src, width = upad[:, g, :], 1
                    to_tmp = g % 2 == 1
                    while width < WINDOWS[g]:
                        dst = wtmp if to_tmp else wsum[:, g, :]
                        a = 2 * width - 1
                        ins = pool.tensor_tensor(dst[:, a:PAD + NP], src[:, a:PAD + NP], src[:, a - width:PAD + NP - width],
                                                 ALU.add)
                        width *= 2
                        if width == WINDOWS[g]:
                            ins.then_inc(wsummed, 1)
                            pool.wait_ge(wsummed, PC * l + g + 1)
                        else:
                            step(ins)
                        src, to_tmp = dst, not to_tmp
                pool.wait_ge(s_decayed, l + 1)
                for i in range(4):
                    pool.wait_ge(side_free, SIDE[l, f"bc{i}"] + 1)
                    pool.tensor_tensor(S[:, 2 * i:2 * i + 2, :, :], S[:, 2 * i:2 * i + 2, :, :], kv[:, i % 2, :, :, :],
                                       ALU.add).then_inc(s_ready, 1)
                pool.wait_ge(side_free, SIDE[l, "S2"] + 1)
                pool.dma_start(t["new_ret_prompt"][l, 0].rearrange("(c a) d e -> (a d) c e", a=2), s2[:, :, :]).then_inc(state_out, 16)
                pool.wait_ge(s_ready, 4 * (l + 1))
                pool.dma_start(t["new_ret_sample"][l].rearrange("s (c a) d e -> (a d) s c e", a=2), S[:, :, :, :]).then_inc(state_out, 16)
                pool.wait_ge(side_free, SIDE[l, "tail"] + 1)
                pool.dma_start(t["new_pool_prompt"][l, 0], utail[0:BUF, :]).then_inc(state_out, 16)
                pool.dma_start(t["new_pool_sample"][l][:, BUF - 1, :], utail[BUF:BUF + NS, :]).then_inc(state_out, 16)
                for c in range(RC):
                    pool.wait_ge(side_free, SIDE[l, f"mu{c}"] + 1)
                    pool.wait_ge(silu_g, RC * (l + 1))
                    pool.tensor_tensor(og[:, c, :], oc[:, c, :], sg[:, c, :], ALU.mult).then_inc(og_ready, 1)
                square_sum(4 if l else 1)
                pool.wait_ge(side_free, SIDE[l, LAST[l][-1]] + 1)
                if l:
                    with pool.Fori(0, FF_STEPS[1]) as p:
                        feed_forward(1, p)
                else:
                    feed_forward(0, 0)
                for m in range(DC):
                    pool.wait_ge(acc_free, A_PLE[l] + m + 1)
                    pool.wait_ge(gate_ready, DC * l + m + 1)
                    pool.tensor_tensor(esb[:, m, :], esb[:, m, :], sgp[:, m % 2, :], ALU.mult).then_inc(ge_ready, 1)
                    if m % 2 and m > 1:
                        add_square(6 if l else 3, m - 3)
                        add_square(6 if l else 3, m - 2)
                add_square(6 if l else 3, DC - 2)
                add_square(6 if l else 3, DC - 1)
            pool.wait_ge(pool_kept, 32)
            pool.wait_ge(state_out, 128)


_OUTS = {"y": [P, DC, T], "new_pool_prompt": [DEPTH, 1, BUF, POOL_W],
         "new_ret_prompt": [DEPTH, 1, HEADS, HD, HD], "new_pool_sample": [DEPTH, NS, BUF, POOL_W],
         "new_ret_sample": [DEPTH, NS, HEADS, HD, HD]}


def kernel(**inputs):
    import concourse.bacc as bacc
    from concourse.bass_utils import run_bass_kernel_spmd

    a = {k: np.asarray(v) for k, v in inputs.items()}

    def columns(prompt, sample, width):
        x = np.concatenate([prompt.reshape(-1, width), sample.reshape(-1, width)])
        return np.ascontiguousarray(x.T.reshape(width // P, P, -1).transpose(1, 0, 2))

    def by_partition(rows):
        return np.ascontiguousarray(rows.reshape(rows.shape[0], -1, P).transpose(2, 0, 1))

    arrays = {
        "x": columns(a["x_prompt"], a["x_sample"], D),
        "p": np.ascontiguousarray(np.stack([columns(a["p_prompt"][l], a["p_sample"][l], PLE) for l in range(DEPTH)], 1)),
        "gains": by_partition(np.concatenate([a["norm1"], a["norm2"], a["final_norm"][None]])),
        "pscale": by_partition(a["pool_scale"]),
        "const": constants(),
        "selb": sample_rows(),
    }
    for name in ("state_pool", "state_ret", "w_in", "w_pool", "w_o", "ffn_w_gate", "ffn_w_up", "ffn_w_down",
                 "moe_router", "moe_w_gate", "moe_w_up", "moe_w_down", "w_ple", "w_ple_gate"):
        arrays[name] = np.ascontiguousarray(a[name])
    nc = bacc.Bacc("TRN2", target_bir_lowering=False, num_devices=1)
    t = {k: nc.dram_tensor(f"in_{k}", list(x.shape), F32, kind="ExternalInput").ap() for k, x in arrays.items()}
    t |= {k: nc.dram_tensor(f"out_{k}", s, F32, kind="ExternalOutput").ap() for k, s in _OUTS.items()}
    program(nc, t)
    got = run_bass_kernel_spmd(nc, [{f"in_{k}": x for k, x in arrays.items()}], core_ids=[0]).results[0]
    y = got["out_y"].transpose(2, 1, 0).reshape(T, D)
    return (y[:NP].reshape(1, NP, D), y[NP:].reshape(NS, 1, D), got["out_new_pool_prompt"],
            got["out_new_ret_prompt"], got["out_new_pool_sample"], got["out_new_ret_sample"])
```

```python
from contextlib import ExitStack

import numpy as np

import concourse.bass as bass
from concourse import mybir

F32 = mybir.dt.float32
F32R = mybir.dt.float32r
I32 = mybir.dt.int32
ALU = mybir.AluOpType
ACT = mybir.ActivationFunctionType
AX_X = mybir.AxisListType.X

P = 128
D = 1024
DC = D // P
NP = 256
NS = 8
T = NP + NS
DEPTH = 2
POOL_W = 512
PC = POOL_W // P
WINDOWS = (2, 4, 8, 16)
BUF = 15
HEADS, HD = 8, 64
RC = 512 // P
IN_W = POOL_W + 4 * 512
FF = 2816
NE = 8
FE = 1408
PLE = 256
EPS = 1e-6
PAST = 2048
CAP = 128
CH = 128
STEPS = ((0, 512), (512, 512), (1024, 384))
PAD = 16

RAW = 4
SPL = 4
UNIT = 2048
AHEAD = 2

CONST = {}
_at = 0
for _name, _n in (("ident", P), ("rot", P), ("mean", P), ("hmean", P), ("upper", P),
                  ("cos", T), ("sin", T), ("decay", 2 * RC * CH), ("xi", RC * CH), ("zeta", HEADS),
                  ("gchunk", RC), ("gamma", RC), ("early", PC * PAD), ("wsel", PC * NS),
                  ("iota", P), ("tie", NE), ("valid", 3), ("eps", 1)):
    CONST[_name] = (_at, _n)
    _at += _n
NCONST = _at


def constants():
    f = np.float32
    c = np.zeros((P, NCONST), f)

    def put(name, v):
        a, n = CONST[name]
        c[:v.shape[0], a:a + n] = v.reshape(v.shape[0], n)

    p = np.arange(P)
    put("ident", np.eye(P, dtype=f))
    rot = np.zeros((P, P), f)
    for m in range(P):
        if m % HD < HD // 2:
            rot[m + HD // 2, m] = -1.0
        else:
            rot[m - HD // 2, m] = 1.0
    put("rot", rot)
    put("mean", np.full((P, P), 1.0 / D, f))
    put("hmean", np.where(p[:, None] // HD == p[None, :] // HD, f(1.0 / HD), f(0)))
    put("upper", np.where(p[:, None] < p[None, :], f(1), f(0)))
    half = HD // 2
    inv = f(10000.0) ** (-np.arange(half, dtype=f) / f(half))
    pos = np.concatenate([np.arange(NP), np.full(NS, PAST)]).astype(f)
    ang = (pos[None, :] * inv[p % half][:, None]).astype(f)
    put("cos", np.cos(ang).astype(f))
    put("sin", np.sin(ang).astype(f))
    log_g = np.log1p(-np.power(f(2), -5 - np.arange(HEADS, dtype=f))).astype(f)
    i = np.arange(CH, dtype=f)
    rel = i[None, :] - i[:, None]
    dec = np.zeros((P, 2, RC, CH), f)
    for h in range(HEADS):
        dec[:, h % 2, h // 2] = np.where(rel >= 0, np.exp(log_g[h] * np.maximum(rel, 0)), 0)
    put("decay", dec)
    own = 2 * np.arange(RC)[None, :] + (p[:, None] // HD)
    put("xi", np.exp(log_g[own][:, :, None] * (i + 1)[None, None, :]).astype(f))
    put("zeta", np.exp(log_g[None, :] * (CH - 1 - i)[:, None]).astype(f))
    put("gchunk", np.exp(log_g[own] * CH).astype(f))
    put("gamma", np.exp(log_g[own]).astype(f))
    early = np.ones((P, PC, PAD), f)
    for g, w in enumerate(WINDOWS):
        early[:, g] = w / np.minimum(np.arange(PAD) + 1, w)
    put("early", early)
    wsel = np.zeros((NS * BUF, PC, NS), f)
    for g, w in enumerate(WINDOWS):
        for b in range(NS):
            wsel[b * BUF + BUF - (w - 1):(b + 1) * BUF, g, b] = 1
    put("wsel", wsel)
    put("iota", np.broadcast_to(np.where(p < CAP, p, -2).astype(f), (P, P)))
    valid = np.ones((P, 3), f)
    valid[NS:, 2] = 0
    put("valid", valid)
    put("tie", np.broadcast_to(NE - np.arange(NE, dtype=f), (P, NE)))
    put("eps", np.full((P, 1), EPS, f))
    return c


def sample_rows():
    z = np.zeros((64, NS, P), np.float32)
    for b in range(NS):
        z[b, b, 0:HD] = 1
        z[32 + b, b, HD:P] = 1
    return z


Z_ORDER = ((512, "q"), (1024, "k"), (1536, "v"), (0, "u"), (2048, "g"))
W_IN = [("w_in", 0, DC, at + 256 * j, 256) for at, _ in Z_ORDER for j in range(2)]
W_O = [("w_o", 0, DC, 256 * j, 256) for j in range(4)]
PLEU = [("w_ple", 0, 2, 0, D)] + [("w_ple_gate", 0, DC, 256 * j, 256) for j in range(4)]

EC = FE // P
GROUPS = (EC + 1) // 2


def part_units():
    out, chunks, full = [], 0, 0
    for i in range(GROUPS):
        w = min(2, EC - 2 * i)
        for kind in ("gate", "up"):
            out.append((kind, 2 * i, w, chunks, full))
            chunks += w
            full += w - 1
    for m in range(DC):
        out.append(("down", m, 1, chunks, full))
        chunks += 1
    return out, chunks, full


PART, PART_CHUNKS, PART_FULL = part_units()
PART_UNITS = len(PART)
STEP_UNITS, STEP_CHUNKS, STEP_FULL = 2 * PART_UNITS, 2 * PART_CHUNKS, 2 * PART_FULL
assert FF == 2 * FE
MOE_FIRST, MOE_EACH, MOE_TAIL = 16, 18, 2
FF_UNITS = (STEP_UNITS, MOE_FIRST + (NE - 1) * MOE_EACH + MOE_TAIL)

PLE_FULL = DC - 1 + 4
U_MIX, A_MIX, F_MIX = [0], [0], [0]
U_WO, U_FF, U_PLE, A_WO, A_FF, A_PLE, F_FF = [], [], [], [], [], [], []
for _l in range(DEPTH):
    U_WO.append(U_MIX[_l] + len(W_IN))
    U_FF.append(U_WO[_l] + len(W_O))
    U_PLE.append(U_FF[_l] + FF_UNITS[_l])
    U_MIX.append(U_PLE[_l] + len(PLEU))
    A_WO.append(A_MIX[_l] + 2 * len(W_IN))
    A_FF.append(A_WO[_l] + 2 * len(W_O))
    A_PLE.append(A_FF[_l] + (STEP_CHUNKS, 0)[_l])
    A_MIX.append(A_PLE[_l] + 2 * DC)
    F_FF.append(F_MIX[_l] + len(W_IN) + len(W_O))
    F_MIX.append(F_FF[_l] + (STEP_FULL, 0)[_l] + PLE_FULL)
N_UNITS = U_MIX[DEPTH]


def chunk_table():
    table, count = {}, 0

    def unit(u, chunks):
        nonlocal count
        for n in chunks[:-1]:
            count += 1
            table[n] = (False, count)
        table[chunks[-1]] = (True, u + 1)

    for l in range(DEPTH):
        for j in range(len(W_IN)):
            unit(U_MIX[l] + j, [A_MIX[l] + 2 * j, A_MIX[l] + 2 * j + 1])
        for j in range(len(W_O)):
            unit(U_WO[l] + j, [A_WO[l] + 2 * j, A_WO[l] + 2 * j + 1])
        assert count == F_FF[l]
        count += (STEP_FULL, 0)[l]
        unit(U_PLE[l], [A_PLE[l] + m for m in range(DC)])
        for j in range(4):
            unit(U_PLE[l] + 1 + j, [A_PLE[l] + 8 + 2 * j, A_PLE[l] + 9 + 2 * j])
    return table


CHUNK_FULL = chunk_table()

PARTS_AT = {0: 0, 1: 8, 2: 16, 3: 24, 5: 32}
SQUARES_AT = {0: 0, 1: 8, 3: 16, 4: 24, 6: 32}
GAIN = {0: 0, 1: 2, 3: 1}
NORM_STAGE = {(0, "norm1"): 0, (0, "norm2"): 1, (1, "norm1"): 3, (1, "norm2"): 4, (2, "norm1"): 6}
NORM_ORDER = {k: i for i, k in enumerate(NORM_STAGE)}

AFTER = [["norm1"], [], [f"rq{c}" for c in range(RC)], [], [f"rk{c}" for c in range(RC)], [],
         ["kt0", "kt1", "vt0", "vt1"], ["vs", "sc00", "sc01", "o0", "win"],
         ["sc10", "sc11", "S1", "S2", "bc0", "bc1"],
         ["bc2", "bc3", "o1", "qS", "tail", "wp0", "wp1", "wp2", "wp3"],
         [f"mu{c}" for c in range(RC)] + [f"va{c}" for c in range(RC)]]
LAST = (["norm2"], ["norm2", "lg"] + [f"tr{i}" for i in range(6)] + ["pos", "over"])
SIDE = {}
_at = 0
for _l in range(DEPTH):
    for _group in AFTER + [LAST[_l]]:
        for _s in _group:
            SIDE[_l, _s] = _at
            _at += 1
SIDE[DEPTH, "norm1"] = _at
SIDE_MOE = _at



def turn_units(first):
    out = {}
    for s, (lo, n) in enumerate(STEPS):
        for half in range(2):
            out[6 * s + 2 * half] = ("moe_w_gate", 0, 4 * half, 4, lo, n, s)
            out[6 * s + 2 * half + 1] = ("moe_w_up", 0, 4 * half, 4, lo, n, s)
        ps = (s + 2) % 3
        if s or not first:
            a, n = STEPS[ps]
            out[6 * s + 4] = ("moe_w_down", int(s == 0), a // P, 2, 0, D, ps)
            out[6 * s + 5] = ("moe_w_down", int(s == 0), a // P + 2, n // P - 2, 0, D, ps)
    return out


FIRST_TURN, TURN = turn_units(True), turn_units(False)
TAIL_TURN = {4: ("moe_w_down", 0, 8, 2, 0, D, 2), 5: ("moe_w_down", 0, 10, 1, 0, D, 2)}
assert len(FIRST_TURN) == MOE_FIRST and len(TURN) == MOE_EACH and len(TAIL_TURN) == MOE_TAIL
U_MOE, U_EXP1, U_TAIL = U_FF[1], U_FF[1] + MOE_FIRST, U_PLE[1] - MOE_TAIL


def turn_events(kind, odd):
    if kind == "tail":
        return {3: [("t", 2)], 5: [("y", 0)] + [("s", m) for m in range(DC)]}
    ev = {7: [("t", 0)], 12: [("p", 0)], 13: [("t", 1)]}
    if kind != "first":
        ev |= {1: [("t", 2)], 5: [("y", 0)], 8: [("s", 1), ("s", 2)], 9: [("s", 3), ("s", 4)],
               10: [("s", 5), ("s", 6)], 11: [("s", 7)]}
        ev[7] += [("s", 0)]
    if kind == "loop" and odd:
        ev[13] += [("k", 0)]
        ev |= {15: [("x", 0), ("x", 1)], 16: [("x", 2), ("x", 3)]}
    return ev


TMP_STEPS = "tspx"


def tmp_steps(kind, odd):
    return sum(ev[0] in TMP_STEPS for v in turn_events(kind, odd).values() for ev in v)


GATHERS = DC // 2
TMP_EXP1 = GATHERS + tmp_steps("first", False)
TMP_ODD, TMP_EVEN = tmp_steps("loop", True), tmp_steps("loop", False)
TMP_TAIL = TMP_EXP1 + (NE - 2) // 2 * (TMP_ODD + TMP_EVEN) + tmp_steps("last", True)
assert (TMP_ODD + TMP_EVEN) % 2 == 0
U_MOE, U_EXP1, U_TAIL = U_FF[1], U_FF[1] + MOE_FIRST, U_PLE[1] - MOE_TAIL


class Turn:

    def __init__(self, kind, pair=0, half=0):
        self.kind = kind
        self.units = {"first": FIRST_TURN, "tail": TAIL_TURN}.get(kind, TURN)
        if kind == "first":
            self.e = self.e_at = 0
            self.u = self.u_at = U_MOE
            self.k = self.k_at = GATHERS
        else:
            i = {"loop": half, "last": NE - 2, "tail": NE - 1}[kind]
            self.e_at = 1 + i
            self.u_at = U_EXP1 + MOE_EACH * i
            self.k_at = TMP_TAIL if kind == "tail" else TMP_EXP1 + i // 2 * (TMP_ODD + TMP_EVEN) + i % 2 * TMP_ODD
            self.e = pair * 2 + self.e_at
            self.u = pair * (2 * MOE_EACH) + self.u_at
            self.k = pair * (TMP_ODD + TMP_EVEN) + self.k_at
        self.pair = pair
        self.slot = self.e_at % 2
        self.events = turn_events(kind, self.slot == 1)
        self.at = {pos: n for n, pos in enumerate(sorted(self.units))}
        self.tmp = {}
        for pos in sorted(self.events):
            for ev in self.events[pos]:
                if ev[0] in TMP_STEPS:
                    self.tmp[ev] = len(self.tmp)

    def unit(self, pos):
        return self.u_at + self.at[pos], self.u + self.at[pos]

    def step(self, ev):
        return self.k_at + self.tmp[ev], self.k + self.tmp[ev]

    def gate_bank(self, s):
        return 2 * ((self.e_at + s) % 2)

    def places(self):
        return sorted(set(self.units) | set(self.events))


OVER_PE, OVER_DVE = 1 + EC + DC, 2 + EC + DC

assert 2 * MOE_EACH % RAW == 0 and 2 * MOE_EACH % SPL == 0 and NE % 2 == 0


def program(nc, t):
    with ExitStack() as ctx:
        at = [16512]

        def place(name, shape, dt=F32, offset=None):
            n = 4 * int(np.prod(shape[1:]))
            if offset is None:
                offset = at[0]
                at[0] += (n + 31) // 32 * 32
            return nc.alloc_sbuf_tensor_at(name, list(shape), dt, offset=offset)

        def sem(name):
            return ctx.enter_context(nc.semaphore(name))

        const = place("const", [P, NCONST])
        raw = [place(f"raw{i}", [P, UNIT]) for i in range(RAW)]
        whi = [place(f"whi{i}", [P, UNIT], F32R) for i in range(SPL)]
        wlo = [place(f"wlo{i}", [P, UNIT], F32R) for i in range(SPL)]
        h = place("h", [P, DC, T])
        x_at, ple_at = at[0], at[0] + 8 * DC * T
        xh = place("xh", [P, DC, T], F32R)
        xl = place("xl", [P, DC, T], F32R)
        ph = place("ph", [P, 2, T], F32R)
        pl = place("pl", [P, 2, T], F32R)
        selb = place("selb", [64, NS, P], F32, ple_at)
        gains = place("gains", [P, 5, DC])
        pscale = place("pscale", [P, DEPTH, PC])
        ssum = place("ssum", [P, T])
        sq = place("sq", [P, 2, T])
        std = place("std", [P, T])
        rstd = place("rstd", [P, T])
        rstd8 = place("rstd8", [P, T])
        wr = place("wr", [P, DC, NE])
        arena = at[0]
        qk = place("qk", [P, 2, RC, T])
        wsum_at = at[0]
        wsum = place("wsum", [P, PC, PAD + T])
        v = place("v", [P, RC, T], F32, wsum_at)
        sg = place("sg", [P, RC, T])
        upad = place("upad", [P, PC, PAD + T])
        sbd = place("sbd", [P, RC, P])
        o = place("o", [P, RC, T])
        S = place("S", [P, NS, RC, HD])
        kv_at = at[0]
        kv = place("kv", [P, 2, 2, RC, HD])
        rt = place("rt", [P, 2, T], F32, kv_at)
        buf = place("buf", [NS * BUF, POOL_W])
        utail = place("utail", [BUF + NS, POOL_W], F32, kv_at)
        s2 = place("s2", [P, RC, HD])
        vs2 = place("vs2", [64, RC, HD])
        qm = place("qm", [P, NS, RC, 2])
        wpool = place("wpool", [P, PC, P])
        pin = place("pin", [P, 2, T])
        mix_at = at[0]
        mh = place("mh", [P, DC, T], F32R)
        ml = place("ml", [P, DC, T], F32R)
        assert at[0] <= 229344, at[0]
        kz = place("kz", [P, 2, 512], F32, mix_at)
        vpad = place("vpad", [P, 2, RC, 3, HD], F32, mix_at + 4096)
        sc = place("sc", [P, 2, RC, CH], F32, mix_at + 4096 + 6144)
        qxi = place("qxi", [P, RC, CH], F32, mix_at + 4096 + 6144 + 4096)
        oc = place("oc", [P, RC, T], F32, x_at)
        osq = place("osq", [P, RC, T], F32, x_at + 4 * RC * T)
        og = place("og", [P, RC, T], F32, x_at + 8 * RC * T)
        stdv = place("stdv", [P, 2, T], F32, x_at + 12 * RC * T)
        fh = place("fh", [P, EC, T], F32R, arena)
        fl = place("fl", [P, EC, T], F32R, arena + 4 * EC * T)
        tg = place("tg", [P, 2, T], F32, mix_at)
        hv = place("hv", [P, 2, T], F32, mix_at + 8 * T)
        esb = place("esb", [P, DC, T], F32, arena)
        sgp = place("sgp", [P, 2, T], F32, arena + 4 * DC * T)
        cur = [arena]

        def moe(name, shape, dt=F32):
            x = place(name, shape, dt, cur[0])
            cur[0] += (4 * int(np.prod(shape[1:])) + 31) // 32 * 32
            return x

        xth = moe("xth", [P, 3, D], F32R)
        xtl = moe("xtl", [P, 3, D], F32R)
        sgate = moe("sgate", [P, 512])
        hid = moe("hid", [P, 512])
        hh = moe("hh", [P, 4, P], F32R)
        hl = moe("hl", [P, 4, P], F32R)
        pick = moe("pick", [P, 3, 2, P], F32R)
        pickT = moe("pickT", [P, T], F32R)
        identr = moe("identr", [P, P], F32R)
        yh = moe("yh", [P, D], F32R)
        yl = moe("yl", [P, D], F32R)
        r = {n: moe("r_" + n, [P, 3, NE]) for n in
             ("lg", "eq", "key", "one", "two", "lg2", "gate", "t2", "sel", "pos", "over")}
        gh = moe("gh", [P, 3, NE], F32R)
        gl = moe("gl", [P, 3, NE], F32R)
        m1, m2, kx, dm, w1, w2 = (moe(n, [P, 3]) for n in ("m1", "m2", "kx", "dm", "w1", "w2"))
        pose = moe("pose", [P, 3, 2])
        gslot = moe("gslot", [P, 1])
        over1 = moe("over1", [P, 1])
        flag = moe("flag", [1, 1], I32)
        assert cur[0] <= mix_at
        xel = moe("xel", [P, DC, 2, P], F32R)
        assert cur[0] <= mix_at + 8 * DC * T, (cur[0], mix_at)
        owt = place("owt", [P, 2, EC * P], F32, arena)
        ohid = place("ohid", [P, EC, T], F32, arena + 8 * EC * P)
        assert 8 * EC * P + 4 * EC * T <= 8 * 3 * D
        osg = place("osg", [P, T], F32, arena + 8 * 3 * D)
        orow = place("orow", [P, T], F32, arena + 8 * 3 * D + 4 * 512)
        ocol = place("ocol", [P, 3], F32, arena + 8 * 3 * D + 8 * 512)
        xn = place("xn", [P, DC, T], F32, x_at)
        xeh = place("xeh", [P, DC, 2, P], F32R, x_at + 4 * DC * T)
        BLK = ((0, P), (1, P), (2, NS))

        bank = [ctx.enter_context(nc.psum_tensor(f"bank{i}", [P, 512], F32)) for i in range(8)]

        raw_landed = [sem(f"raw_landed{i}") for i in range(RAW)]
        hi_ready, lo_ready, unit_used = sem("hi_ready"), sem("lo_ready"), sem("unit_used")
        base_in, layer_in = sem("base_in"), sem("layer_in")
        pool_kept, state_out, y_out = sem("pool_kept"), sem("state_out"), sem("y_out")
        acc_full, acc_free = sem("acc_full"), sem("acc_free")
        side_full, side_free = sem("side_full"), sem("side_free")
        part_hi, part_lo, sq_ready, ss_added = sem("part_hi"), sem("part_lo"), sem("sq_ready"), sem("ss_added")
        std_ready = sem("std_ready")
        zeroed, cosed, roped, silu_g = sem("zeroed"), sem("cosed"), sem("roped"), sem("silu_g")
        s_decayed, s_ready, qm_ready = sem("s_decayed"), sem("s_ready"), sem("qm_ready")
        qxi_ready, wsummed, d_ready = sem("qxi_ready"), sem("wsummed"), sem("d_ready")
        osq_ready, og_ready, stdv_ready = sem("osq_ready"), sem("og_ready"), sem("stdv_ready")
        s2_ready = sem("s2_ready")
        on_ready, mix_hi, mix_lo = sem("on_ready"), sem("mix_hi"), sem("mix_lo")
        silu_f, scaled_f, f_hi, f_lo = sem("silu_f"), sem("scaled_f"), sem("f_hi"), sem("f_lo")
        ple_hi, ple_lo, gate_ready, ge_ready = sem("ple_hi"), sem("ple_lo"), sem("gate_ready"), sem("ge_ready")
        identr_ready, moe_zeroed, xn_ready = sem("identr_ready"), sem("moe_zeroed"), sem("xn_ready")
        dm_ready, sig_ready, routed, gate_hi, gate_lo = (sem("dm_ready"), sem("sig_ready"), sem("routed"),
                                                         sem("gate_hi"), sem("gate_lo"))
        xt_hi, y_ready = sem("xt_hi"), sem("y_ready")
        tmp_full, tmp_free = sem("tmp_full"), sem("tmp_free")
        sgate_ready, hid_ready, hh_ready = sem("sgate_ready"), sem("hid_ready"), sem("hh_ready")
        pose_ready, pick_ready, xe_hi = sem("pose_ready"), sem("pick_ready"), sem("xe_hi")
        y_hi, y_lo, over_ready = sem("y_hi"), sem("y_lo"), sem("over_ready")
        o_landed = [sem("o_landed0"), sem("o_landed1")]
        o_used, o_silu, o_done, o_scaled = sem("o_used"), sem("o_silu"), sem("o_done"), sem("o_scaled")
        dve_step, pool_step = sem("dve_step"), sem("pool_step")

        def C(name, rows=P):
            a, n = CONST[name]
            return const[0:rows, a:a + n]

        ident, rot, mean = C("ident"), C("rot"), C("mean")
        decay = C("decay").rearrange("p (a c n) -> p a c n", a=2, c=RC)
        xi = C("xi").rearrange("p (c n) -> p c n", c=RC)
        wsel = C("wsel", NS * BUF).rearrange("p (g b) -> p g b", g=PC)
        def chunk_full(eng, n):
            by_unit, count = CHUNK_FULL[n]
            eng.wait_ge(unit_used if by_unit else acc_full, count)

        def h_final(eng, stage, m):
            if stage == 0:
                eng.wait_ge(base_in, 80)
            else:
                if stage == 5:
                    eng.wait_ge(tmp_free, TMP_TAIL + 2 + m)
                    return
                first = {1: A_WO[0], 2: A_PLE[0] - DC, 3: A_PLE[0] + DC, 4: A_WO[1],
                         6: A_PLE[1] + DC}[stage]
                eng.wait_ge(acc_free, first + m + 1)

        part_cols = [(DC if kind != "down" else EC) * w * P for kind, _, w, _, _ in PART]
        cols = {}
        for l in range(DEPTH):
            for first, specs in ((U_MIX[l], W_IN), (U_WO[l], W_O), (U_PLE[l], PLEU)):
                cols |= {first + j: x[2] * x[4] for j, x in enumerate(specs)}
        cols |= {U_FF[l] + j: UNIT for l in range(DEPTH) for j in range(AHEAD)}
        assert all(cols[U_PLE[l] + j] == UNIT for l in range(DEPTH) for j in range(AHEAD))

        def turn_cols(turn, i):
            n = len(turn.units)
            if i >= n:
                if turn.kind != "last":
                    return UNIT
                x = TAIL_TURN[sorted(TAIL_TURN)[i - n]]
            else:
                x = turn.units[sorted(turn.units)[i]]
            return x[3] * x[5]

        class Count:

            def __init__(self, half):
                self.unit = U_FF[0] + half * PART_UNITS
                self.chunk = A_FF[0] + half * PART_CHUNKS
                self.full = F_FF[0] + half * PART_FULL
                self.hidden = half * EC

        block = ctx.enter_context(nc.Block())

        @block.sync
        def _(sp):
            def load(slot, vector_through, src, n, w):
                if vector_through is not None:
                    sp.wait_ge(lo_ready, vector_through)
                dst = raw[slot][:, 0:n * w].rearrange("p (k w) -> p k w", k=n)
                sp.dma_start(dst, src.rearrange("(k p) w -> p k w", p=P)).then_inc(raw_landed[slot], 16)

            def dense(layer, first, specs):
                for j, (name, k0, n, c0, w) in enumerate(specs):
                    u = first + j
                    m = t[name][layer]
                    load(u % RAW, u - RAW + 1 if u >= RAW else None, m[k0 * P:(k0 + n) * P, c0:c0 + w], n, w)

            def feed_forward():
                for half in range(2):
                    n = Count(half)
                    own = slice(half * FE, (half + 1) * FE)
                    gate, up, down = t["ffn_w_gate"][0][:, own], t["ffn_w_up"][0][:, own], t["ffn_w_down"][0][own, :]
                    for i, (kind, c, w, _, _) in enumerate(PART):
                        src = {"gate": gate, "up": up, "down": down}[kind]
                        load((n.unit + i) % RAW, n.unit + (i - RAW + 1), src[:, c * P:(c + w) * P],
                             EC if kind == "down" else DC, w * P)

            def experts(turn):
                for pos in sorted(turn.units):
                    name, back, k0, n, c0, w, _ = turn.units[pos]
                    off, u = turn.unit(pos)
                    e = turn.e - (back + (turn.kind == "tail"))
                    m = t[name][0][e] if isinstance(e, int) else t[name][0][bass.ds(e, 1)].rearrange("a k w -> (a k) w")
                    load(off % RAW, u - (RAW - 1), m[k0 * P:(k0 + n) * P, c0:c0 + w], n, w)

            sp.dma_start(h[:, :, :], t["x"]).then_inc(base_in, 16)
            sp.dma_start(gains[:, :, :], t["gains"]).then_inc(base_in, 16)
            sp.dma_start(const[:, :], t["const"]).then_inc(base_in, 16)
            sp.dma_start(pscale[:, :, :], t["pscale"]).then_inc(base_in, 16)
            sp.dma_start(wr[:, :, :], t["moe_router"][0].rearrange("(c p) e -> p c e", p=P)).then_inc(base_in, 16)
            dense(0, U_MIX[0], W_IN)
            dense(0, U_WO[0], W_O)
            feed_forward()
            dense(0, U_PLE[0], PLEU)
            dense(1, U_MIX[1], W_IN)
            dense(1, U_WO[1], W_O)
            experts(Turn("first"))
            with sp.Fori(0, (NE - 2) // 2) as pair:
                for half in range(2):
                    experts(Turn("loop", pair, half))
            experts(Turn("last"))
            experts(Turn("tail"))
            dense(1, U_PLE[1], PLEU[:AHEAD])
            sp.wait_ge(side_free, SIDE_MOE)
            with sp.If(sp.value_load(flag[0:1, 0:1], min_val=0, max_val=2 * T) > 0):
                with sp.Fori(0, NE) as e:
                    gate, up, down = (t[name][0][bass.ds(e, 1)].rearrange("a k w -> (a k) w")
                                      for name in ("moe_w_gate", "moe_w_up", "moe_w_down"))
                    for i in range(EC + DC):
                        for a, src in enumerate((gate, up) if i < EC else (down,)):
                            n = DC if i < EC else EC
                            c = i if i < EC else i - EC
                            sp.wait_ge(o_used, e * OVER_PE + (i + 1))
                            dst = owt[:, a, 0:n * P].rearrange("p (k w) -> p k w", k=n)
                            sp.dma_start(dst, src[:, c * P:(c + 1) * P].rearrange("(k p) w -> p k w", p=P)).then_inc(o_landed[a], 16)
            dense(1, U_PLE[1] + AHEAD, PLEU[AHEAD:])
            for j in range(4):
                sp.wait_ge(y_ready, 2 * j + 2)
                sp.dma_start(t["y"][:, 2 * j:2 * j + 2, :], h[:, 2 * j:2 * j + 2, :]).then_inc(y_out, 16)
            sp.wait_ge(y_out, 64)

        @block.tensor
        def _(pe):
            def weights_first(out, w_hi, w_lo, x_hi, x_lo, start, stop):
                pe.matmul(out, w_hi, x_hi, start=start, stop=False)
                pe.matmul(out, w_hi, x_lo, start=False, stop=False)
                return pe.matmul(out, w_lo, x_hi, start=False, stop=stop)

            def chunk(at, n, u, k, w, m, xhi, xlo, row_ready=None):
                if at >= 4:
                    pe.wait_ge(acc_free, n - 3)
                out = bank[at % 4][:, 0:T]
                H = whi[u % SPL][:, 0:k * w].rearrange("p (k w) -> p k w", k=k)
                L = wlo[u % SPL][:, 0:k * w].rearrange("p (k w) -> p k w", k=k)
                for kc in range(k):
                    if row_ready is not None:
                        pe.wait_ge(f_lo, row_ready + (kc + 1))
                    mm = weights_first(out, H[:, kc, m * P:(m + 1) * P], L[:, kc, m * P:(m + 1) * P],
                                       xhi[:, kc, :], xlo[:, kc, :], kc == 0, kc == k - 1)
                return mm

            def unit_pair(u, n, xhi, xlo):
                pe.wait_ge(lo_ready, u + 1)
                chunk(n, n, u, DC, 256, 0, xhi, xlo).then_inc(acc_full, 1)
                chunk(n + 1, n + 1, u, DC, 256, 1, xhi, xlo).then_inc(unit_used, 1)

            def feed_forward():
                for half in range(2):
                    n = Count(half)
                    for i, (kind, _, w, a, _) in enumerate(PART):
                        pe.wait_ge(lo_ready, n.unit + (i + 1))
                        for m in range(w):
                            down = kind == "down"
                            mm = chunk(n.chunk + a + m, n.chunk + (a + m), n.unit + i, EC if down else DC, w * P, m,
                                       fh if down else xh, fl if down else xl,
                                       n.hidden if i == 2 * GROUPS else None)
                            mm.then_inc(acc_full if m < w - 1 else unit_used, 1)

            def side_step(l, name):
                i = SIDE[l, name]
                if i >= 4:
                    pe.wait_ge(side_free, i - 3)
                b = bank[4 + i % 4]
                if name in ("norm1", "norm2"):
                    pe.wait_ge(ss_added, SQUARES_AT[NORM_STAGE[l, name]] + DC)
                    mm = pe.matmul(b[:, 0:T], mean, ssum[:, :], start=True, stop=True)
                elif name[:2] in ("rq", "rk"):
                    a, c = int(name[1] == "k"), int(name[2])
                    pe.wait_ge(acc_free, A_MIX[l] + 4 * a + c + 1)
                    mm = pe.matmul(b[:, 0:T], rot, qk[:, a, c, :], start=True, stop=True)
                elif name[:2] in ("kt", "vt"):
                    blk = int(name[2])
                    if name[0] == "k":
                        pe.wait_ge(roped, 8 * (l + 1))
                    else:
                        pe.wait_ge(acc_free, A_MIX[l] + 12)
                    for c in range(RC):
                        src = qk[:, 1, c, :] if name[0] == "k" else v[:, c, :]
                        mm = pe.transpose(b[:, c * P:(c + 1) * P], src[:, blk * CH:(blk + 1) * CH], ident)
                elif name == "vs":
                    for c in range(RC):
                        mm = pe.transpose(b[0:NS, c * P:(c + 1) * P], v[:, c, NP:T], ident)
                elif name[:2] == "sc":
                    blk, hp = int(name[2]) * CH, int(name[3])
                    rows = slice(hp * HD, (hp + 1) * HD)
                    for c in range(RC):
                        mm = pe.matmul(b[:, c * CH:(c + 1) * CH], qk[rows, 1, c, blk:blk + CH],
                                       qk[rows, 0, c, blk:blk + CH], start=True, stop=True)
                elif name == "win":
                    pe.wait_ge(layer_in, 80 * (l + 1))
                    for g in range(PC):
                        mm = pe.matmul(b[:, g * NS:(g + 1) * NS], buf[:, g * P:(g + 1) * P], wsel[:, g, :],
                                       start=True, stop=True)
                elif name in ("S1", "S2"):
                    blk = int(name == "S2")
                    pe.wait_ge(side_free, SIDE[l, "vt1"] + 1)
                    for c in range(RC):
                        mm = pe.matmul(b[:, c * P:(c + 1) * P], kz[:, blk, c * P:(c + 1) * P],
                                       vpad[:, blk, c, 0:3:2, :], start=True, stop=True)
                elif name in ("o0", "o1"):
                    blk = int(name[1])
                    pe.wait_ge(side_free, SIDE[l, f"sc{blk}1"] + 1)
                    pe.wait_ge(zeroed, 5 * (l + 1))
                    if blk:
                        pe.wait_ge(side_free, SIDE[l, "S1"] + 1)
                        pe.wait_ge(qxi_ready, l + 1)
                    for c in range(RC):
                        out = b[:, c * CH:(c + 1) * CH]
                        vc = vpad[:, blk, c, :, :].rearrange("p a e -> p (a e)")
                        pe.matmul(out, vc[:, 0:P], sc[:, 0, c, :], start=True, stop=False)
                        mm = pe.matmul(out, vc[:, HD:HD + P], sc[:, 1, c, :], start=False, stop=not blk)
                        if blk:
                            mm = pe.matmul(out, sbd[:, c, :], qxi[:, c, :], start=False, stop=True)
                elif name[:2] == "bc":
                    pe.wait_ge(side_free, SIDE[l, "vs"] + 1)
                    pe.wait_ge(layer_in, 80 * (l + 1))
                    for a in range(2):
                        mm = pe.matmul(b[:, a * 256:(a + 1) * 256], selb[:, 2 * int(name[2]) + a, :],
                                       vs2[:, :, :].rearrange("p c e -> p (c e)"), start=True, stop=True)
                elif name == "qS":
                    pe.wait_ge(s_ready, 4 * (l + 1))
                    pe.wait_ge(qm_ready, 2 * (l + 1))
                    for s in range(NS):
                        for c in range(RC):
                            a = 2 * (s * RC + c)
                            mm = pe.matmul(b[0:HD, a:a + 2], S[:, s, c, :], qm[:, s, c, :], start=True, stop=True)
                elif name == "tail":
                    pe.wait_ge(acc_free, A_MIX[l] + 16)
                    for g in range(PC):
                        mm = pe.transpose(b[0:BUF + NS, g * P:(g + 1) * P], upad[:, g, PAD + NP - BUF:PAD + T], ident)
                elif name[:2] == "wp":
                    g = int(name[2])
                    pe.wait_ge(d_ready, PC * l + g + 1)
                    mm = pe.matmul(b[:, 0:T], wpool[:, g, :], wsum[:, g, PAD:PAD + T], start=True, stop=True)
                elif name[:2] == "mu":
                    pe.wait_ge(side_free, SIDE[l, "qS"] + 1)
                    mm = pe.matmul(b[:, 0:T], C("hmean"), o[:, int(name[2]), :], start=True, stop=True)
                elif name[:2] == "va":
                    pe.wait_ge(osq_ready, RC * l + int(name[2]) + 1)
                    mm = pe.matmul(b[:, 0:T], C("hmean"), osq[:, int(name[2]), :], start=True, stop=True)
                elif name == "lg":
                    pe.wait_ge(xn_ready, DC)
                    for j, w in BLK:
                        for c in range(DC):
                            mm = pe.matmul(b[0:w, j * NE:(j + 1) * NE], xn[:, c, j * P:j * P + w], wr[:, c, :],
                                           start=(c == 0), stop=(c == DC - 1))
                elif name[:2] == "tr":
                    j, half = divmod(int(name[2]), 2)
                    w = BLK[j][1]
                    for c in range(4):
                        mm = pe.transpose(b[0:w, c * P:(c + 1) * P], xn[:, 4 * half + c, j * P:j * P + w], ident)
                elif name == "pos":
                    pe.wait_ge(routed, 1)
                    ones = C("valid")[:, 0:1].to_broadcast([P, P])
                    for j in range(3):
                        for i2 in range(j + 1):
                            mm = pe.matmul(b[:, j * NE:(j + 1) * NE], C("upper") if i2 == j else ones,
                                           r["sel"][:, i2, :], start=(i2 == 0), stop=(i2 == j))
                elif name == "over":
                    pe.wait_ge(over_ready, 1)
                    mm = pe.matmul(b[0:1, 0:1], over1[:, :], C("valid")[:, 0:1], start=True, stop=True)
                mm.then_inc(side_full, 1)

            def tmp_bank(off, k):
                if off >= 2:
                    pe.wait_ge(tmp_free, k - 1)
                return bank[6 + off % 2]

            def gather(i, off, k, count):
                b = tmp_bank(off, k)
                if i == 0:
                    pe.wait_ge(pick_ready, count)
                for c in range(2):
                    f = (2 * i + c) * P
                    for j, w in BLK:
                        out, sel = b[:, 2 * c * P:2 * (c + 1) * P], pick[0:w, j, :, :].rearrange("p a n -> p (a n)")
                        pe.matmul(out, xth[0:w, j, f:f + P], sel, start=(j == 0), stop=False)
                        mm = pe.matmul(out, xtl[0:w, j, f:f + P], sel, start=False, stop=(j == 2))
                mm.then_inc(tmp_full, 1)

            def run_turn(turn):
                e = turn.e
                for pos in turn.places():
                    if pos in turn.units:
                        name, back, k0, n, c0, w, s = turn.units[pos]
                        off, u = turn.unit(pos)
                        pe.wait_ge(lo_ready, u + 1)
                        H = whi[off % SPL][:, 0:n * w].rearrange("p (k w) -> p k w", k=n)
                        L = wlo[off % SPL][:, 0:n * w].rearrange("p (k w) -> p k w", k=n)
                    if pos in turn.units and name != "moe_w_down":
                        if pos == 0:
                            pe.wait_ge(tmp_free, turn.k)
                        if pos % 6 == 0 and not (turn.kind == "first" and s < 2):
                            pe.wait_ge(hid_ready, e * 3 + (s - 1))
                        b = bank[turn.gate_bank(s) + pos % 2][:, 0:w]
                        for kc in range(n):
                            X, Y = xeh[:, k0 + kc, turn.slot, :], xel[:, k0 + kc, turn.slot, :]
                            pe.matmul(b, X, H[:, kc, :], start=(k0 + kc == 0), stop=False)
                            pe.matmul(b, X, L[:, kc, :], start=False, stop=False)
                            mm = pe.matmul(b, Y, H[:, kc, :], start=False, stop=(k0 + kc == DC - 1))
                        mm.then_inc(unit_used, 1)
                    elif pos in turn.units:
                        if pos % 6 == 4:
                            pe.wait_ge(tmp_free, turn.step(("t", s))[1] + 1)
                            if s == 0 and turn.kind != "first":
                                pe.wait_ge(y_lo, e * 2)
                        for i2 in range(n):
                            f = k0 + i2
                            X, Y = hh[:, f - 4 * s, :], hl[:, f - 4 * s, :]
                            for half in range(2):
                                b = bank[4 + half][:, :]
                                lo_, hi_ = half * 512, (half + 1) * 512
                                pe.matmul(b, X, H[:, i2, lo_:hi_], start=(f == 0), stop=False)
                                pe.matmul(b, X, L[:, i2, lo_:hi_], start=False, stop=False)
                                mm = pe.matmul(b, Y, H[:, i2, lo_:hi_], start=False, stop=(f == FE // P - 1))
                        mm.then_inc(unit_used, 1)
                    for ev in turn.events.get(pos, []):
                        kind, i2 = ev
                        if kind == "t":
                            off, k = turn.step(ev)
                            b = tmp_bank(off, k)
                            pe.wait_ge(hid_ready, e * 3 + (i2 + 1 - 3 * (i2 == 2)))
                            for c in range(STEPS[i2][1] // P):
                                mm = pe.transpose(b[:, c * P:(c + 1) * P], hid[:, c * P:(c + 1) * P], ident)
                            mm.then_inc(tmp_full, 1)
                        elif kind == "s":
                            off, k = turn.step(ev)
                            b = tmp_bank(off, k)
                            if i2 == 0:
                                pe.wait_ge(y_lo, e * 2)
                            pe.matmul(b[:, 0:T], yh[:, i2 * P:(i2 + 1) * P], pickT[:, :], start=True, stop=False)
                            pe.matmul(b[:, 0:T], yl[:, i2 * P:(i2 + 1) * P], pickT[:, :], start=False,
                                      stop=True).then_inc(tmp_full, 1)
                        elif kind == "p":
                            off, k = turn.step(ev)
                            b = tmp_bank(off, k)
                            for j, w in BLK:
                                pe.transpose(b[:, j * P:j * P + w].bitcast(F32R), pick[0:w, j, turn.slot, :], identr[0:w, 0:w])
                            for j, w in BLK:
                                pe.matmul(b[:, 272:272 + NE], pick[0:w, j, turn.slot, :], gh[0:w, j, :], start=(j == 0), stop=False)
                                mm = pe.matmul(b[:, 272:272 + NE], pick[0:w, j, turn.slot, :], gl[0:w, j, :], start=False,
                                               stop=(j == 2))
                            mm.then_inc(tmp_full, 1)
                        elif kind == "x":
                            off, k = turn.step(ev)
                            gather(i2, off, k, turn.pair + 2)

            def over_expert(e):
                pe.wait_ge(o_done, e * OVER_DVE + 1)
                for j, w in BLK:
                    mm = pe.matmul(bank[2][:, j * P:j * P + w], ocol[0:w, j:j + 1].to_broadcast([w, P]),
                                   ident[0:w, 0:w], start=True, stop=True)
                mm.then_inc(o_used, 1)
                for i in range(EC + DC):
                    pe.wait_ge(o_landed[0], e * (16 * (EC + DC)) + 16 * (i + 1))
                    pe.wait_ge(o_done, e * OVER_DVE + (i + 2))
                    if i < EC:
                        pe.wait_ge(o_landed[1], e * (16 * EC) + 16 * (i + 1))
                        for a in range(2):
                            for k in range(DC):
                                mm = pe.matmul(bank[a][:, 0:T], owt[:, a, k * P:(k + 1) * P], xn[:, k, :],
                                               start=(k == 0), stop=(k == DC - 1))
                    else:
                        for k in range(EC):
                            mm = pe.matmul(bank[0][:, 0:T], owt[:, 0, k * P:(k + 1) * P], ohid[:, k, :],
                                           start=(k == 0), stop=(k == EC - 1))
                    mm.then_inc(o_used, 1)

            pe.wait_ge(base_in, 80)
            for l in range(DEPTH):
                for j in range(10):
                    if j == 0:
                        pe.wait_ge(part_lo, PARTS_AT[3 * l] + DC)
                    unit_pair(U_MIX[l] + j, A_MIX[l] + 2 * j, xh, xl)
                    for name in AFTER[j]:
                        side_step(l, name)
                for name in AFTER[10]:
                    side_step(l, name)
                pe.wait_ge(side_free, SIDE[l, "wp3"] + 1)
                pe.wait_ge(mix_lo, RC * (l + 1))
                for j in range(4):
                    unit_pair(U_WO[l] + j, A_WO[l] + 2 * j, mh, ml)
                for name in LAST[l]:
                    side_step(l, name)
                if l == 0:
                    pe.wait_ge(part_lo, PARTS_AT[1] + DC)
                    feed_forward()
                else:
                    pe.wait_ge(acc_free, A_FF[1])
                    pe.wait_ge(side_free, SIDE_MOE)
                    pe.wait_ge(gate_lo, 1)
                    pe.wait_ge(identr_ready, 1)
                    for i in range(GATHERS):
                        gather(i, i, i, 1)
                    run_turn(Turn("first"))
                    with pe.Fori(0, (NE - 2) // 2) as pair:
                        for half in range(2):
                            run_turn(Turn("loop", pair, half))
                    run_turn(Turn("last"))
                    run_turn(Turn("tail"))
                    pe.wait_ge(hid_ready, 3 * NE)
                    pe.wait_ge(tmp_free, TMP_TAIL + 1 + DC)
                    with pe.If(pe.value_load(flag[0:1, 0:1], min_val=0, max_val=2 * T) > 0):
                        with pe.Fori(0, NE) as e:
                            over_expert(e)
                        pe.wait_ge(o_done, NE * OVER_DVE)
                u = U_PLE[l]
                pe.wait_ge(lo_ready, u + 1)
                pe.wait_ge(ple_lo, l + 1)
                for m in range(DC):
                    chunk(A_PLE[l] + m, A_PLE[l] + m, u, 2, D, m, ph, pl).then_inc(acc_full if m < DC - 1 else unit_used, 1)
                pe.wait_ge(part_lo, PARTS_AT[5 if l else 2] + DC)
                for j in range(4):
                    unit_pair(U_PLE[l] + 1 + j, A_PLE[l] + 8 + 2 * j, mh, ml)
            side_step(DEPTH, "norm1")

        @block.scalar
        def _(act):
            def hi(off, n, pair=0):
                act.wait_ge(raw_landed[off % RAW], pair * (16 * 2 * MOE_EACH // RAW) + 16 * (off // RAW + 1))
                if off >= SPL:
                    act.wait_ge(unit_used, pair * (2 * MOE_EACH) + (off - (SPL - 1)))
                act.activation(whi[off % SPL][:, 0:n], raw[off % RAW][:, 0:n], ACT.Copy).then_inc(hi_ready, 1)

            def ahead(u):
                if u + AHEAD < N_UNITS:
                    hi(u + AHEAD, cols[u + AHEAD])

            def finish(stage, m):
                h_final(act, stage, m)
                if stage in PARTS_AT:
                    dst = xh if stage in GAIN else mh
                    scale = gains[:, GAIN[stage], m:m + 1] if stage in GAIN else 1.0
                    act.activation(dst[:, m, :], h[:, m, :], ACT.Copy, scale=scale).then_inc(part_hi, 1)
                if stage in SQUARES_AT:
                    n = SQUARES_AT[stage] + m
                    if n >= 2:
                        act.wait_ge(ss_added, n - 1)
                    act.activation(sq[:, n % 2, :], h[:, m, :], ACT.Square).then_inc(sq_ready, 1)

            def norm(l, name):
                act.wait_ge(side_full, SIDE[l, name] + 1)
                i = SIDE[l, name] % 4
                act.activation(std[:, :], bank[4 + i][:, 0:T], ACT.Sqrt, bias=C("eps")).then_inc(std_ready, 1)

            def feed_forward():
                for half in range(2):
                    n = Count(half)
                    for i, (kind, c, w, a, _) in enumerate(PART):
                        hi(n.unit + i + AHEAD, part_cols[(i + AHEAD) % PART_UNITS])
                        for m in range(w):
                            if kind == "gate":
                                act.wait_ge(acc_free, n.chunk + (a + m + 1))
                                act.activation(tg[:, m, :], tg[:, m, :], ACT.Silu).then_inc(silu_f, 1)
                            elif kind == "up":
                                act.wait_ge(acc_free, n.chunk + (a + m + 1))
                                act.activation(fh[:, c + m, :], hv[:, m, :], ACT.Copy).then_inc(f_hi, 1)

            def wait_step(turn, ev):
                off, k = turn.step(ev)
                act.wait_ge(tmp_full, k + 1)
                return bank[6 + off % 2]

            def run_turn(turn):
                e = turn.e
                for pos in turn.places():
                    if pos in turn.units:
                        i = turn.at[pos]
                        hi(turn.u_at + i + AHEAD, turn_cols(turn, i + AHEAD), turn.pair)
                    if pos % 6 == 3 and pos in turn.units:
                        s = pos // 6
                        off, u = turn.unit(pos)
                        act.wait_ge(unit_used, u + 1)
                        n = STEPS[s][1]
                        b = bank[turn.gate_bank(s)]
                        act.activation(sgate[:, 0:n], b[:, 0:n], ACT.Silu).then_inc(sgate_ready, 1)
                    for ev in turn.events.get(pos, []):
                        kind, i = ev
                        if kind == "t":
                            b = wait_step(turn, ev)
                            n = STEPS[i][1]
                            act.activation(hh[:, 0:n // P, :].rearrange("p c s -> p (c s)"), b[:, 0:n],
                                           ACT.Copy).then_inc(hh_ready, 1)
                        elif kind == "y":
                            off, u = turn.unit(pos)
                            act.wait_ge(unit_used, u + 1)
                            for half in range(2):
                                act.activation(yh[:, half * 512:(half + 1) * 512], bank[4 + half][:, :], ACT.Copy,
                                               scale=gslot[:, 0:1]).then_inc(y_hi, 1)
                        elif kind == "x":
                            b = wait_step(turn, ev)
                            act.activation(xeh[:, 2 * i:2 * i + 2, :, :].rearrange("p c a s -> p (c a s)"), b[:, :],
                                           ACT.Copy).then_inc(xe_hi, 1)

            act.wait_ge(base_in, 80)
            for m in range(DC):
                finish(0, m)
                if m == 1:
                    hi(0, cols[0])
                if m == 4:
                    hi(1, cols[1])
            for l in range(DEPTH):
                for j in range(10):
                    ahead(U_MIX[l] + j)
                    if j == 0:
                        norm(l, "norm1")
                    if j >= 8:
                        for c in range(2 * (j - 8), 2 * (j - 8) + 2):
                            act.wait_ge(acc_free, A_MIX[l] + 16 + c + 1)
                            act.activation(sg[:, c, :], sg[:, c, :], ACT.Silu).then_inc(silu_g, 1)
                for g in range(PC):
                    i = SIDE[l, f"wp{g}"]
                    act.wait_ge(side_full, i + 1)
                    act.activation(mh[:, g, :], bank[4 + i % 4][:, 0:T], ACT.Copy,
                                   scale=pscale[:, l, g:g + 1]).then_inc(mix_hi, 1)
                for c in range(RC):
                    act.wait_ge(side_free, SIDE[l, f"mu{c}"] + 1)
                    act.activation(osq[:, c, :], oc[:, c, :], ACT.Square).then_inc(osq_ready, 1)
                for c in range(RC):
                    i = SIDE[l, f"va{c}"]
                    act.wait_ge(side_full, i + 1)
                    if c >= 2:
                        act.wait_ge(on_ready, RC * l + c - 1)
                    act.activation(stdv[:, c % 2, :], bank[4 + i % 4][:, 0:T], ACT.Sqrt,
                                   bias=C("eps")).then_inc(stdv_ready, 1)
                for c in range(RC):
                    act.wait_ge(on_ready, RC * l + c + 1)
                    act.activation(mh[:, PC + c, :], og[:, c, :], ACT.Copy).then_inc(mix_hi, 1)
                act.wait_ge(side_free, SIDE[l, "bc3"] + 1)
                act.activation(ph[:, :, :].rearrange("p a n -> p (a n)"), pin[:, :, :].rearrange("p a n -> p (a n)"),
                               ACT.Copy).then_inc(ple_hi, 1)
                for j in range(4):
                    ahead(U_WO[l] + j)
                    for m in (2 * j, 2 * j + 1):
                        finish(4 if l else 1, m)
                norm(l, "norm2")
                act.wait_ge(state_out, 64 * (l + 1))
                if l:
                    act.wait_ge(dm_ready, 1)
                    act.activation(w1[:, :], dm[:, :], ACT.Sigmoid)
                    act.activation(w2[:, :], dm[:, :], ACT.Sigmoid, scale=-1.0).then_inc(sig_ready, 1)
                    act.activation(identr[:, :], ident, ACT.Copy).then_inc(identr_ready, 1)
                    for i in range(6):
                        j, half = divmod(i, 2)
                        w = BLK[j][1]
                        act.wait_ge(side_full, SIDE[1, f"tr{i}"] + 1)
                        act.activation(xth[0:w, j, half * 512:(half + 1) * 512], bank[4 + SIDE[1, f"tr{i}"] % 4][0:w, :],
                                       ACT.Copy).then_inc(xt_hi, 1)
                    act.wait_ge(routed, 2)
                    act.activation(gh[:, :, :].rearrange("p a n -> p (a n)"), r["gate"][:, :, :].rearrange("p a n -> p (a n)"),
                                   ACT.Copy).then_inc(gate_hi, 1)
                    for i in range(GATHERS):
                        act.wait_ge(tmp_full, i + 1)
                        act.activation(xeh[:, 2 * i:2 * i + 2, :, :].rearrange("p c a s -> p (c a s)"),
                                       bank[6 + i % 2][:, :], ACT.Copy).then_inc(xe_hi, 1)
                    run_turn(Turn("first"))
                    with act.Fori(0, (NE - 2) // 2) as pair:
                        for half in range(2):
                            run_turn(Turn("loop", pair, half))
                    run_turn(Turn("last"))
                    run_turn(Turn("tail"))
                    act.wait_ge(side_free, SIDE_MOE)
                    with act.If(act.value_load(flag[0:1, 0:1], min_val=0, max_val=2 * T) > 0):
                        with act.Fori(0, NE) as e:
                            for i in range(EC):
                                act.wait_ge(o_used, e * OVER_PE + (i + 2))
                                act.activation(osg[:, :], bank[0][:, 0:T], ACT.Silu).then_inc(o_silu, 1)
                        act.wait_ge(o_done, NE * OVER_DVE)
                else:
                    feed_forward()
                for m in range(DC):
                    finish(5 if l else 2, m)
                ahead(U_PLE[l])
                for j in range(4):
                    ahead(U_PLE[l] + 1 + j)
                    for m in (2 * j, 2 * j + 1):
                        n = A_PLE[l] + 8 + m
                        chunk_full(act, n)
                        if DC * l + m >= 2:
                            act.wait_ge(ge_ready, DC * l + m - 1)
                        act.activation(sgp[:, m % 2, :], bank[n % 4][:, 0:T], ACT.Sigmoid).then_inc(gate_ready, 1)
                    for m in (2 * j, 2 * j + 1):
                        finish(6 if l else 3, m)
            norm(DEPTH, "norm1")

        @block.vector
        def _(dve):
            steps = 0

            def step(ins):
                nonlocal steps
                steps += 1
                ins.then_inc(dve_step, 1)
                dve.wait_ge(dve_step, steps)

            def lo(off, n, u=None):
                u = off if u is None else u
                dve.wait_ge(hi_ready, u + 1)
                dve.tensor_tensor(wlo[off % SPL][:, 0:n], raw[off % RAW][:, 0:n],
                                  whi[off % SPL][:, 0:n].bitcast(F32), ALU.subtract).then_inc(lo_ready, 1)

            def ahead(u):
                if u + AHEAD < N_UNITS:
                    lo(u + AHEAD, cols[u + AHEAD])

            def finish(stage, m):
                n = PARTS_AT[stage] + m
                dve.wait_ge(part_hi, n + 1)
                if stage in GAIN:
                    dve.scalar_tensor_tensor(out=xl[:, m, :], in0=h[:, m, :], scalar=gains[:, GAIN[stage], m:m + 1],
                                             in1=xh[:, m, :].bitcast(F32), op0=ALU.mult,
                                             op1=ALU.subtract).then_inc(part_lo, 1)
                else:
                    dve.tensor_tensor(ml[:, m, :], h[:, m, :], mh[:, m, :].bitcast(F32), ALU.subtract).then_inc(part_lo, 1)

            def feed_forward():
                for half in range(2):
                    n = Count(half)
                    for i, (kind, c, w, a, full) in enumerate(PART):
                        j = i + AHEAD
                        lo(n.unit + j, part_cols[j % PART_UNITS], n.unit + j)
                        for m in range(w):
                            if m < w - 1:
                                dve.wait_ge(acc_full, n.full + (full + 1))
                            else:
                                dve.wait_ge(unit_used, n.unit + (i + 1))
                            b = bank[(n.chunk + a + m) % 4][:, 0:T]
                            if kind == "gate":
                                dve.tensor_tensor(tg[:, m, :], b, rstd[:, :], ALU.mult).then_inc(acc_free, 1)
                            elif kind == "up":
                                dve.wait_ge(scaled_f, n.hidden + (c + m + 1))
                                dve.tensor_tensor(hv[:, m, :], b, tg[:, m, :], ALU.mult).then_inc(acc_free, 1)
                            else:
                                dve.tensor_tensor(h[:, c, :], h[:, c, :], b, ALU.add).then_inc(acc_free, 1)
                        if kind == "up":
                            for m in range(w):
                                dve.wait_ge(f_hi, n.hidden + (c + m + 1))
                                dve.tensor_tensor(fl[:, c + m, :], hv[:, m, :], fh[:, c + m, :].bitcast(F32),
                                                  ALU.subtract).then_inc(f_lo, 1)

            def side(l, name):
                i = SIDE[l, name]
                dve.wait_ge(side_full, i + 1)
                return bank[4 + i % 4]

            def side_step(l, name):
                if name in ("norm1", "norm2"):
                    dve.wait_ge(std_ready, NORM_ORDER[l, name] + 1)
                    step(dve.reciprocal(rstd[:, :], std[:, :]))
                    dve.tensor_scalar(rstd8[:, :], rstd[:, :], float(HD) ** -0.5, None, ALU.mult).then_inc(side_free, 1)
                    dve.wait_ge(side_free, SIDE[l, name] + 1)
                    return
                b = side(l, name)
                if name[:2] in ("rq", "rk"):
                    a, c = int(name[1] == "k"), int(name[2])
                    i = SIDE[l, name]
                    dve.tensor_tensor(rt[:, c % 2, :], b[:, 0:T], C("sin"), ALU.mult).then_inc(side_free, 1)
                    dve.wait_ge(side_free, i + 1)
                    dve.wait_ge(cosed, 8 * l + 4 * a + c + 1)
                    dve.tensor_tensor(qk[:, a, c, :], qk[:, a, c, :], rt[:, c % 2, :], ALU.add).then_inc(roped, 1)
                    return
                if name[:2] == "kt":
                    last = dve.tensor_tensor(kz[:, int(name[2]), :].rearrange("p (a d) -> p a d", a=HEADS),
                                             b[:, :].rearrange("p (a d) -> p a d", a=HEADS),
                                             C("zeta").unsqueeze(2).to_broadcast([P, HEADS, HD]), ALU.mult)
                elif name[:2] == "vt":
                    last = dve.tensor_copy(vpad[:, int(name[2]), :, 0:3:2, :],
                                           b[:, :].rearrange("p (c a e) -> p c a e", c=RC, a=2))
                elif name == "vs":
                    dve.wait_ge(zeroed, 5 * (l + 1))
                    src = b[0:NS, :].rearrange("p (c a e) -> p c a e", c=RC, a=2)
                    dve.tensor_copy(vs2[0:NS, :, :], src[:, :, 0, :])
                    last = dve.tensor_copy(vs2[32:32 + NS, :, :], src[:, :, 1, :])
                elif name[:2] == "sc":
                    hp = int(name[3])
                    last = dve.tensor_tensor(sc[:, hp, :, :], b[:, :].rearrange("p (c n) -> p c n", c=RC),
                                             decay[:, hp, :, :], ALU.mult)
                elif name == "win":
                    last = dve.tensor_tensor(wsum[:, :, PAD + NP:], b[:, 0:PC * NS].rearrange("p (g s) -> p g s", g=PC),
                                             upad[:, :, PAD + NP:], ALU.add)
                elif name == "S1":
                    dve.wait_ge(zeroed, 5 * (l + 1))
                    for hp in range(2):
                        rows = slice(hp * HD, (hp + 1) * HD)
                        last = dve.tensor_copy(sbd[rows, :, rows], b[rows, :].rearrange("p (c n) -> p c n", c=RC)[:, :, rows])
                elif name == "S2":
                    dve.wait_ge(side_free, SIDE[l, "S1"] + 1)
                    for hp in range(2):
                        rows = slice(hp * HD, (hp + 1) * HD)
                        decay_c = C("gchunk")[rows, :].unsqueeze(2).to_broadcast([HD, RC, HD])
                        step(dve.tensor_tensor(s2[rows, :, :], sbd[rows, :, rows], decay_c, ALU.mult))
                        last = dve.tensor_tensor(s2[rows, :, :], s2[rows, :, :],
                                                 b[rows, :].rearrange("p (c n) -> p c n", c=RC)[:, :, rows], ALU.add)
                elif name in ("o0", "o1"):
                    a = int(name[1]) * CH
                    last = dve.tensor_copy(o[:, :, a:a + CH], b[:, :].rearrange("p (c n) -> p c n", c=RC))
                elif name[:2] == "bc":
                    i = int(name[2])
                    if i >= 2:
                        dve.wait_ge(s_ready, 4 * l + i - 1)
                    k = qk[:, 1, :, NP + 2 * i:NP + 2 * i + 2].rearrange("p c s -> p s c")
                    last = dve.tensor_tensor(kv[:, i % 2, :, :, :],
                                             b[:, :].rearrange("p (s c e) -> p s c e", s=2, c=RC),
                                             k.unsqueeze(3).to_broadcast([P, 2, RC, HD]), ALU.mult)
                elif name == "qS":
                    src = b[0:HD, 0:2 * NS * RC].rearrange("p (s c a) -> p a c s", s=NS, c=RC)
                    dve.tensor_copy(o[0:HD, :, NP:T], src[:, 0, :, :])
                    last = dve.tensor_copy(o[HD:P, :, NP:T], src[:, 1, :, :])
                elif name == "tail":
                    last = dve.tensor_copy(utail[:, :], b[0:BUF + NS, :])
                elif name[:2] == "wp":
                    g = int(name[2])
                    dve.wait_ge(mix_hi, 8 * l + g + 1)
                    last = dve.scalar_tensor_tensor(out=ml[:, g, :], in0=b[:, 0:T], scalar=pscale[:, l, g:g + 1],
                                                    in1=mh[:, g, :].bitcast(F32), op0=ALU.mult, op1=ALU.subtract)
                elif name[:2] == "mu":
                    c = int(name[2])
                    if c == 0:
                        dve.wait_ge(side_free, SIDE[l, "qS"] + 1)
                    last = dve.tensor_tensor(oc[:, c, :], o[:, c, :], b[:, 0:T], ALU.subtract)
                elif name[:2] == "va":
                    c = int(name[2])
                    dve.wait_ge(stdv_ready, RC * l + c + 1)
                    dve.reciprocal(stdv[:, c % 2, :], stdv[:, c % 2, :]).then_inc(side_free, 1)
                    dve.wait_ge(side_free, SIDE[l, name] + 1)
                    dve.wait_ge(og_ready, RC * l + c + 1)
                    dve.tensor_tensor(og[:, c, :], og[:, c, :], stdv[:, c % 2, :], ALU.mult).then_inc(on_ready, 1)
                    if c:
                        mix_part(l, c - 1)
                    return
                last.then_inc(side_free, 1)

            def mix_part(l, c):
                dve.wait_ge(mix_hi, 8 * l + PC + c + 1)
                dve.tensor_tensor(ml[:, PC + c, :], og[:, c, :], mh[:, PC + c, :].bitcast(F32),
                                  ALU.subtract).then_inc(mix_lo, 1)

            def z_chunk(l, c):
                n = A_MIX[l] + c
                chunk_full(dve, n)
                part, i = divmod(c, 4)
                dst = (qk[:, 0, i, :], qk[:, 1, i, :], v[:, i, :], upad[:, i, PAD:PAD + T], sg[:, i, :])[part]
                scale = rstd8 if part == 1 else rstd
                dve.tensor_tensor(dst, bank[n % 4][:, 0:T], scale[:, :], ALU.mult).then_inc(acc_free, 1)

            def pool_diff(l, g):
                dve.wait_ge(wsummed, PC * l + g + 1)
                dve.wait_ge(side_free, SIDE[l, "win"] + 1)
                early = C("early").rearrange("p (g n) -> p g n", g=PC)[:, g, :]
                step(dve.tensor_tensor(wsum[:, g, PAD:2 * PAD], wsum[:, g, PAD:2 * PAD], early, ALU.mult))
                dve.scalar_tensor_tensor(out=wsum[:, g, PAD:], in0=wsum[:, g, PAD:], scalar=1.0 / WINDOWS[g],
                                         in1=upad[:, g, PAD:], op0=ALU.mult, op1=ALU.subtract).then_inc(d_ready, 1)

            def add_h(n, m, src=None):
                if src is None:
                    chunk_full(dve, n)
                    src = bank[n % 4][:, 0:T]
                dve.tensor_tensor(h[:, m, :], h[:, m, :], src, ALU.add).then_inc(acc_free, 1)

            def route():
                def bc(x):
                    return x[:, :].unsqueeze(2).to_broadcast([P, 3, NE])

                tie = C("tie").unsqueeze(1).to_broadcast([P, 3, NE])
                dve.wait_ge(moe_zeroed, 1)
                b = side(1, "lg")
                for j, w in BLK:
                    last = dve.tensor_copy(r["lg"][0:w, j, :], b[0:w, j * NE:(j + 1) * NE])
                last.then_inc(side_free, 1)
                dve.wait_ge(side_free, SIDE[1, "lg"] + 1)

                def best(src, top, out):
                    step(dve.tensor_reduce(top[:, :], src[:, :, :], AX_X, ALU.max))
                    step(dve.tensor_tensor(r["eq"][:, :, :], src[:, :, :], bc(top), ALU.is_equal))
                    step(dve.tensor_tensor(r["key"][:, :, :], r["eq"][:, :, :], tie, ALU.mult))
                    step(dve.tensor_reduce(kx[:, :], r["key"][:, :, :], AX_X, ALU.max))
                    step(dve.tensor_tensor(out[:, :, :], r["key"][:, :, :], bc(kx), ALU.is_equal))

                best(r["lg"], m1, r["one"])
                step(dve.scalar_tensor_tensor(out=r["lg2"][:, :, :], in0=r["one"][:, :, :], scalar=-3.0e38,
                                              in1=r["lg"][:, :, :], op0=ALU.mult, op1=ALU.add))
                best(r["lg2"], m2, r["two"])
                dve.tensor_tensor(dm[:, :], m1[:, :], m2[:, :], ALU.subtract).then_inc(dm_ready, 1)
                step(dve.tensor_tensor(r["sel"][:, :, :], r["one"][:, :, :], r["two"][:, :, :], ALU.add))
                dve.tensor_tensor(r["sel"][:, :, :], r["sel"][:, :, :],
                                  C("valid").unsqueeze(2).to_broadcast([P, 3, NE]), ALU.mult).then_inc(routed, 1)
                for i in range(6):
                    j, half = divmod(i, 2)
                    w = BLK[j][1]
                    b = side(1, f"tr{i}")
                    dve.wait_ge(xt_hi, i + 1)
                    dve.tensor_tensor(xtl[0:w, j, half * 512:(half + 1) * 512], b[0:w, :],
                                      xth[0:w, j, half * 512:(half + 1) * 512].bitcast(F32), ALU.subtract).then_inc(side_free, 1)
                dve.wait_ge(sig_ready, 1)
                step(dve.tensor_tensor(r["gate"][:, :, :], r["one"][:, :, :], bc(w1), ALU.mult))
                step(dve.tensor_tensor(r["t2"][:, :, :], r["two"][:, :, :], bc(w2), ALU.mult))
                dve.tensor_tensor(r["gate"][:, :, :], r["gate"][:, :, :], r["t2"][:, :, :], ALU.add).then_inc(routed, 1)
                dve.wait_ge(routed, 2)
                b = side(1, "pos")
                step(dve.scalar_tensor_tensor(out=r["t2"][:, :, :], in0=b[:, 0:3 * NE].rearrange("p (a n) -> p a n", a=3),
                                              scalar=1.0, in1=r["sel"][:, :, :], op0=ALU.add, op1=ALU.mult))
                dve.tensor_scalar(r["pos"][:, :, :], r["t2"][:, :, :], -1.0, None, ALU.add).then_inc(side_free, 1)
                dve.wait_ge(side_free, SIDE[1, "pos"] + 1)
                picks(0, 1)
                dve.wait_ge(gate_hi, 1)
                dve.tensor_tensor(gl[:, :, :], r["gate"][:, :, :], gh[:, :, :].bitcast(F32), ALU.subtract).then_inc(gate_lo, 1)
                step(dve.tensor_scalar(r["key"][:, :, :], r["pos"][:, :, :], float(CAP), None, ALU.is_ge))
                dve.tensor_tensor(r["over"][:, :, :], r["key"][:, :, :], r["gate"][:, :, :], ALU.mult)
                dve.tensor_reduce(over1[:, :], r["key"][:, :, :].rearrange("p a n -> p (a n)"), AX_X, ALU.add).then_inc(over_ready, 1)
                dve.tensor_copy(flag[:, :], side(1, "over")[0:1, 0:1]).then_inc(side_free, 1)

            def picks(e, count):
                pos = r["pos"][:, :, e:e + 2] if isinstance(e, int) else r["pos"][:, :, bass.ds(e, 2)]
                dve.tensor_copy(pose[:, :, :], pos).then_inc(pose_ready, 1)
                dve.wait_ge(pose_ready, count)
                dve.tensor_tensor(pick[:, :, :, :].rearrange("p j a n -> p (j a) n"),
                                  C("iota").unsqueeze(1).to_broadcast([P, 6, P]),
                                  pose[:, :, :].rearrange("p j a -> p (j a)").unsqueeze(2).to_broadcast([P, 6, P]),
                                  ALU.is_equal).then_inc(pick_ready, 1)

            def wait_step(turn, ev):
                off, k = turn.step(ev)
                dve.wait_ge(tmp_full, k + 1)
                return bank[6 + off % 2]

            def gathered(i, b, count):
                dve.wait_ge(xe_hi, count)
                dve.tensor_tensor(xel[:, 2 * i:2 * i + 2, :, :].rearrange("p c a s -> p (c a s)"), b[:, :],
                                  xeh[:, 2 * i:2 * i + 2, :, :].rearrange("p c a s -> p (c a s)").bitcast(F32),
                                  ALU.subtract).then_inc(tmp_free, 1)

            def run_turn(turn):
                e = turn.e
                for pos in turn.places():
                    if pos in turn.units:
                        i = turn.at[pos]
                        lo(turn.u_at + i + AHEAD, turn_cols(turn, i + AHEAD), turn.u + i + AHEAD)
                    if pos % 6 == 3 and pos in turn.units:
                        s = pos // 6
                        n = STEPS[s][1]
                        dve.wait_ge(sgate_ready, e * 3 + (s + 1))
                        b = bank[turn.gate_bank(s) + 1]
                        dve.tensor_tensor(hid[:, 0:n], sgate[:, 0:n], b[:, 0:n], ALU.mult).then_inc(hid_ready, 1)
                    for ev in turn.events.get(pos, []):
                        kind, i = ev
                        if kind == "t":
                            b = wait_step(turn, ev)
                            n = STEPS[i][1]
                            dve.wait_ge(hh_ready, e * 3 + (i + 1 - 3 * (i == 2)))
                            dve.tensor_tensor(hl[:, 0:n // P, :].rearrange("p c s -> p (c s)"), b[:, 0:n],
                                              hh[:, 0:n // P, :].rearrange("p c s -> p (c s)").bitcast(F32),
                                              ALU.subtract).then_inc(tmp_free, 1)
                        elif kind == "y":
                            for half in range(2):
                                dve.wait_ge(y_hi, e * 2 + (half - 1))
                                dve.scalar_tensor_tensor(out=yl[:, half * 512:(half + 1) * 512], in0=bank[4 + half][:, :],
                                                         scalar=gslot[:, 0:1],
                                                         in1=yh[:, half * 512:(half + 1) * 512].bitcast(F32),
                                                         op0=ALU.mult, op1=ALU.subtract).then_inc(y_lo, 1)
                        elif kind == "s":
                            b = wait_step(turn, ev)
                            dve.tensor_tensor(h[:, i, :], h[:, i, :], b[:, 0:T], ALU.add).then_inc(tmp_free, 1)
                        elif kind == "p":
                            b = wait_step(turn, ev)
                            dve.tensor_copy(pickT[:, :], b[:, 0:T])
                            gate = b[:, 272 + e:273 + e] if isinstance(e, int) else b[:, bass.ds(e + 272, 1)]
                            dve.tensor_copy(gslot[:, :], gate).then_inc(tmp_free, 1)
                        elif kind == "k":
                            picks(e + 1, turn.pair + 2)
                        elif kind == "x":
                            gathered(i, wait_step(turn, ev), turn.pair * GATHERS + (GATHERS + i + 1))

            def over_expert(e):
                dve.tensor_copy(ocol[:, :].unsqueeze(2), r["over"][:, :, bass.ds(e, 1)]).then_inc(o_done, 1)
                dve.wait_ge(o_used, e * OVER_PE + 1)
                dve.tensor_copy(orow[:, :], bank[2][:, 0:T]).then_inc(o_done, 1)
                for i in range(EC):
                    dve.wait_ge(o_silu, e * EC + (i + 1))
                    dve.tensor_tensor(ohid[:, i, :], osg[:, :], bank[1][:, 0:T], ALU.mult).then_inc(o_done, 1)
                for m in range(DC):
                    dve.wait_ge(o_used, e * OVER_PE + (EC + m + 2))
                    dve.tensor_tensor(osg[:, :], bank[0][:, 0:T], orow[:, :], ALU.mult).then_inc(o_scaled, 1)
                    dve.wait_ge(o_scaled, e * DC + (m + 1))
                    dve.tensor_tensor(h[:, m, :], h[:, m, :], osg[:, :], ALU.add).then_inc(o_done, 1)

            dve.wait_ge(base_in, 80)
            for m in range(DC):
                finish(0, m)
                if m == 1:
                    lo(0, cols[0])
                if m == 4:
                    lo(1, cols[1])
            for l in range(DEPTH):
                for j in range(10):
                    ahead(U_MIX[l] + j)
                    if j == 0:
                        side_step(l, "norm1")
                    for c in (2 * j, 2 * j + 1):
                        z_chunk(l, c)
                    for name in AFTER[j]:
                        if name == "norm1":
                            continue
                        if name == "wp0":
                            for g in range(PC):
                                pool_diff(l, g)
                        side_step(l, name)
                    if j == 6:
                        dve.tensor_tensor(qxi[:, :, :], qk[:, 0, :, CH:2 * CH], xi, ALU.mult).then_inc(qxi_ready, 1)
                for name in AFTER[10]:
                    side_step(l, name)
                mix_part(l, RC - 1)
                dve.wait_ge(ple_hi, l + 1)
                dve.tensor_tensor(pl[:, :, :], pin[:, :, :], ph[:, :, :].bitcast(F32), ALU.subtract).then_inc(ple_lo, 1)
                for j in range(4):
                    ahead(U_WO[l] + j)
                    for m in (2 * j, 2 * j + 1):
                        add_h(A_WO[l] + m, m)
                    if l == 0:
                        for m in (2 * j, 2 * j + 1):
                            finish(1, m)
                side_step(l, "norm2")
                if l == 0:
                    feed_forward()
                else:
                    dve.wait_ge(state_out, 128)
                    for m in range(DC):
                        dve.scalar_tensor_tensor(out=xn[:, m, :], in0=h[:, m, :], scalar=gains[:, 3, m:m + 1],
                                                 in1=rstd[:, :], op0=ALU.mult, op1=ALU.mult).then_inc(xn_ready, 1)
                    route()
                    for i in range(GATHERS):
                        dve.wait_ge(tmp_full, i + 1)
                        gathered(i, bank[6 + i % 2], i + 1)
                    run_turn(Turn("first"))
                    with dve.Fori(0, (NE - 2) // 2) as pair:
                        for half in range(2):
                            run_turn(Turn("loop", pair, half))
                    run_turn(Turn("last"))
                    run_turn(Turn("tail"))
                    with dve.If(dve.value_load(flag[0:1, 0:1], min_val=0, max_val=2 * T) > 0):
                        with dve.Fori(0, NE) as e:
                            over_expert(e)
                for m in range(DC):
                    finish(5 if l else 2, m)
                ahead(U_PLE[l])
                for m in range(DC):
                    n = A_PLE[l] + m
                    chunk_full(dve, n)
                    dve.tensor_copy(esb[:, m, :], bank[n % 4][:, 0:T]).then_inc(acc_free, 1)
                for j in range(4):
                    ahead(U_PLE[l] + 1 + j)
                    for m in (2 * j, 2 * j + 1):
                        dve.wait_ge(ge_ready, DC * l + m + 1)
                        add_h(None, m, esb[:, m, :])
                    if l == 0:
                        for m in (2 * j, 2 * j + 1):
                            finish(3, m)
            side_step(DEPTH, "norm1")
            for m in range(DC):
                dve.scalar_tensor_tensor(out=h[:, m, :], in0=h[:, m, :], scalar=gains[:, 4, m:m + 1], in1=rstd[:, :],
                                         op0=ALU.mult, op1=ALU.mult).then_inc(y_ready, 1)

        @block.gpsimd
        def _(pool):
            steps = 0

            def step(ins):
                nonlocal steps
                steps += 1
                ins.then_inc(pool_step, 1)
                pool.wait_ge(pool_step, steps)

            def add_square(stage, m):
                n = SQUARES_AT[stage] + m
                pool.wait_ge(sq_ready, n + 1)
                if m == 0:
                    pool.tensor_copy(ssum[:, :], sq[:, n % 2, :]).then_inc(ss_added, 1)
                else:
                    pool.wait_ge(ss_added, n)
                    pool.tensor_tensor(ssum[:, :], ssum[:, :], sq[:, n % 2, :], ALU.add).then_inc(ss_added, 1)

            def square_sum(stage):
                for m in range(DC):
                    add_square(stage, m)

            def feed_forward():
                for half in range(2):
                    n = Count(half)
                    for f in range(EC):
                        pool.wait_ge(silu_f, n.hidden + (f + 1))
                        pool.tensor_tensor(tg[:, f % 2, :], tg[:, f % 2, :], rstd[:, :], ALU.mult).then_inc(scaled_f, 1)

            square_sum(0)
            for l in range(DEPTH):
                if l:
                    pool.wait_ge(acc_free, A_MIX[l])
                pool.dma_start(S[:, :, :, :], t["state_ret"][l].rearrange("s (c a) d e -> (a d) s c e", a=2)).then_inc(layer_in, 16)
                pool.dma_start(buf[:, :], t["state_pool"][l].rearrange("s r w -> (s r) w")).then_inc(layer_in, 16)
                pool.dma_start(wpool[:, :, :], t["w_pool"][l].rearrange("g c d -> c g d")).then_inc(layer_in, 16)
                pool.dma_start(selb[:, :, :], t["selb"]).then_inc(layer_in, 16)
                pool.dma_start(pin[:, :, :], t["p"][:, l, :, :]).then_inc(layer_in, 16)
                pool.dma_start(t["new_pool_sample"][l][:, 0:BUF - 1, :], t["state_pool"][l][:, 1:BUF, :]).then_inc(pool_kept, 16)
                pool.memset(upad[:, :, 0:PAD], 0.0).then_inc(zeroed, 1)
                pool.memset(sbd[:, :, :], 0.0).then_inc(zeroed, 1)
                pool.memset(vpad[:, :, :, 1, :], 0.0).then_inc(zeroed, 1)
                pool.memset(vs2[:, :, :], 0.0).then_inc(zeroed, 1)
                pool.memset(qm[:, :, :, :], 0.0).then_inc(zeroed, 1)
                pool.wait_ge(layer_in, 80 * (l + 1))
                pool.tensor_tensor(S[:, :, :, :].rearrange("p s c e -> p s c e"), S[:, :, :, :],
                                   C("gamma").unsqueeze(1).unsqueeze(3).to_broadcast([P, NS, RC, HD]),
                                   ALU.mult).then_inc(s_decayed, 1)
                for a, name in enumerate(("rq", "rk")):
                    for c in range(RC):
                        pool.wait_ge(side_full, SIDE[l, f"{name}{c}"] + 1)
                        pool.tensor_tensor(qk[:, a, c, :], qk[:, a, c, :], C("cos"), ALU.mult).then_inc(cosed, 1)
                pool.wait_ge(roped, 8 * l + 4)
                pool.wait_ge(zeroed, 5 * (l + 1))
                pool.wait_ge(cosed, 8 * (l + 1))
                for a in range(2):
                    rows = slice(a * HD, (a + 1) * HD)
                    pool.tensor_copy(qm[rows, :, :, a], qk[rows, 0, :, NP:T].rearrange("p c s -> p s c")).then_inc(qm_ready, 1)
                    pool.wait_ge(qm_ready, 2 * l + a + 1)
                pool.wait_ge(side_full, SIDE[l, "vs"] + 1)
                wtmp = sq[:, :, :].rearrange("p a n -> p (a n)")
                pool.wait_ge(acc_free, A_MIX[l] + 16)
                for g in range(PC):
                    src, width = upad[:, g, :], 1
                    to_tmp = g % 2 == 1
                    while width < WINDOWS[g]:
                        dst = wtmp if to_tmp else wsum[:, g, :]
                        a = 2 * width - 1
                        ins = pool.tensor_tensor(dst[:, a:PAD + NP], src[:, a:PAD + NP], src[:, a - width:PAD + NP - width],
                                                 ALU.add)
                        width *= 2
                        if width == WINDOWS[g]:
                            ins.then_inc(wsummed, 1)
                            pool.wait_ge(wsummed, PC * l + g + 1)
                        else:
                            step(ins)
                        src, to_tmp = dst, not to_tmp
                pool.wait_ge(s_decayed, l + 1)
                for i in range(4):
                    pool.wait_ge(side_free, SIDE[l, f"bc{i}"] + 1)
                    pool.tensor_tensor(S[:, 2 * i:2 * i + 2, :, :], S[:, 2 * i:2 * i + 2, :, :], kv[:, i % 2, :, :, :],
                                       ALU.add).then_inc(s_ready, 1)
                pool.wait_ge(side_free, SIDE[l, "S2"] + 1)
                pool.dma_start(t["new_ret_prompt"][l, 0].rearrange("(c a) d e -> (a d) c e", a=2), s2[:, :, :]).then_inc(state_out, 16)
                pool.wait_ge(s_ready, 4 * (l + 1))
                pool.dma_start(t["new_ret_sample"][l].rearrange("s (c a) d e -> (a d) s c e", a=2), S[:, :, :, :]).then_inc(state_out, 16)
                pool.wait_ge(side_free, SIDE[l, "tail"] + 1)
                pool.dma_start(t["new_pool_prompt"][l, 0], utail[0:BUF, :]).then_inc(state_out, 16)
                pool.dma_start(t["new_pool_sample"][l][:, BUF - 1, :], utail[BUF:BUF + NS, :]).then_inc(state_out, 16)
                for c in range(RC):
                    pool.wait_ge(side_free, SIDE[l, f"mu{c}"] + 1)
                    pool.wait_ge(silu_g, RC * (l + 1))
                    pool.tensor_tensor(og[:, c, :], oc[:, c, :], sg[:, c, :], ALU.mult).then_inc(og_ready, 1)
                if l:
                    pool.wait_ge(state_out, 128)
                    pool.memset(r["lg"][:, :, :], 0.0).then_inc(moe_zeroed, 1)
                square_sum(4 if l else 1)
                if l == 0:
                    pool.wait_ge(side_free, SIDE[0, "norm2"] + 1)
                    feed_forward()
                for m in range(DC):
                    pool.wait_ge(acc_free, A_PLE[l] + m + 1)
                    pool.wait_ge(gate_ready, DC * l + m + 1)
                    pool.tensor_tensor(esb[:, m, :], esb[:, m, :], sgp[:, m % 2, :], ALU.mult).then_inc(ge_ready, 1)
                    if m % 2 and m > 1:
                        add_square(6 if l else 3, m - 3)
                        add_square(6 if l else 3, m - 2)
                add_square(6 if l else 3, DC - 2)
                add_square(6 if l else 3, DC - 1)
            pool.wait_ge(pool_kept, 32)
            pool.wait_ge(state_out, 128)


_OUTS = {"y": [P, DC, T], "new_pool_prompt": [DEPTH, 1, BUF, POOL_W],
         "new_ret_prompt": [DEPTH, 1, HEADS, HD, HD], "new_pool_sample": [DEPTH, NS, BUF, POOL_W],
         "new_ret_sample": [DEPTH, NS, HEADS, HD, HD]}


def kernel(**inputs):
    import concourse.bacc as bacc
    from concourse.bass_utils import run_bass_kernel_spmd

    a = {k: np.asarray(v) for k, v in inputs.items()}

    def columns(prompt, sample, width):
        x = np.concatenate([prompt.reshape(-1, width), sample.reshape(-1, width)])
        return np.ascontiguousarray(x.T.reshape(width // P, P, -1).transpose(1, 0, 2))

    def by_partition(rows):
        return np.ascontiguousarray(rows.reshape(rows.shape[0], -1, P).transpose(2, 0, 1))

    arrays = {
        "x": columns(a["x_prompt"], a["x_sample"], D),
        "p": np.ascontiguousarray(np.stack([columns(a["p_prompt"][l], a["p_sample"][l], PLE) for l in range(DEPTH)], 1)),
        "gains": by_partition(np.concatenate([a["norm1"], a["norm2"], a["final_norm"][None]])),
        "pscale": by_partition(a["pool_scale"]),
        "const": constants(),
        "selb": sample_rows(),
    }
    for name in ("state_pool", "state_ret", "w_in", "w_pool", "w_o", "ffn_w_gate", "ffn_w_up", "ffn_w_down",
                 "moe_router", "moe_w_gate", "moe_w_up", "moe_w_down", "w_ple", "w_ple_gate"):
        arrays[name] = np.ascontiguousarray(a[name])
    nc = bacc.Bacc("TRN2", target_bir_lowering=False, num_devices=1)
    t = {k: nc.dram_tensor(f"in_{k}", list(x.shape), F32, kind="ExternalInput").ap() for k, x in arrays.items()}
    t |= {k: nc.dram_tensor(f"out_{k}", s, F32, kind="ExternalOutput").ap() for k, s in _OUTS.items()}
    program(nc, t)
    got = run_bass_kernel_spmd(nc, [{f"in_{k}": x for k, x in arrays.items()}], core_ids=[0]).results[0]
    y = got["out_y"].transpose(2, 1, 0).reshape(T, D)
    return (y[:NP].reshape(1, NP, D), y[NP:].reshape(NS, 1, D), got["out_new_pool_prompt"],
            got["out_new_ret_prompt"], got["out_new_pool_sample"], got["out_new_ret_sample"])
```

```python
from contextlib import ExitStack

import numpy as np

import concourse.bass as bass
from concourse import mybir

F32 = mybir.dt.float32
F32R = mybir.dt.float32r
I32 = mybir.dt.int32
ALU = mybir.AluOpType
ACT = mybir.ActivationFunctionType
AX_X = mybir.AxisListType.X

P = 128
D = 1024
DC = D // P
NP = 256
NS = 8
T = NP + NS
DEPTH = 2
POOL_W = 512
PC = POOL_W // P
WINDOWS = (2, 4, 8, 16)
BUF = 15
HEADS, HD = 8, 64
RC = 512 // P
FF = 2816
NE = 8
FE = 1408
PLE = 256
EPS = 1e-6
PAST = 2048
CAP = 128
CH = 128
STEPS = ((0, 512), (512, 512), (1024, 384))
PAD = 16

RAW = 4
SPL = 4
UNIT = 2048
AHEAD = 2

CONST = {}
_at = 0
for _name, _n in (("mean", P), ("eps", 1), ("ident", P), ("rot", P), ("hmean", P), ("upper", P),
                  ("cos", T), ("sin", T), ("decay", 2 * RC * CH), ("xi", RC * CH), ("zeta", HEADS),
                  ("gchunk", RC), ("gamma", RC), ("early", PC * PAD), ("wsel", PC * NS),
                  ("iota", P), ("tie", NE), ("valid", 3), ("hvar", RC * HEADS)):
    CONST[_name] = (_at, _n)
    _at += _n
NCONST = _at
FIRST_CONST = P + 1


def constants():
    f = np.float32
    c = np.zeros((P, NCONST), f)

    def put(name, v):
        a, n = CONST[name]
        c[:v.shape[0], a:a + n] = v.reshape(v.shape[0], n)

    p = np.arange(P)
    put("ident", np.eye(P, dtype=f))
    rot = np.zeros((P, P), f)
    for m in range(P):
        if m % HD < HD // 2:
            rot[m + HD // 2, m] = -1.0
        else:
            rot[m - HD // 2, m] = 1.0
    put("rot", rot)
    put("mean", np.full((P, P), 1.0 / D, f))
    put("hmean", np.where(p[:, None] // HD == p[None, :] // HD, f(1.0 / HD), f(0)))
    heads = 2 * np.arange(RC)[None, :, None] + p[:, None, None] // HD
    put("hvar", np.where(heads == np.arange(HEADS)[None, None, :], f(1.0 / HD), f(0)))
    put("upper", np.where(p[:, None] < p[None, :], f(1), f(0)))
    half = HD // 2
    inv = f(10000.0) ** (-np.arange(half, dtype=f) / f(half))
    pos = np.concatenate([np.arange(NP), np.full(NS, PAST)]).astype(f)
    ang = (pos[None, :] * inv[p % half][:, None]).astype(f)
    put("cos", np.cos(ang).astype(f))
    put("sin", np.sin(ang).astype(f))
    log_g = np.log1p(-np.power(f(2), -5 - np.arange(HEADS, dtype=f))).astype(f)
    i = np.arange(CH, dtype=f)
    rel = i[None, :] - i[:, None]
    dec = np.zeros((P, 2, RC, CH), f)
    for h in range(HEADS):
        dec[:, h % 2, h // 2] = np.where(rel >= 0, np.exp(log_g[h] * np.maximum(rel, 0)), 0)
    put("decay", dec)
    own = 2 * np.arange(RC)[None, :] + (p[:, None] // HD)
    put("xi", np.exp(log_g[own][:, :, None] * (i + 1)[None, None, :]).astype(f))
    put("zeta", np.exp(log_g[None, :] * (CH - 1 - i)[:, None]).astype(f))
    put("gchunk", np.exp(log_g[own] * CH).astype(f))
    put("gamma", np.exp(log_g[own]).astype(f))
    early = np.ones((P, PC, PAD), f)
    for g, w in enumerate(WINDOWS):
        early[:, g] = w / np.minimum(np.arange(PAD) + 1, w)
    put("early", early)
    wsel = np.zeros((NS * BUF, PC, NS), f)
    for g, w in enumerate(WINDOWS):
        for b in range(NS):
            wsel[b * BUF + BUF - (w - 1):(b + 1) * BUF, g, b] = 1
    put("wsel", wsel)
    put("iota", np.broadcast_to(np.where(p < CAP, p, -2).astype(f), (P, P)))
    valid = np.ones((P, 3), f)
    valid[NS:, 2] = 0
    put("valid", valid)
    put("tie", np.broadcast_to(NE - np.arange(NE, dtype=f), (P, NE)))
    put("eps", np.full((P, 1), EPS, f))
    return c


def sample_rows():
    z = np.zeros((64, NS, P), np.float32)
    for b in range(NS):
        z[b, b, 0:HD] = 1
        z[32 + b, b, HD:P] = 1
    return z


def head_rows():
    h = np.arange(HEADS)[:, None, None]
    return (h == 2 * np.arange(RC)[None, :, None] + np.arange(P)[None, None, :] // HD).astype(np.float32)


Z_ORDER = ((512, "q"), (1024, "k"), (1536, "v"), (0, "u"), (2048, "g"))
W_IN = [("w_in", 0, DC, at + 256 * j, 256) for at, _ in Z_ORDER for j in range(2)]
W_O = [("w_o", 0, DC, 256 * j, 256) for j in range(4)]
PLEU = [("w_ple", 0, 2, 0, D)] + [("w_ple_gate", 0, DC, 256 * j, 256) for j in range(4)]

EC = FE // P
GROUPS = (EC + 1) // 2


def part_units():
    out, chunks, full = [], 0, 0
    for i in range(GROUPS):
        w = min(2, EC - 2 * i)
        for kind in ("gate", "up"):
            out.append((kind, 2 * i, w, chunks, full))
            chunks += w
            full += w - 1
    for m in range(DC):
        out.append(("down", m, 1, chunks, full))
        chunks += 1
    return out, chunks, full


PART, PART_CHUNKS, PART_FULL = part_units()
PART_UNITS = len(PART)
STEP_UNITS, STEP_CHUNKS, STEP_FULL = 2 * PART_UNITS, 2 * PART_CHUNKS, 2 * PART_FULL
assert FF == 2 * FE
MOE_FIRST, MOE_EACH, MOE_TAIL = 16, 18, 2
FF_UNITS = (STEP_UNITS, MOE_FIRST + (NE - 1) * MOE_EACH + MOE_TAIL)

PLE_FULL = DC - 1 + 4
U_MIX, A_MIX, F_MIX = [0], [0], [0]
U_WO, U_FF, U_PLE, A_WO, A_FF, A_PLE, F_FF = [], [], [], [], [], [], []
for _l in range(DEPTH):
    U_WO.append(U_MIX[_l] + len(W_IN))
    U_FF.append(U_WO[_l] + len(W_O))
    U_PLE.append(U_FF[_l] + FF_UNITS[_l])
    U_MIX.append(U_PLE[_l] + len(PLEU))
    A_WO.append(A_MIX[_l] + 2 * len(W_IN))
    A_FF.append(A_WO[_l] + 2 * len(W_O))
    A_PLE.append(A_FF[_l] + (STEP_CHUNKS, 0)[_l])
    A_MIX.append(A_PLE[_l] + 2 * DC)
    F_FF.append(F_MIX[_l] + len(W_IN) + len(W_O))
    F_MIX.append(F_FF[_l] + (STEP_FULL, 0)[_l] + PLE_FULL)
N_UNITS = U_MIX[DEPTH]


def chunk_table():
    table, count = {}, 0

    def unit(u, chunks):
        nonlocal count
        for n in chunks[:-1]:
            count += 1
            table[n] = (False, count)
        table[chunks[-1]] = (True, u + 1)

    for l in range(DEPTH):
        for j in range(len(W_IN)):
            unit(U_MIX[l] + j, [A_MIX[l] + 2 * j, A_MIX[l] + 2 * j + 1])
        for j in range(len(W_O)):
            unit(U_WO[l] + j, [A_WO[l] + 2 * j, A_WO[l] + 2 * j + 1])
        assert count == F_FF[l]
        count += (STEP_FULL, 0)[l]
        unit(U_PLE[l], [A_PLE[l] + m for m in range(DC)])
        for j in range(4):
            unit(U_PLE[l] + 1 + j, [A_PLE[l] + 8 + 2 * j, A_PLE[l] + 9 + 2 * j])
    return table


CHUNK_FULL = chunk_table()

PARTS_AT = {0: 0, 1: 8, 2: 16, 3: 24, 5: 32}
SQUARES_AT = {0: 0, 1: 8, 3: 16, 4: 24, 6: 32}
GAIN = {0: 0, 1: 2, 3: 1}
NORM_STAGE = {(0, "norm1"): 0, (0, "norm2"): 1, (1, "norm1"): 3, (2, "norm1"): 6}
NORM_ORDER = {k: i for i, k in enumerate(NORM_STAGE)}

AFTER = [["norm1"], [], [f"rq{c}" for c in range(RC)], [], [f"rk{c}" for c in range(RC)],
         ["kt0", "kt1", "sc00", "sc01"],
         ["vt0", "vt1", "vs", "o0"], ["sc10", "sc11", "bc0", "bc1", "bc2", "bc3"],
         ["S1", "S2", "win", "tail", "o1"],
         ["qS", "wp0", "wp1", "wp2", "wp3"] + [f"mu{c}" for c in range(RC)],
         ["va"] + [f"rb{c}" for c in range(RC)]]
LAST = (["norm2"], ["tr0", "tr2", "tr4", "lg", "tr1", "lt", "tr3", "tr5", "rt", "pos", "over"])
TOKEN_ORDER = (0, 2, 4, 1, 3, 5)
SIDE = {}
_at = 0
for _l in range(DEPTH):
    for _group in AFTER + [LAST[_l]]:
        for _s in _group:
            SIDE[_l, _s] = _at
            _at += 1
SIDE[DEPTH, "norm1"] = _at
SIDE_MOE = _at



def turn_units(first):
    out = {}
    for s, (lo, n) in enumerate(STEPS):
        for half in range(2):
            out[6 * s + 2 * half] = ("moe_w_gate", 0, 4 * half, 4, lo, n, s)
            out[6 * s + 2 * half + 1] = ("moe_w_up", 0, 4 * half, 4, lo, n, s)
        ps = (s + 2) % 3
        if s or not first:
            a, n = STEPS[ps]
            out[6 * s + 4] = ("moe_w_down", int(s == 0), a // P, 2, 0, D, ps)
            out[6 * s + 5] = ("moe_w_down", int(s == 0), a // P + 2, n // P - 2, 0, D, ps)
    return out


FIRST_TURN, TURN = turn_units(True), turn_units(False)
TAIL_TURN = {4: ("moe_w_down", 0, 8, 2, 0, D, 2), 5: ("moe_w_down", 0, 10, 1, 0, D, 2)}
assert len(FIRST_TURN) == MOE_FIRST and len(TURN) == MOE_EACH and len(TAIL_TURN) == MOE_TAIL


def turn_events(kind, odd):
    if kind == "tail":
        return {3: [("t", 2)], 5: [("y", 0), ("e", 0)] + [("s", m) for m in range(DC)]}
    ev = {6: [("t", 0)], 12: [("t", 1), ("p", 0)]}
    if kind != "first":
        ev |= {0: [("t", 2)], 5: [("y", 0)], 7: [("s", 0)], 8: [("s", 1), ("s", 2)], 9: [("s", 3)],
               10: [("s", 4), ("s", 5)], 11: [("s", 6), ("s", 7)]}
    if kind == "loop" and odd:
        ev[12] += [("k", 0)]
        ev |= {14: [("g", 0), ("g", 1)], 15: [("x", 0), ("x", 1)], 16: [("x", 2), ("x", 3)]}
    return ev


TMP_STEPS = "tspxg"


def tmp_steps(kind, odd):
    return sum(ev[0] in TMP_STEPS for v in turn_events(kind, odd).values() for ev in v)


GATHERS = DC // 2
FIRST_GATHER = 2 + GATHERS
TMP_EXP1 = FIRST_GATHER + tmp_steps("first", False)
TMP_ODD, TMP_EVEN = tmp_steps("loop", True), tmp_steps("loop", False)
TMP_TAIL = TMP_EXP1 + (NE - 2) // 2 * (TMP_ODD + TMP_EVEN) + tmp_steps("last", True)
assert (TMP_ODD + TMP_EVEN) % 2 == 0
U_MOE, U_EXP1, U_TAIL = U_FF[1], U_FF[1] + MOE_FIRST, U_PLE[1] - MOE_TAIL


class Turn:

    def __init__(self, kind, pair=0, half=0):
        self.kind = kind
        self.units = {"first": FIRST_TURN, "tail": TAIL_TURN}.get(kind, TURN)
        if kind == "first":
            self.e = self.e_at = 0
            self.u = self.u_at = U_MOE
            self.k = self.k_at = FIRST_GATHER
        else:
            i = {"loop": half, "last": NE - 2, "tail": NE - 1}[kind]
            self.e_at = 1 + i
            self.u_at = U_EXP1 + MOE_EACH * i
            self.k_at = TMP_TAIL if kind == "tail" else TMP_EXP1 + i // 2 * (TMP_ODD + TMP_EVEN) + i % 2 * TMP_ODD
            self.e = pair * 2 + self.e_at
            self.u = pair * (2 * MOE_EACH) + self.u_at
            self.k = pair * (TMP_ODD + TMP_EVEN) + self.k_at
        self.pair = pair
        self.slot = self.e_at % 2
        self.events = turn_events(kind, self.slot == 1)
        self.at = {pos: n for n, pos in enumerate(sorted(self.units))}
        self.tmp = {}
        for pos in sorted(self.events):
            for ev in self.events[pos]:
                if ev[0] in TMP_STEPS:
                    self.tmp[ev] = len(self.tmp)

    def unit(self, pos):
        return self.u_at + self.at[pos], self.u + self.at[pos]

    def step(self, ev):
        return self.k_at + self.tmp[ev], self.k + self.tmp[ev]

    def gate_bank(self, s):
        return 2 * ((self.e_at + s) % 2)

    def places(self):
        return sorted(set(self.units) | set(self.events))


OVER_PE, OVER_DVE = 1 + EC + DC, 2 + EC + DC

assert 2 * MOE_EACH % RAW == 0 and 2 * MOE_EACH % SPL == 0 and NE % 2 == 0


def program(nc, t):
    with ExitStack() as ctx:
        at = [16512]

        def place(name, shape, dt=F32, offset=None):
            n = 4 * int(np.prod(shape[1:]))
            if offset is None:
                offset = at[0]
                at[0] += (n + 31) // 32 * 32
            return nc.alloc_sbuf_tensor_at(name, list(shape), dt, offset=offset)

        def sem(name):
            return ctx.enter_context(nc.semaphore(name))

        const = place("const", [P, NCONST])
        raw = [place(f"raw{i}", [P, UNIT]) for i in range(RAW)]
        whi = [place(f"whi{i}", [P, UNIT], F32R) for i in range(SPL)]
        wlo = [place(f"wlo{i}", [P, UNIT], F32R) for i in range(SPL)]
        h = place("h", [P, DC, T])
        x_at, ple_at = at[0], at[0] + 8 * DC * T
        xh = place("xh", [P, DC, T], F32R)
        xl = place("xl", [P, DC, T], F32R)
        ph = place("ph", [P, 2, T], F32R)
        pl = place("pl", [P, 2, T], F32R)
        selb = place("selb", [64, NS, P], F32, ple_at)
        gains = place("gains", [P, 5, DC])
        pscale = place("pscale", [P, DEPTH, PC])
        ssum = place("ssum", [P, T])
        sq = place("sq", [P, 2, T])
        rstd = place("rstd", [P, T])
        hrow = place("hrow", [HEADS, RC, P])
        wr = place("wr", [P, DC, NE])
        arena = at[0]
        qk = place("qk", [P, 2, RC, T])
        wsum_at = at[0]
        wsum = place("wsum", [P, PC, PAD + T])
        v = place("v", [P, RC, T], F32, wsum_at)
        sg = place("sg", [P, RC, T])
        upad = place("upad", [P, PC, PAD + T])
        sbd = place("sbd", [P, RC, P])
        o = place("o", [P, RC, T])
        S = place("S", [P, NS, RC, HD])
        kv_at = at[0]
        kv = place("kv", [P, 2, 2, RC, HD])
        rt = place("rt", [P, 2, T], F32, kv_at)
        buf = place("buf", [NS * BUF, POOL_W])
        utail = place("utail", [BUF + NS, POOL_W], F32, kv_at)
        s2 = place("s2", [P, RC, HD])
        vs2 = place("vs2", [64, RC, HD])
        qm = place("qm", [P, NS, RC, 2])
        wpool = place("wpool", [P, PC, P])
        pin = place("pin", [P, 2, T])
        mix_at = at[0]
        mh = place("mh", [P, DC, T], F32R)
        ml = place("ml", [P, DC, T], F32R)
        assert at[0] <= 229344, at[0]
        kz = place("kz", [P, 2, 512], F32, mix_at)
        vpad = place("vpad", [P, 2, RC, 3, HD], F32, mix_at + 4096)
        sc = place("sc", [P, 2, RC, CH], F32, mix_at + 4096 + 6144)
        qxi = place("qxi", [P, RC, CH], F32, mix_at + 4096 + 6144 + 4096)
        oc = place("oc", [P, RC, T], F32, x_at)
        osq = place("osq", [P, RC, T], F32, x_at + 4 * RC * T)
        og = place("og", [P, RC, T], F32, x_at + 8 * RC * T)
        rvar = place("rvar", [HEADS, T], F32, x_at + 12 * RC * T)
        fh = place("fh", [P, EC, T], F32R, arena)
        fl = place("fl", [P, EC, T], F32R, arena + 4 * EC * T)
        tg = place("tg", [P, 2, T], F32, mix_at)
        hv = place("hv", [P, 2, T], F32, mix_at + 8 * T)
        esb = (place("esb0", [P, DC, T], F32, arena), place("esb1", [P, DC, T], F32, x_at + 4 * DC * T))
        sgp = place("sgp", [P, 2, T], F32, arena + 4 * DC * T)
        cur = [arena]

        def moe(name, shape, dt=F32):
            x = place(name, shape, dt, cur[0])
            cur[0] += (4 * int(np.prod(shape[1:])) + 31) // 32 * 32
            return x

        xth = moe("xth", [P, 3, D], F32R)
        xtl = moe("xtl", [P, 3, D], F32R)
        sgate = moe("sgate", [P, 512])
        hid = moe("hid", [P, 512])
        hh = moe("hh", [P, 4, P], F32R)
        hl = moe("hl", [P, 4, P], F32R)
        pick = moe("pick", [P, 3, 2, P], F32R)
        pickT = moe("pickT", [P, T], F32R)
        identr = moe("identr", [P, P], F32R)
        yh = moe("yh", [P, D], F32R)
        yl = moe("yl", [P, D], F32R)
        r = {n: moe("r_" + n, [P, 3, NE]) for n in
             ("lg", "eq", "key", "one", "two", "lg2", "gate", "t2", "sel", "pos", "over")}
        m1, m2, kx, dm, w1, w2 = (moe(n, [P, 3]) for n in ("m1", "m2", "kx", "dm", "w1", "w2"))
        rs = moe("rs", [P, 3])
        rslot = moe("rslot", [P, 2])
        rnext = moe("rnext", [P, 2])
        lgs = moe("lgs", [NE, T])
        pose = moe("pose", [P, 3, 2])
        gslot = moe("gslot", [P, 1])
        over1 = moe("over1", [P, 1])
        flag = moe("flag", [1, 1], I32)
        assert cur[0] <= mix_at
        xel = moe("xel", [P, DC, 2, P], F32R)
        assert cur[0] <= mix_at + 8 * DC * T, (cur[0], mix_at)
        owt = place("owt", [P, 2, EC * P], F32, arena)
        ohid = place("ohid", [P, EC, T], F32, arena + 8 * EC * P)
        assert 8 * EC * P + 4 * EC * T <= 8 * 3 * D
        osg = place("osg", [P, T], F32, arena + 8 * 3 * D)
        orow = place("orow", [P, T], F32, arena + 8 * 3 * D + 4 * 512)
        ocol = place("ocol", [P, 3], F32, arena + 8 * 3 * D + 8 * 512)
        hg = place("hg", [P, DC, T], F32, x_at)
        xeh = place("xeh", [P, DC, 2, P], F32R, x_at + 4 * DC * T)
        BLK = ((0, P), (1, P), (2, NS))

        bank = [ctx.enter_context(nc.psum_tensor(f"bank{i}", [P, 512], F32)) for i in range(8)]

        raw_landed = [sem(f"raw_landed{i}") for i in range(RAW)]
        hi_ready, lo_ready, unit_used = sem("hi_ready"), sem("lo_ready"), sem("unit_used")
        x_in, first_in, const_in, layer_in = sem("x_in"), sem("first_in"), sem("const_in"), sem("layer_in")
        pool_kept, state_out, y_out = sem("pool_kept"), sem("state_out"), sem("y_out")
        acc_full, acc_free = sem("acc_full"), sem("acc_free")
        side_full, side_free = sem("side_full"), sem("side_free")
        part_hi, part_lo, sq_ready, ss_added = sem("part_hi"), sem("part_lo"), sem("sq_ready"), sem("ss_added")
        std_ready = sem("std_ready")
        zeroed, cosed, roped, silu_g = sem("zeroed"), sem("cosed"), sem("roped"), sem("silu_g")
        s_decayed, s_ready, qm_ready = sem("s_decayed"), sem("s_ready"), sem("qm_ready")
        qxi_ready, wsummed, d_ready = sem("qxi_ready"), sem("wsummed"), sem("d_ready")
        osq_ready, og_ready, stdv_ready = sem("osq_ready"), sem("og_ready"), sem("stdv_ready")
        mix_hi, mix_lo = sem("mix_hi"), sem("mix_lo")
        silu_f, scaled_f, f_hi, f_lo = sem("silu_f"), sem("scaled_f"), sem("f_hi"), sem("f_lo")
        ple_hi, ple_lo, gate_ready, ge_ready = sem("ple_hi"), sem("ple_lo"), sem("gate_ready"), sem("ge_ready")
        identr_ready, moe_zeroed, hg_ready = sem("identr_ready"), sem("moe_zeroed"), sem("hg_ready")
        dm_ready, sig_ready, routed, rowstd = sem("dm_ready"), sem("sig_ready"), sem("routed"), sem("rowstd")
        xt_hi, y_ready = sem("xt_hi"), sem("y_ready")
        tmp_full, tmp_free = sem("tmp_full"), sem("tmp_free")
        sgate_ready, hid_ready, hh_ready = sem("sgate_ready"), sem("hid_ready"), sem("hh_ready")
        pose_ready, pick_ready, xe_hi = sem("pose_ready"), sem("pick_ready"), sem("xe_hi")
        y_hi, y_lo, over_ready = sem("y_hi"), sem("y_lo"), sem("over_ready")
        o_landed = [sem("o_landed0"), sem("o_landed1")]
        o_mean, o_std, o_norm = sem("o_mean"), sem("o_std"), sem("o_norm")
        o_used, o_silu, o_done, o_scaled = sem("o_used"), sem("o_silu"), sem("o_done"), sem("o_scaled")
        dve_step, pool_step = sem("dve_step"), sem("pool_step")

        def C(name, rows=P):
            a, n = CONST[name]
            return const[0:rows, a:a + n]

        ident, rot, mean = C("ident"), C("rot"), C("mean")
        decay = C("decay").rearrange("p (a c n) -> p a c n", a=2, c=RC)
        xi = C("xi").rearrange("p (c n) -> p c n", c=RC)
        wsel = C("wsel", NS * BUF).rearrange("p (g b) -> p g b", g=PC)
        def side_bank(l, name):
            return 4 + (0 if name == "over" else SIDE[l, name] % 4)

        def chunk_full(eng, n):
            by_unit, count = CHUNK_FULL[n]
            eng.wait_ge(unit_used if by_unit else acc_full, count)

        def h_final(eng, stage, m):
            if stage == 0:
                eng.wait_ge(x_in, 48)
            else:
                if stage == 5:
                    eng.wait_ge(tmp_free, TMP_TAIL + 2 + m)
                    return
                first = {1: A_WO[0], 2: A_PLE[0] - DC, 3: A_PLE[0] + DC, 4: A_WO[1],
                         6: A_PLE[1] + DC}[stage]
                eng.wait_ge(acc_free, first + m + 1)

        part_cols = [(DC if kind != "down" else EC) * w * P for kind, _, w, _, _ in PART]
        cols = {}
        for l in range(DEPTH):
            for first, specs in ((U_MIX[l], W_IN), (U_WO[l], W_O), (U_PLE[l], PLEU)):
                cols |= {first + j: x[2] * x[4] for j, x in enumerate(specs)}
        cols |= {U_FF[l] + j: UNIT for l in range(DEPTH) for j in range(AHEAD)}
        assert all(cols[U_PLE[l] + j] == UNIT for l in range(DEPTH) for j in range(AHEAD))

        def turn_cols(turn, i):
            n = len(turn.units)
            if i >= n:
                if turn.kind != "last":
                    return UNIT
                x = TAIL_TURN[sorted(TAIL_TURN)[i - n]]
            else:
                x = turn.units[sorted(turn.units)[i]]
            return x[3] * x[5]

        class Count:

            def __init__(self, half):
                self.unit = U_FF[0] + half * PART_UNITS
                self.chunk = A_FF[0] + half * PART_CHUNKS
                self.full = F_FF[0] + half * PART_FULL
                self.hidden = half * EC

        block = ctx.enter_context(nc.Block())

        @block.sync
        def _(sp):
            def load(slot, vector_through, src, n, w):
                if vector_through is not None:
                    sp.wait_ge(lo_ready, vector_through)
                dst = raw[slot][:, 0:n * w].rearrange("p (k w) -> p k w", k=n)
                sp.dma_start(dst, src.rearrange("(k p) w -> p k w", p=P)).then_inc(raw_landed[slot], 16)

            def dense(layer, first, specs):
                for j, (name, k0, n, c0, w) in enumerate(specs):
                    u = first + j
                    m = t[name][layer]
                    load(u % RAW, u - RAW + 1 if u >= RAW else None, m[k0 * P:(k0 + n) * P, c0:c0 + w], n, w)

            def feed_forward():
                for half in range(2):
                    n = Count(half)
                    own = slice(half * FE, (half + 1) * FE)
                    gate, up, down = t["ffn_w_gate"][0][:, own], t["ffn_w_up"][0][:, own], t["ffn_w_down"][0][own, :]
                    for i, (kind, c, w, _, _) in enumerate(PART):
                        src = {"gate": gate, "up": up, "down": down}[kind]
                        load((n.unit + i) % RAW, n.unit + (i - RAW + 1), src[:, c * P:(c + w) * P],
                             EC if kind == "down" else DC, w * P)

            def experts(turn):
                for pos in sorted(turn.units):
                    name, back, k0, n, c0, w, _ = turn.units[pos]
                    off, u = turn.unit(pos)
                    e = turn.e - (back + (turn.kind == "tail"))
                    m = t[name][0][e] if isinstance(e, int) else t[name][0][bass.ds(e, 1)].rearrange("a k w -> (a k) w")
                    load(off % RAW, u - (RAW - 1), m[k0 * P:(k0 + n) * P, c0:c0 + w], n, w)

            dense(0, U_MIX[0], W_IN[:1])
            sp.dma_start(gains[:, :, :], t["gains"]).then_inc(x_in, 16)
            sp.dma_start(h[:, 0:4, :], t["x"][:, 0:4, :]).then_inc(x_in, 16)
            sp.dma_start(h[:, 4:8, :], t["x"][:, 4:8, :]).then_inc(x_in, 16)
            sp.dma_start(const[:, 0:FIRST_CONST], t["const"][:, 0:FIRST_CONST]).then_inc(first_in, 16)
            dense(0, U_MIX[0] + 1, W_IN[1:2])
            sp.dma_start(const[:, FIRST_CONST:], t["const"][:, FIRST_CONST:]).then_inc(const_in, 16)
            sp.dma_start(pscale[:, :, :], t["pscale"]).then_inc(const_in, 16)
            sp.dma_start(wr[:, :, :], t["moe_router"][0].rearrange("(c p) e -> p c e", p=P)).then_inc(const_in, 16)
            sp.dma_start(hrow[:, :, :], t["hrow"]).then_inc(const_in, 16)
            dense(0, U_MIX[0] + 2, W_IN[2:])
            dense(0, U_WO[0], W_O)
            feed_forward()
            dense(0, U_PLE[0], PLEU)
            dense(1, U_MIX[1], W_IN)
            dense(1, U_WO[1], W_O)
            experts(Turn("first"))
            with sp.Fori(0, (NE - 2) // 2) as pair:
                for half in range(2):
                    experts(Turn("loop", pair, half))
            experts(Turn("last"))
            experts(Turn("tail"))
            dense(1, U_PLE[1], PLEU[:AHEAD])
            sp.wait_ge(side_free, SIDE_MOE)
            with sp.If(sp.value_load(flag[0:1, 0:1], min_val=0, max_val=2 * T) > 0):
                with sp.Fori(0, NE) as e:
                    gate, up, down = (t[name][0][bass.ds(e, 1)].rearrange("a k w -> (a k) w")
                                      for name in ("moe_w_gate", "moe_w_up", "moe_w_down"))
                    for i in range(EC + DC):
                        for a, src in enumerate((gate, up) if i < EC else (down,)):
                            n = DC if i < EC else EC
                            c = i if i < EC else i - EC
                            sp.wait_ge(o_used, e * OVER_PE + (i + 1))
                            dst = owt[:, a, 0:n * P].rearrange("p (k w) -> p k w", k=n)
                            sp.dma_start(dst, src[:, c * P:(c + 1) * P].rearrange("(k p) w -> p k w", p=P)).then_inc(o_landed[a], 16)
            dense(1, U_PLE[1] + AHEAD, PLEU[AHEAD:])
            for j in range(4):
                sp.wait_ge(y_ready, 2 * j + 2)
                sp.dma_start(t["y"][:, 2 * j:2 * j + 2, :], h[:, 2 * j:2 * j + 2, :]).then_inc(y_out, 16)
            sp.wait_ge(y_out, 64)

        @block.tensor
        def _(pe):
            def weights_first(out, w_hi, w_lo, x_hi, x_lo, start, stop):
                pe.matmul(out, w_hi, x_hi, start=start, stop=False)
                pe.matmul(out, w_hi, x_lo, start=False, stop=False)
                return pe.matmul(out, w_lo, x_hi, start=False, stop=stop)

            def chunk(at, n, u, k, w, m, xhi, xlo, row_ready=None):
                if at >= 4:
                    pe.wait_ge(acc_free, n - 3)
                out = bank[at % 4][:, 0:T]
                H = whi[u % SPL][:, 0:k * w].rearrange("p (k w) -> p k w", k=k)
                L = wlo[u % SPL][:, 0:k * w].rearrange("p (k w) -> p k w", k=k)
                for kc in range(k):
                    if row_ready is not None:
                        ready, before = row_ready
                        pe.wait_ge(ready, before + (kc + 1))
                    mm = weights_first(out, H[:, kc, m * P:(m + 1) * P], L[:, kc, m * P:(m + 1) * P],
                                       xhi[:, kc, :], xlo[:, kc, :], kc == 0, kc == k - 1)
                return mm

            def unit_pair(u, n, xhi, xlo, row_ready=None):
                pe.wait_ge(lo_ready, u + 1)
                chunk(n, n, u, DC, 256, 0, xhi, xlo, row_ready).then_inc(acc_full, 1)
                chunk(n + 1, n + 1, u, DC, 256, 1, xhi, xlo).then_inc(unit_used, 1)

            def feed_forward():
                for half in range(2):
                    n = Count(half)
                    for i, (kind, _, w, a, _) in enumerate(PART):
                        pe.wait_ge(lo_ready, n.unit + (i + 1))
                        row_ready = (f_lo, n.hidden) if i == 2 * GROUPS else (part_lo, PARTS_AT[1]) if i + half == 0 else None
                        for m in range(w):
                            down = kind == "down"
                            mm = chunk(n.chunk + a + m, n.chunk + (a + m), n.unit + i, EC if down else DC, w * P, m,
                                       fh if down else xh, fl if down else xl,
                                       row_ready if m == 0 else None)
                            mm.then_inc(acc_full if m < w - 1 else unit_used, 1)
                        if i + half == 0:
                            side_step(0, "norm2")

            def ple_chunks(l):
                u = U_PLE[l]
                pe.wait_ge(lo_ready, u + 1)
                pe.wait_ge(ple_lo, l + 1)
                for m in range(DC):
                    chunk(A_PLE[l] + m, A_PLE[l] + m, u, 2, D, m, ph, pl).then_inc(acc_full if m < DC - 1 else unit_used, 1)

            def logits(chunks):
                i = SIDE[1, "lg"]
                pe.wait_ge(side_free, i - 3)
                for c in chunks:
                    pe.wait_ge(hg_ready, c + 1)
                    mm = pe.matmul(bank[4 + i % 4][0:NE, 0:T], wr[:, c, :], hg[:, c, :], start=(c == 0), stop=(c == DC - 1))
                return mm

            def side_step(l, name):
                i = SIDE[l, name]
                if i >= 4:
                    pe.wait_ge(side_free, i - 3)
                b = bank[side_bank(l, name)]
                if name in ("norm1", "norm2"):
                    pe.wait_ge(first_in, 16)
                    pe.wait_ge(ss_added, SQUARES_AT[NORM_STAGE[l, name]] + DC)
                    mm = pe.matmul(b[:, 0:T], mean, ssum[:, :], start=True, stop=True)
                elif name[:2] in ("rq", "rk"):
                    a, c = int(name[1] == "k"), int(name[2])
                    pe.wait_ge(const_in, 64)
                    pe.wait_ge(acc_free, A_MIX[l] + 4 * a + c + 1)
                    mm = pe.matmul(b[:, 0:T], rot, qk[:, a, c, :], start=True, stop=True)
                elif name[:2] in ("kt", "vt"):
                    blk = int(name[2])
                    if name[0] == "k":
                        pe.wait_ge(roped, 8 * (l + 1))
                    else:
                        pe.wait_ge(acc_free, A_MIX[l] + 12)
                    for c in range(RC):
                        src = qk[:, 1, c, :] if name[0] == "k" else v[:, c, :]
                        mm = pe.transpose(b[:, c * P:(c + 1) * P], src[:, blk * CH:(blk + 1) * CH], ident)
                elif name == "vs":
                    for c in range(RC):
                        mm = pe.transpose(b[0:NS, c * P:(c + 1) * P], v[:, c, NP:T], ident)
                elif name[:2] == "sc":
                    blk, hp = int(name[2]) * CH, int(name[3])
                    rows = slice(hp * HD, (hp + 1) * HD)
                    for c in range(RC):
                        mm = pe.matmul(b[:, c * CH:(c + 1) * CH], qk[rows, 1, c, blk:blk + CH],
                                       qk[rows, 0, c, blk:blk + CH], start=True, stop=True)
                elif name == "win":
                    pe.wait_ge(layer_in, 80 * (l + 1))
                    for g in range(PC):
                        mm = pe.matmul(b[:, g * NS:(g + 1) * NS], buf[:, g * P:(g + 1) * P], wsel[:, g, :],
                                       start=True, stop=True)
                elif name in ("S1", "S2"):
                    blk = int(name == "S2")
                    pe.wait_ge(side_free, SIDE[l, "vt1"] + 1)
                    for c in range(RC):
                        mm = pe.matmul(b[:, c * P:(c + 1) * P], kz[:, blk, c * P:(c + 1) * P],
                                       vpad[:, blk, c, 0:3:2, :], start=True, stop=True)
                elif name in ("o0", "o1"):
                    blk = int(name[1])
                    pe.wait_ge(side_free, max(SIDE[l, f"sc{blk}1"], SIDE[l, f"vt{blk}"]) + 1)
                    pe.wait_ge(zeroed, 5 * (l + 1))
                    if blk:
                        pe.wait_ge(side_free, SIDE[l, "S1"] + 1)
                        pe.wait_ge(qxi_ready, l + 1)
                    for c in range(RC):
                        out = b[:, c * CH:(c + 1) * CH]
                        vc = vpad[:, blk, c, :, :].rearrange("p a e -> p (a e)")
                        pe.matmul(out, vc[:, 0:P], sc[:, 0, c, :], start=True, stop=False)
                        mm = pe.matmul(out, vc[:, HD:HD + P], sc[:, 1, c, :], start=False, stop=not blk)
                        if blk:
                            mm = pe.matmul(out, sbd[:, c, :], qxi[:, c, :], start=False, stop=True)
                elif name[:2] == "bc":
                    pe.wait_ge(side_free, SIDE[l, "vs"] + 1)
                    pe.wait_ge(layer_in, 80 * (l + 1))
                    for a in range(2):
                        mm = pe.matmul(b[:, a * 256:(a + 1) * 256], selb[:, 2 * int(name[2]) + a, :],
                                       vs2[:, :, :].rearrange("p c e -> p (c e)"), start=True, stop=True)
                elif name == "qS":
                    pe.wait_ge(s_ready, 4 * (l + 1))
                    pe.wait_ge(qm_ready, 2 * (l + 1))
                    for s in range(NS):
                        for c in range(RC):
                            a = 2 * (s * RC + c)
                            mm = pe.matmul(b[0:HD, a:a + 2], S[:, s, c, :], qm[:, s, c, :], start=True, stop=True)
                elif name == "tail":
                    pe.wait_ge(acc_free, A_MIX[l] + 16)
                    for g in range(PC):
                        mm = pe.transpose(b[0:BUF + NS, g * P:(g + 1) * P], upad[:, g, PAD + NP - BUF:PAD + T], ident)
                elif name[:2] == "wp":
                    g = int(name[2])
                    pe.wait_ge(d_ready, PC * l + g + 1)
                    mm = pe.matmul(b[:, 0:T], wpool[:, g, :], wsum[:, g, PAD:PAD + T], start=True, stop=True)
                elif name[:2] == "mu":
                    pe.wait_ge(side_free, SIDE[l, "qS"] + 1)
                    mm = pe.matmul(b[:, 0:T], C("hmean"), o[:, int(name[2]), :], start=True, stop=True)
                elif name == "va":
                    hvar = C("hvar").rearrange("p (c e) -> p c e", c=RC)
                    for c in range(RC):
                        pe.wait_ge(osq_ready, RC * l + c + 1)
                        mm = pe.matmul(b[0:HEADS, 0:T], hvar[:, c, :], osq[:, c, :], start=(c == 0), stop=(c == RC - 1))
                elif name[:2] == "rb":
                    pe.wait_ge(side_free, SIDE[l, "va"] + 1)
                    mm = pe.matmul(b[:, 0:T], hrow[:, int(name[2]), :], rvar[:, :], start=True, stop=True)
                elif name == "lg":
                    mm = logits(range(4, DC))
                elif name == "lt":
                    pe.wait_ge(side_free, SIDE[1, "lg"] + 1)
                    for j, w in BLK:
                        mm = pe.transpose(b[0:w, j * NE:(j + 1) * NE], lgs[:, j * P:j * P + w], ident[0:NE, 0:NE])
                elif name == "rt":
                    pe.wait_ge(ss_added, SQUARES_AT[4] + DC)
                    for j, w in BLK:
                        mm = pe.matmul(b[0:w, j:j + 1], ssum[:, j * P:j * P + w], mean[:, 0:1], start=True, stop=True)
                elif name[:2] == "tr":
                    j, half = divmod(int(name[2]), 2)
                    w = BLK[j][1]
                    pe.wait_ge(hg_ready, 4 * (half + 1))
                    for c in range(4):
                        mm = pe.transpose(b[0:w, c * P:(c + 1) * P], hg[:, 4 * half + c, j * P:j * P + w], ident)
                elif name == "pos":
                    pe.wait_ge(routed, 1)
                    ones = C("valid")[:, 0:1].to_broadcast([P, P])
                    for j in range(3):
                        for i2 in range(j + 1):
                            mm = pe.matmul(b[:, j * NE:(j + 1) * NE], C("upper") if i2 == j else ones,
                                           r["sel"][:, i2, :], start=(i2 == 0), stop=(i2 == j))
                elif name == "over":
                    pe.wait_ge(over_ready, 1)
                    mm = pe.matmul(b[0:1, 0:1], over1[:, :], C("valid")[:, 0:1], start=True, stop=True)
                mm.then_inc(side_full, 1)

            def tmp_bank(off, k):
                if off >= 2:
                    pe.wait_ge(tmp_free, k - 1)
                return bank[6 + off % 2]

            def gather_rstd(a, off, k, count):
                b = tmp_bank(off, k)
                pe.wait_ge(pick_ready, count)
                for j, w in BLK:
                    mm = pe.matmul(b[:, 0:1], pick[0:w, j, a, :].bitcast(F32), rs[0:w, j:j + 1], start=(j == 0), stop=(j == 2))
                mm.then_inc(tmp_full, 1)

            def gather(i, off, k):
                b = tmp_bank(off, k)
                for c in range(2):
                    f = (2 * i + c) * P
                    for j, w in BLK:
                        out, sel = b[:, 2 * c * P:2 * (c + 1) * P], pick[0:w, j, :, :].rearrange("p a n -> p (a n)")
                        pe.matmul(out, xth[0:w, j, f:f + P], sel, start=(j == 0), stop=False)
                        mm = pe.matmul(out, xtl[0:w, j, f:f + P], sel, start=False, stop=(j == 2))
                mm.then_inc(tmp_full, 1)

            def run_turn(turn):
                e = turn.e
                for pos in turn.places():
                    if pos in turn.units:
                        name, back, k0, n, c0, w, s = turn.units[pos]
                        off, u = turn.unit(pos)
                        pe.wait_ge(lo_ready, u + 1)
                        H = whi[off % SPL][:, 0:n * w].rearrange("p (k w) -> p k w", k=n)
                        L = wlo[off % SPL][:, 0:n * w].rearrange("p (k w) -> p k w", k=n)
                    if pos in turn.units and name != "moe_w_down":
                        if pos == 0:
                            pe.wait_ge(tmp_free, turn.k)
                        if pos % 6 == 0 and not (turn.kind == "first" and s < 2):
                            pe.wait_ge(hid_ready, e * 3 + (s - 1))
                        b = bank[turn.gate_bank(s) + pos % 2][:, 0:w]
                        for kc in range(n):
                            X, Y = xeh[:, k0 + kc, turn.slot, :], xel[:, k0 + kc, turn.slot, :]
                            pe.matmul(b, X, H[:, kc, :], start=(k0 + kc == 0), stop=False)
                            pe.matmul(b, X, L[:, kc, :], start=False, stop=False)
                            mm = pe.matmul(b, Y, H[:, kc, :], start=False, stop=(k0 + kc == DC - 1))
                        mm.then_inc(unit_used, 1)
                    elif pos in turn.units:
                        if pos % 6 == 4:
                            pe.wait_ge(tmp_free, turn.step(("t", s))[1] + 1)
                            if s == 0 and turn.kind == "first":
                                pe.wait_ge(side_free, SIDE_MOE)
                            if s == 0 and turn.kind != "first":
                                pe.wait_ge(y_lo, e * 2)
                        for i2 in range(n):
                            f = k0 + i2
                            X, Y = hh[:, f - 4 * s, :], hl[:, f - 4 * s, :]
                            for half in range(2):
                                b = bank[4 + half][:, :]
                                lo_, hi_ = half * 512, (half + 1) * 512
                                pe.matmul(b, X, H[:, i2, lo_:hi_], start=(f == 0), stop=False)
                                pe.matmul(b, X, L[:, i2, lo_:hi_], start=False, stop=False)
                                mm = pe.matmul(b, Y, H[:, i2, lo_:hi_], start=False, stop=(f == FE // P - 1))
                        mm.then_inc(unit_used, 1)
                    if turn.kind == "first" and pos == 3:
                        side_step(1, "over")
                        pe.wait_ge(routed, 2)
                    for ev in turn.events.get(pos, []):
                        kind, i2 = ev
                        if kind == "t":
                            off, k = turn.step(ev)
                            b = tmp_bank(off, k)
                            pe.wait_ge(hid_ready, e * 3 + (i2 + 1 - 3 * (i2 == 2)))
                            for c in range(STEPS[i2][1] // P):
                                mm = pe.transpose(b[:, c * P:(c + 1) * P], hid[:, c * P:(c + 1) * P], ident)
                            mm.then_inc(tmp_full, 1)
                        elif kind == "s":
                            off, k = turn.step(ev)
                            b = tmp_bank(off, k)
                            if i2 == 0:
                                pe.wait_ge(y_lo, e * 2)
                            pe.matmul(b[:, 0:T], yh[:, i2 * P:(i2 + 1) * P], pickT[:, :], start=True, stop=False)
                            pe.matmul(b[:, 0:T], yl[:, i2 * P:(i2 + 1) * P], pickT[:, :], start=False,
                                      stop=True).then_inc(tmp_full, 1)
                        elif kind == "p":
                            off, k = turn.step(ev)
                            b = tmp_bank(off, k)
                            for j, w in BLK:
                                pe.transpose(b[:, j * P:j * P + w].bitcast(F32R), pick[0:w, j, turn.slot, :], identr[0:w, 0:w])
                            for j, w in BLK:
                                mm = pe.matmul(b[:, 272:272 + NE], pick[0:w, j, turn.slot, :].bitcast(F32), r["gate"][0:w, j, :],
                                               start=(j == 0), stop=(j == 2))
                            mm.then_inc(tmp_full, 1)
                        elif kind == "x":
                            off, k = turn.step(ev)
                            gather(i2, off, k)
                        elif kind == "e":
                            pe.wait_ge(hid_ready, 3 * NE)
                            ple_chunks(1)
                        elif kind == "g":
                            off, k = turn.step(ev)
                            gather_rstd(i2, off, k, turn.pair + 2)

            def over_expert(e):
                pe.wait_ge(o_done, e * OVER_DVE + 1)
                for j, w in BLK:
                    mm = pe.matmul(bank[2][:, j * P:j * P + w], ocol[0:w, j:j + 1].to_broadcast([w, P]),
                                   ident[0:w, 0:w], start=True, stop=True)
                mm.then_inc(o_used, 1)
                for i in range(EC + DC):
                    pe.wait_ge(o_landed[0], e * (16 * (EC + DC)) + 16 * (i + 1))
                    pe.wait_ge(o_done, e * OVER_DVE + (i + 2))
                    if i < EC:
                        pe.wait_ge(o_landed[1], e * (16 * EC) + 16 * (i + 1))
                        for a in range(2):
                            for k in range(DC):
                                mm = pe.matmul(bank[a][:, 0:T], owt[:, a, k * P:(k + 1) * P], hg[:, k, :],
                                               start=(k == 0), stop=(k == DC - 1))
                    else:
                        for k in range(EC):
                            mm = pe.matmul(bank[0][:, 0:T], owt[:, 0, k * P:(k + 1) * P], ohid[:, k, :],
                                           start=(k == 0), stop=(k == EC - 1))
                    mm.then_inc(o_used, 1)

            for l in range(DEPTH):
                for j in range(10):
                    unit_pair(U_MIX[l] + j, A_MIX[l] + 2 * j, xh, xl, (part_lo, PARTS_AT[3 * l]) if j == 0 else None)
                    for name in AFTER[j]:
                        side_step(l, name)
                side_step(l, "va")
                pe.wait_ge(side_free, SIDE[l, "wp3"] + 1)
                for first_row in (0, PC):
                    if first_row:
                        for c in range(RC):
                            side_step(l, f"rb{c}")
                    for m in range(4):
                        u, n = U_WO[l] + m // 2, A_WO[l] + m
                        H = whi[u % SPL][:, :].rearrange("p (k w) -> p k w", k=DC)
                        L = wlo[u % SPL][:, :].rearrange("p (k w) -> p k w", k=DC)
                        own = slice(m % 2 * P, (m % 2 + 1) * P)
                        pe.wait_ge(lo_ready, u + 1)
                        if first_row == 0:
                            pe.wait_ge(acc_free, n - 3)
                        for k in range(first_row, first_row + PC):
                            if k >= PC and m == 0:
                                pe.wait_ge(mix_lo, RC * l + k - PC + 1)
                            mm = weights_first(bank[n % 4][:, 0:T], H[:, k, own], L[:, k, own], mh[:, k, :], ml[:, k, :],
                                               k == 0, k == DC - 1)
                        if first_row:
                            mm.then_inc(acc_full if m % 2 == 0 else unit_used, 1)
                for j in range(2, 4):
                    unit_pair(U_WO[l] + j, A_WO[l] + 2 * j, mh, ml)
                    if l and j == 2:
                        logits(range(4))
                        for name in ("tr0", "tr2", "tr4"):
                            side_step(1, name)
                if l:
                    for name in LAST[1][3:-1]:
                        side_step(1, name)
                if l == 0:
                    feed_forward()
                else:
                    pe.wait_ge(acc_free, A_FF[1])
                    pe.wait_ge(side_free, SIDE[1, "pos"] + 1)
                    pe.wait_ge(identr_ready, 1)
                    for a in range(2):
                        gather_rstd(a, a, a, 1)
                    for i in range(GATHERS):
                        gather(i, i + 2, i + 2)
                    run_turn(Turn("first"))
                    with pe.Fori(0, (NE - 2) // 2) as pair:
                        for half in range(2):
                            run_turn(Turn("loop", pair, half))
                    run_turn(Turn("last"))
                    run_turn(Turn("tail"))
                    pe.wait_ge(hid_ready, 3 * NE)
                    pe.wait_ge(tmp_free, TMP_TAIL + 1 + DC)
                    with pe.If(pe.value_load(flag[0:1, 0:1], min_val=0, max_val=2 * T) > 0):
                        pe.matmul(bank[3][:, 0:T], mean, ssum[:, :], start=True, stop=True).then_inc(o_mean, 1)
                        pe.wait_ge(o_norm, 1 + DC)
                        with pe.Fori(0, NE) as e:
                            over_expert(e)
                        pe.wait_ge(o_done, NE * OVER_DVE)
                if l == 0:
                    ple_chunks(0)
                for j in range(4):
                    unit_pair(U_PLE[l] + 1 + j, A_PLE[l] + 8 + 2 * j, mh, ml, (part_lo, PARTS_AT[5 if l else 2]) if j == 0 else None)
            side_step(DEPTH, "norm1")

        @block.scalar
        def _(act):
            def hi(off, n, pair=0):
                act.wait_ge(raw_landed[off % RAW], pair * (16 * 2 * MOE_EACH // RAW) + 16 * (off // RAW + 1))
                if off >= SPL:
                    act.wait_ge(unit_used, pair * (2 * MOE_EACH) + (off - (SPL - 1)))
                act.activation(whi[off % SPL][:, 0:n], raw[off % RAW][:, 0:n], ACT.Copy).then_inc(hi_ready, 1)

            def ahead(u):
                if u + AHEAD < N_UNITS:
                    hi(u + AHEAD, cols[u + AHEAD])

            def part(stage, m):
                dst = xh if stage in GAIN else mh
                scale = gains[:, GAIN[stage], m:m + 1] if stage in GAIN else 1.0
                act.activation(dst[:, m, :], h[:, m, :], ACT.Copy, scale=scale).then_inc(part_hi, 1)

            def square(stage, m):
                n = SQUARES_AT[stage] + m
                if n >= 2:
                    act.wait_ge(ss_added, n - 1)
                act.activation(sq[:, n % 2, :], h[:, m, :], ACT.Square).then_inc(sq_ready, 1)

            def finish_pair(stage, first):
                for m in (first, first + 1):
                    h_final(act, stage, m)
                    if stage in PARTS_AT:
                        part(stage, m)
                for m in (first, first + 1):
                    square(stage, m)

            def token_hi(i):
                j, half = divmod(i, 2)
                w = BLK[j][1]
                act.wait_ge(side_full, SIDE[1, f"tr{i}"] + 1)
                act.activation(xth[0:w, j, half * 512:(half + 1) * 512], bank[side_bank(1, f"tr{i}")][0:w, :],
                               ACT.Copy).then_inc(xt_hi, 1)

            def norm(l, name):
                act.wait_ge(first_in, 16)
                act.wait_ge(side_full, SIDE[l, name] + 1)
                i = SIDE[l, name] % 4
                act.activation(rstd[:, :], bank[4 + i][:, 0:T], ACT.Sqrt, bias=C("eps")).then_inc(std_ready, 1)

            def feed_forward():
                for half in range(2):
                    n = Count(half)
                    for i, (kind, c, w, a, _) in enumerate(PART):
                        hi(n.unit + i + AHEAD, part_cols[(i + AHEAD) % PART_UNITS])
                        if i + half == 0:
                            norm(0, "norm2")
                        for m in range(w):
                            if kind == "gate":
                                act.wait_ge(acc_free, n.chunk + (a + m + 1))
                                act.activation(tg[:, m, :], tg[:, m, :], ACT.Silu).then_inc(silu_f, 1)
                            elif kind == "up":
                                act.wait_ge(acc_free, n.chunk + (a + m + 1))
                                act.activation(fh[:, c + m, :], hv[:, m, :], ACT.Copy).then_inc(f_hi, 1)

            def wait_step(turn, ev):
                off, k = turn.step(ev)
                act.wait_ge(tmp_full, k + 1)
                return bank[6 + off % 2]

            def run_turn(turn):
                e = turn.e
                for pos in turn.places():
                    if pos in turn.units:
                        i = turn.at[pos]
                        hi(turn.u_at + i + AHEAD, turn_cols(turn, i + AHEAD), turn.pair)
                    if pos % 6 == 3 and pos in turn.units:
                        s = pos // 6
                        off, u = turn.unit(pos)
                        act.wait_ge(unit_used, u + 1)
                        n = STEPS[s][1]
                        b = bank[turn.gate_bank(s)]
                        act.activation(sgate[:, 0:n], b[:, 0:n], ACT.Silu, scale=rslot[:, turn.slot:turn.slot + 1]).then_inc(sgate_ready, 1)
                    for ev in turn.events.get(pos, []):
                        kind, i = ev
                        if kind == "t":
                            b = wait_step(turn, ev)
                            n = STEPS[i][1]
                            act.activation(hh[:, 0:n // P, :].rearrange("p c s -> p (c s)"), b[:, 0:n],
                                           ACT.Copy).then_inc(hh_ready, 1)
                        elif kind == "y":
                            off, u = turn.unit(pos)
                            act.wait_ge(unit_used, u + 1)
                            for half in range(2):
                                act.activation(yh[:, half * 512:(half + 1) * 512], bank[4 + half][:, :], ACT.Copy,
                                               scale=gslot[:, 0:1]).then_inc(y_hi, 1)
                        elif kind == "x":
                            b = wait_step(turn, ev)
                            act.activation(xeh[:, 2 * i:2 * i + 2, :, :].rearrange("p c a s -> p (c a s)"), b[:, :],
                                           ACT.Copy).then_inc(xe_hi, 1)

            hi(0, cols[0])
            h_final(act, 0, 0)
            for m in range(DC):
                part(0, m)
            for m in range(DC):
                square(0, m)
                if m == 2:
                    hi(1, cols[1])
            for l in range(DEPTH):
                for j in range(10):
                    ahead(U_MIX[l] + j)
                    if j == 0:
                        norm(l, "norm1")
                    if j >= 8:
                        for c in range(2 * (j - 8), 2 * (j - 8) + 2):
                            act.wait_ge(acc_free, A_MIX[l] + 16 + c + 1)
                            act.activation(sg[:, c, :], sg[:, c, :], ACT.Silu).then_inc(silu_g, 1)
                for g in range(PC):
                    i = SIDE[l, f"wp{g}"]
                    act.wait_ge(side_full, i + 1)
                    act.activation(mh[:, g, :], bank[4 + i % 4][:, 0:T], ACT.Copy,
                                   scale=pscale[:, l, g:g + 1]).then_inc(mix_hi, 1)
                for c in range(RC):
                    act.wait_ge(side_free, SIDE[l, f"mu{c}"] + 1)
                    act.activation(osq[:, c, :], oc[:, c, :], ACT.Square).then_inc(osq_ready, 1)
                i = SIDE[l, "va"]
                act.wait_ge(side_full, i + 1)
                act.activation(rvar[:, :], bank[4 + i % 4][0:HEADS, 0:T], ACT.Sqrt, bias=C("eps", HEADS)).then_inc(stdv_ready, 1)
                for c in range(RC):
                    act.wait_ge(side_free, SIDE[l, f"rb{c}"] + 1)
                    act.activation(mh[:, PC + c, :], og[:, c, :], ACT.Copy).then_inc(mix_hi, 1)
                act.wait_ge(side_free, SIDE[l, "bc3"] + 1)
                act.activation(ph[:, :, :].rearrange("p a n -> p (a n)"), pin[:, :, :].rearrange("p a n -> p (a n)"),
                               ACT.Copy).then_inc(ple_hi, 1)
                for j in range(4):
                    if j < 3:
                        ahead(U_WO[l] + j)
                    finish_pair(4 if l else 1, 2 * j)
                    if j == 3:
                        ahead(U_WO[l] + j)
                    if l and j == 2:
                        act.wait_ge(state_out, 128)
                        act.activation(identr[:, :], ident, ACT.Copy).then_inc(identr_ready, 1)
                        for i in (0, 2, 4):
                            token_hi(i)
                if l == 0:
                    act.wait_ge(state_out, 64)
                if l:
                    for i in (1, 3, 5):
                        token_hi(i)
                    act.wait_ge(side_full, SIDE[1, "rt"] + 1)
                    act.wait_ge(moe_zeroed, 2)
                    b = bank[side_bank(1, "rt")]
                    act.activation(rs[:, 0:2], b[:, 0:2], ACT.Sqrt, bias=C("eps")).then_inc(rowstd, 1)
                    act.activation(rs[0:NS, 2:3], b[0:NS, 2:3], ACT.Sqrt, bias=C("eps", NS)).then_inc(rowstd, 1)
                    act.wait_ge(dm_ready, 1)
                    act.activation(w1[:, :], dm[:, :], ACT.Sigmoid)
                    act.activation(w2[:, :], dm[:, :], ACT.Sigmoid, scale=-1.0).then_inc(sig_ready, 1)
                    for i in range(GATHERS):
                        act.wait_ge(tmp_full, i + 3)
                        act.activation(xeh[:, 2 * i:2 * i + 2, :, :].rearrange("p c a s -> p (c a s)"),
                                       bank[6 + i % 2][:, :], ACT.Copy).then_inc(xe_hi, 1)
                    run_turn(Turn("first"))
                    with act.Fori(0, (NE - 2) // 2) as pair:
                        for half in range(2):
                            run_turn(Turn("loop", pair, half))
                    run_turn(Turn("last"))
                    run_turn(Turn("tail"))
                    act.wait_ge(side_free, SIDE_MOE)
                    with act.If(act.value_load(flag[0:1, 0:1], min_val=0, max_val=2 * T) > 0):
                        act.wait_ge(o_mean, 1)
                        act.activation(rstd[:, :], bank[3][:, 0:T], ACT.Sqrt, bias=C("eps")).then_inc(o_std, 1)
                        with act.Fori(0, NE) as e:
                            for i in range(EC):
                                act.wait_ge(o_used, e * OVER_PE + (i + 2))
                                act.activation(osg[:, :], bank[0][:, 0:T], ACT.Silu).then_inc(o_silu, 1)
                        act.wait_ge(o_done, NE * OVER_DVE)
                else:
                    feed_forward()
                for m in range(DC):
                    h_final(act, 5 if l else 2, m)
                    part(5 if l else 2, m)
                ahead(U_PLE[l])
                for j in range(4):
                    if j < 3:
                        ahead(U_PLE[l] + 1 + j)
                    for m in (2 * j, 2 * j + 1):
                        n = A_PLE[l] + 8 + m
                        chunk_full(act, n)
                        if DC * l + m >= 2:
                            act.wait_ge(ge_ready, DC * l + m - 1)
                        act.activation(sgp[:, m % 2, :], bank[n % 4][:, 0:T], ACT.Sigmoid).then_inc(gate_ready, 1)
                    finish_pair(6 if l else 3, 2 * j)
                ahead(U_PLE[l] + 4)
            norm(DEPTH, "norm1")

        @block.vector
        def _(dve):
            steps = 0

            def step(ins):
                nonlocal steps
                steps += 1
                ins.then_inc(dve_step, 1)
                dve.wait_ge(dve_step, steps)

            def lo(off, n, u=None):
                u = off if u is None else u
                dve.wait_ge(hi_ready, u + 1)
                dve.tensor_tensor(wlo[off % SPL][:, 0:n], raw[off % RAW][:, 0:n],
                                  whi[off % SPL][:, 0:n].bitcast(F32), ALU.subtract).then_inc(lo_ready, 1)

            def ahead(u):
                if u + AHEAD < N_UNITS:
                    lo(u + AHEAD, cols[u + AHEAD])

            def finish(stage, m):
                n = PARTS_AT[stage] + m
                dve.wait_ge(part_hi, n + 1)
                if stage in GAIN:
                    dve.scalar_tensor_tensor(out=xl[:, m, :], in0=h[:, m, :], scalar=gains[:, GAIN[stage], m:m + 1],
                                             in1=xh[:, m, :].bitcast(F32), op0=ALU.mult,
                                             op1=ALU.subtract).then_inc(part_lo, 1)
                else:
                    dve.tensor_tensor(ml[:, m, :], h[:, m, :], mh[:, m, :].bitcast(F32), ALU.subtract).then_inc(part_lo, 1)

            def feed_forward():
                for half in range(2):
                    n = Count(half)
                    for i, (kind, c, w, a, full) in enumerate(PART):
                        j = i + AHEAD
                        lo(n.unit + j, part_cols[j % PART_UNITS])
                        if i + half == 0:
                            side_step(0, "norm2")
                        for m in range(w):
                            if m < w - 1:
                                dve.wait_ge(acc_full, n.full + (full + 1))
                            else:
                                dve.wait_ge(unit_used, n.unit + (i + 1))
                            b = bank[(n.chunk + a + m) % 4][:, 0:T]
                            if kind == "gate":
                                dve.tensor_tensor(tg[:, m, :], b, rstd[:, :], ALU.mult).then_inc(acc_free, 1)
                            elif kind == "up":
                                dve.wait_ge(scaled_f, n.hidden + (c + m + 1))
                                dve.tensor_tensor(hv[:, m, :], b, tg[:, m, :], ALU.mult).then_inc(acc_free, 1)
                            else:
                                dve.tensor_tensor(h[:, c, :], h[:, c, :], b, ALU.add).then_inc(acc_free, 1)
                        if kind == "up":
                            for m in range(w):
                                dve.wait_ge(f_hi, n.hidden + (c + m + 1))
                                dve.tensor_tensor(fl[:, c + m, :], hv[:, m, :], fh[:, c + m, :].bitcast(F32),
                                                  ALU.subtract).then_inc(f_lo, 1)

            def side(l, name):
                dve.wait_ge(side_full, SIDE[l, name] + 1)
                return bank[side_bank(l, name)]

            def side_step(l, name):
                if name in ("norm1", "norm2"):
                    dve.wait_ge(std_ready, NORM_ORDER[l, name] + 1)
                    dve.reciprocal(rstd[:, :], rstd[:, :]).then_inc(side_free, 1)
                    dve.wait_ge(side_free, SIDE[l, name] + 1)
                    return
                b = side(l, name)
                if name[:2] in ("rq", "rk"):
                    a, c = int(name[1] == "k"), int(name[2])
                    i = SIDE[l, name]
                    dve.tensor_tensor(rt[:, c % 2, :], b[:, 0:T], C("sin"), ALU.mult).then_inc(side_free, 1)
                    dve.wait_ge(side_free, i + 1)
                    dve.wait_ge(cosed, 8 * l + 4 * a + c + 1)
                    dve.tensor_tensor(qk[:, a, c, :], qk[:, a, c, :], rt[:, c % 2, :], ALU.add).then_inc(roped, 1)
                    return
                if name[:2] == "kt":
                    last = dve.tensor_tensor(kz[:, int(name[2]), :].rearrange("p (a d) -> p a d", a=HEADS),
                                             b[:, :].rearrange("p (a d) -> p a d", a=HEADS),
                                             C("zeta").unsqueeze(2).to_broadcast([P, HEADS, HD]), ALU.mult)
                elif name[:2] == "vt":
                    last = dve.tensor_copy(vpad[:, int(name[2]), :, 0:3:2, :],
                                           b[:, :].rearrange("p (c a e) -> p c a e", c=RC, a=2))
                elif name == "vs":
                    dve.wait_ge(zeroed, 5 * (l + 1))
                    src = b[0:NS, :].rearrange("p (c a e) -> p c a e", c=RC, a=2)
                    dve.tensor_copy(vs2[0:NS, :, :], src[:, :, 0, :])
                    last = dve.tensor_copy(vs2[32:32 + NS, :, :], src[:, :, 1, :])
                elif name[:2] == "sc":
                    hp = int(name[3])
                    last = dve.tensor_tensor(sc[:, hp, :, :], b[:, :].rearrange("p (c n) -> p c n", c=RC),
                                             decay[:, hp, :, :], ALU.mult)
                elif name == "win":
                    last = dve.tensor_tensor(wsum[:, :, PAD + NP:], b[:, 0:PC * NS].rearrange("p (g s) -> p g s", g=PC),
                                             upad[:, :, PAD + NP:], ALU.add)
                elif name == "S1":
                    dve.wait_ge(zeroed, 5 * (l + 1))
                    for hp in range(2):
                        rows = slice(hp * HD, (hp + 1) * HD)
                        last = dve.tensor_copy(sbd[rows, :, rows], b[rows, :].rearrange("p (c n) -> p c n", c=RC)[:, :, rows])
                elif name == "S2":
                    dve.wait_ge(side_free, SIDE[l, "S1"] + 1)
                    for hp in range(2):
                        rows = slice(hp * HD, (hp + 1) * HD)
                        decay_c = C("gchunk")[rows, :].unsqueeze(2).to_broadcast([HD, RC, HD])
                        step(dve.tensor_tensor(s2[rows, :, :], sbd[rows, :, rows], decay_c, ALU.mult))
                        last = dve.tensor_tensor(s2[rows, :, :], s2[rows, :, :],
                                                 b[rows, :].rearrange("p (c n) -> p c n", c=RC)[:, :, rows], ALU.add)
                elif name in ("o0", "o1"):
                    a = int(name[1]) * CH
                    last = dve.tensor_copy(o[:, :, a:a + CH], b[:, :].rearrange("p (c n) -> p c n", c=RC))
                elif name[:2] == "bc":
                    i = int(name[2])
                    if i >= 2:
                        dve.wait_ge(s_ready, 4 * l + i - 1)
                    k = qk[:, 1, :, NP + 2 * i:NP + 2 * i + 2].rearrange("p c s -> p s c")
                    last = dve.tensor_tensor(kv[:, i % 2, :, :, :],
                                             b[:, :].rearrange("p (s c e) -> p s c e", s=2, c=RC),
                                             k.unsqueeze(3).to_broadcast([P, 2, RC, HD]), ALU.mult)
                elif name == "qS":
                    src = b[0:HD, 0:2 * NS * RC].rearrange("p (s c a) -> p a c s", s=NS, c=RC)
                    dve.tensor_copy(o[0:HD, :, NP:T], src[:, 0, :, :])
                    last = dve.tensor_copy(o[HD:P, :, NP:T], src[:, 1, :, :])
                elif name == "tail":
                    dve.wait_ge(s_ready, 4 * (l + 1))
                    last = dve.tensor_copy(utail[:, :], b[0:BUF + NS, :])
                elif name[:2] == "wp":
                    g = int(name[2])
                    dve.wait_ge(mix_hi, 8 * l + g + 1)
                    last = dve.scalar_tensor_tensor(out=ml[:, g, :], in0=b[:, 0:T], scalar=pscale[:, l, g:g + 1],
                                                    in1=mh[:, g, :].bitcast(F32), op0=ALU.mult, op1=ALU.subtract)
                elif name[:2] == "mu":
                    c = int(name[2])
                    if c == 0:
                        dve.wait_ge(side_free, SIDE[l, "qS"] + 1)
                    last = dve.tensor_tensor(oc[:, c, :], o[:, c, :], b[:, 0:T], ALU.subtract)
                elif name == "va":
                    dve.wait_ge(stdv_ready, l + 1)
                    last = dve.reciprocal(rvar[:, :], rvar[:, :])
                elif name[:2] == "rb":
                    c = int(name[2])
                    dve.wait_ge(og_ready, RC * l + c + 1)
                    dve.tensor_tensor(og[:, c, :], og[:, c, :], b[:, 0:T], ALU.mult).then_inc(side_free, 1)
                    if c:
                        mix_part(l, c - 1)
                    return
                last.then_inc(side_free, 1)

            def mix_part(l, c):
                dve.wait_ge(mix_hi, 8 * l + PC + c + 1)
                dve.tensor_tensor(ml[:, PC + c, :], og[:, c, :], mh[:, PC + c, :].bitcast(F32),
                                  ALU.subtract).then_inc(mix_lo, 1)

            def z_chunk(l, c):
                n = A_MIX[l] + c
                chunk_full(dve, n)
                part, i = divmod(c, 4)
                dst = (qk[:, 0, i, :], qk[:, 1, i, :], v[:, i, :], upad[:, i, PAD:PAD + T], sg[:, i, :])[part]
                if part == 1:
                    dve.scalar_tensor_tensor(out=dst, in0=bank[n % 4][:, 0:T], scalar=float(HD) ** -0.5, in1=rstd[:, :],
                                             op0=ALU.mult, op1=ALU.mult).then_inc(acc_free, 1)
                else:
                    dve.tensor_tensor(dst, bank[n % 4][:, 0:T], rstd[:, :], ALU.mult).then_inc(acc_free, 1)

            def pool_diff(l, g):
                dve.wait_ge(wsummed, PC * l + g + 1)
                dve.wait_ge(side_free, SIDE[l, "win"] + 1)
                early = C("early").rearrange("p (g n) -> p g n", g=PC)[:, g, :]
                step(dve.tensor_tensor(wsum[:, g, PAD:2 * PAD], wsum[:, g, PAD:2 * PAD], early, ALU.mult))
                dve.scalar_tensor_tensor(out=wsum[:, g, PAD:], in0=wsum[:, g, PAD:], scalar=1.0 / WINDOWS[g],
                                         in1=upad[:, g, PAD:], op0=ALU.mult, op1=ALU.subtract).then_inc(d_ready, 1)

            def add_h(n, m, src=None):
                if src is None:
                    chunk_full(dve, n)
                    src = bank[n % 4][:, 0:T]
                dve.tensor_tensor(h[:, m, :], h[:, m, :], src, ALU.add).then_inc(acc_free, 1)

            def ple_out(l, m):
                n = A_PLE[l] + m
                chunk_full(dve, n)
                dve.tensor_copy(esb[l][:, m, :], bank[n % 4][:, 0:T]).then_inc(acc_free, 1)

            def token_lo(i):
                j, half = divmod(i, 2)
                w = BLK[j][1]
                b = side(1, f"tr{i}")
                dve.wait_ge(xt_hi, TOKEN_ORDER.index(i) + 1)
                dve.tensor_tensor(xtl[0:w, j, half * 512:(half + 1) * 512], b[0:w, :],
                                  xth[0:w, j, half * 512:(half + 1) * 512].bitcast(F32), ALU.subtract).then_inc(side_free, 1)

            def bc(x):
                return x[:, :].unsqueeze(2).to_broadcast([P, 3, NE])

            def best(src, top, out):
                tie = C("tie").unsqueeze(1).to_broadcast([P, 3, NE])
                step(dve.tensor_reduce(top[:, :], src[:, :, :], AX_X, ALU.max))
                step(dve.tensor_tensor(r["eq"][:, :, :], src[:, :, :], bc(top), ALU.is_equal))
                step(dve.tensor_tensor(r["key"][:, :, :], r["eq"][:, :, :], tie, ALU.mult))
                step(dve.tensor_reduce(kx[:, :], r["key"][:, :, :], AX_X, ALU.max))
                step(dve.tensor_tensor(out[:, :, :], r["key"][:, :, :], bc(kx), ALU.is_equal))

            def route():
                dve.tensor_copy(lgs[:, :], side(1, "lg")[0:NE, 0:T]).then_inc(side_free, 1)
                token_lo(1)
                dve.wait_ge(moe_zeroed, 2)
                b = side(1, "lt")
                for j, w in BLK:
                    last = dve.tensor_copy(r["lg"][0:w, j, :], b[0:w, j * NE:(j + 1) * NE])
                last.then_inc(side_free, 1)
                dve.wait_ge(side_free, SIDE[1, "lt"] + 1)
                best(r["lg"], m1, r["one"])
                step(dve.scalar_tensor_tensor(out=r["lg2"][:, :, :], in0=r["one"][:, :, :], scalar=-3.0e38,
                                              in1=r["lg"][:, :, :], op0=ALU.mult, op1=ALU.add))
                best(r["lg2"], m2, r["two"])
                step(dve.tensor_tensor(r["sel"][:, :, :], r["one"][:, :, :], r["two"][:, :, :], ALU.add))
                dve.tensor_tensor(r["sel"][:, :, :], r["sel"][:, :, :],
                                  C("valid").unsqueeze(2).to_broadcast([P, 3, NE]), ALU.mult).then_inc(routed, 1)
                token_lo(3)
                token_lo(5)
                side(1, "rt")
                dve.wait_ge(rowstd, 2)
                dve.reciprocal(rs[:, :], rs[:, :]).then_inc(side_free, 1)
                b = side(1, "pos")
                step(dve.scalar_tensor_tensor(out=r["t2"][:, :, :], in0=b[:, 0:3 * NE].rearrange("p (a n) -> p a n", a=3),
                                              scalar=1.0, in1=r["sel"][:, :, :], op0=ALU.add, op1=ALU.mult))
                dve.tensor_scalar(r["pos"][:, :, :], r["t2"][:, :, :], -1.0, None, ALU.add).then_inc(side_free, 1)
                dve.wait_ge(side_free, SIDE[1, "pos"] + 1)
                picks(0, 1)
                step(dve.tensor_tensor(dm[:, :], m1[:, :], m2[:, :], ALU.subtract))
                dve.tensor_tensor(dm[:, :], dm[:, :], rs[:, :], ALU.mult).then_inc(dm_ready, 1)

            def gates():
                dve.wait_ge(sig_ready, 1)
                step(dve.tensor_tensor(r["gate"][:, :, :], r["one"][:, :, :], bc(w1), ALU.mult))
                step(dve.tensor_tensor(r["t2"][:, :, :], r["two"][:, :, :], bc(w2), ALU.mult))
                dve.tensor_tensor(r["gate"][:, :, :], r["gate"][:, :, :], r["t2"][:, :, :], ALU.add).then_inc(routed, 1)
                dve.wait_ge(routed, 2)
                step(dve.tensor_scalar(r["key"][:, :, :], r["pos"][:, :, :], float(CAP), None, ALU.is_ge))
                dve.tensor_tensor(r["over"][:, :, :], r["key"][:, :, :], r["gate"][:, :, :], ALU.mult)
                dve.tensor_reduce(over1[:, :], r["key"][:, :, :].rearrange("p a n -> p (a n)"), AX_X, ALU.add).then_inc(over_ready, 1)

            def picks(e, count):
                pos = r["pos"][:, :, e:e + 2] if isinstance(e, int) else r["pos"][:, :, bass.ds(e, 2)]
                dve.tensor_copy(pose[:, :, :], pos).then_inc(pose_ready, 1)
                dve.wait_ge(pose_ready, count)
                dve.tensor_tensor(pick[:, :, :, :].rearrange("p j a n -> p (j a) n"),
                                  C("iota").unsqueeze(1).to_broadcast([P, 6, P]),
                                  pose[:, :, :].rearrange("p j a -> p (j a)").unsqueeze(2).to_broadcast([P, 6, P]),
                                  ALU.is_equal).then_inc(pick_ready, 1)

            def wait_step(turn, ev):
                off, k = turn.step(ev)
                dve.wait_ge(tmp_full, k + 1)
                return bank[6 + off % 2]

            def gathered(i, b, count):
                dve.wait_ge(xe_hi, count)
                dve.tensor_tensor(xel[:, 2 * i:2 * i + 2, :, :].rearrange("p c a s -> p (c a s)"), b[:, :],
                                  xeh[:, 2 * i:2 * i + 2, :, :].rearrange("p c a s -> p (c a s)").bitcast(F32),
                                  ALU.subtract).then_inc(tmp_free, 1)

            def run_turn(turn):
                e = turn.e
                for pos in turn.places():
                    if pos in turn.units:
                        i = turn.at[pos]
                        lo(turn.u_at + i + AHEAD, turn_cols(turn, i + AHEAD), turn.u + i + AHEAD)
                    if turn.kind == "first" and pos == 6:
                        dve.tensor_copy(flag[:, :], side(1, "over")[0:1, 0:1]).then_inc(side_free, 1)
                    if pos % 6 == 3 and pos in turn.units:
                        s = pos // 6
                        n = STEPS[s][1]
                        dve.wait_ge(sgate_ready, e * 3 + (s + 1))
                        b = bank[turn.gate_bank(s) + 1]
                        dve.scalar_tensor_tensor(out=hid[:, 0:n], in0=b[:, 0:n], scalar=rslot[:, turn.slot:turn.slot + 1],
                                                 in1=sgate[:, 0:n], op0=ALU.mult, op1=ALU.mult).then_inc(hid_ready, 1)
                    for ev in turn.events.get(pos, []):
                        kind, i = ev
                        if kind == "t":
                            b = wait_step(turn, ev)
                            n = STEPS[i][1]
                            dve.wait_ge(hh_ready, e * 3 + (i + 1 - 3 * (i == 2)))
                            dve.tensor_tensor(hl[:, 0:n // P, :].rearrange("p c s -> p (c s)"), b[:, 0:n],
                                              hh[:, 0:n // P, :].rearrange("p c s -> p (c s)").bitcast(F32),
                                              ALU.subtract).then_inc(tmp_free, 1)
                        elif kind == "y":
                            for half in range(2):
                                dve.wait_ge(y_hi, e * 2 + (half - 1))
                                dve.scalar_tensor_tensor(out=yl[:, half * 512:(half + 1) * 512], in0=bank[4 + half][:, :],
                                                         scalar=gslot[:, 0:1],
                                                         in1=yh[:, half * 512:(half + 1) * 512].bitcast(F32),
                                                         op0=ALU.mult, op1=ALU.subtract).then_inc(y_lo, 1)
                        elif kind == "s":
                            b = wait_step(turn, ev)
                            dve.tensor_tensor(h[:, i, :], h[:, i, :], b[:, 0:T], ALU.add).then_inc(tmp_free, 1)
                        elif kind == "p":
                            b = wait_step(turn, ev)
                            dve.tensor_copy(pickT[:, :], b[:, 0:T])
                            gate = b[:, 272 + e:273 + e] if isinstance(e, int) else b[:, bass.ds(e + 272, 1)]
                            dve.tensor_copy(gslot[:, :], gate).then_inc(tmp_free, 1)
                        elif kind == "e":
                            for m in range(DC):
                                ple_out(1, m)
                        elif kind == "g":
                            b = wait_step(turn, ev)
                            dve.tensor_copy(rnext[:, i:i + 1], b[:, 0:1]).then_inc(tmp_free, 1)
                        elif kind == "k":
                            picks(e + 1, turn.pair + 2)
                        elif kind == "x":
                            if i == 0:
                                dve.wait_ge(tmp_free, turn.step(("g", 1))[1] + 1)
                                dve.wait_ge(hid_ready, e * 3 + 3)
                                dve.tensor_copy(rslot[:, :], rnext[:, :])
                            gathered(i, wait_step(turn, ev), turn.pair * GATHERS + (GATHERS + i + 1))

            def over_expert(e):
                dve.tensor_copy(ocol[:, :].unsqueeze(2), r["over"][:, :, bass.ds(e, 1)]).then_inc(o_done, 1)
                dve.wait_ge(o_used, e * OVER_PE + 1)
                dve.tensor_copy(orow[:, :], bank[2][:, 0:T]).then_inc(o_done, 1)
                for i in range(EC):
                    dve.wait_ge(o_silu, e * EC + (i + 1))
                    dve.tensor_tensor(ohid[:, i, :], osg[:, :], bank[1][:, 0:T], ALU.mult).then_inc(o_done, 1)
                for m in range(DC):
                    dve.wait_ge(o_used, e * OVER_PE + (EC + m + 2))
                    dve.tensor_tensor(osg[:, :], bank[0][:, 0:T], orow[:, :], ALU.mult).then_inc(o_scaled, 1)
                    dve.wait_ge(o_scaled, e * DC + (m + 1))
                    dve.tensor_tensor(h[:, m, :], h[:, m, :], osg[:, :], ALU.add).then_inc(o_done, 1)

            lo(0, cols[0])
            for m in range(DC):
                finish(0, m)
            lo(1, cols[1])
            for l in range(DEPTH):
                for j in range(10):
                    ahead(U_MIX[l] + j)
                    if j == 0:
                        side_step(l, "norm1")
                    for c in (2 * j, 2 * j + 1):
                        z_chunk(l, c)
                    for name in AFTER[j]:
                        if name == "norm1":
                            continue
                        if name in ("rq0", "wp0"):
                            dve.wait_ge(const_in, 64)
                        if name == "wp0":
                            for g in range(PC):
                                pool_diff(l, g)
                        side_step(l, name)
                    if j == 6:
                        dve.tensor_tensor(qxi[:, :, :], qk[:, 0, :, CH:2 * CH], xi, ALU.mult).then_inc(qxi_ready, 1)
                for name in AFTER[10]:
                    side_step(l, name)
                mix_part(l, RC - 1)
                dve.wait_ge(ple_hi, l + 1)
                dve.tensor_tensor(pl[:, :, :], pin[:, :, :], ph[:, :, :].bitcast(F32), ALU.subtract).then_inc(ple_lo, 1)
                for j in range(4):
                    if j < 3:
                        ahead(U_WO[l] + j)
                    for m in (2 * j, 2 * j + 1):
                        add_h(A_WO[l] + m, m)
                        if l:
                            dve.wait_ge(acc_free, A_WO[1] + m + 1)
                            dve.tensor_scalar(hg[:, m, :], h[:, m, :], gains[:, 3, m:m + 1], None, ALU.mult).then_inc(hg_ready, 1)
                    if l and j == 2:
                        dve.wait_ge(state_out, 128)
                        for i in (0, 2, 4):
                            token_lo(i)
                    if l == 0:
                        for m in (2 * j, 2 * j + 1):
                            finish(1, m)
                        if j == 3:
                            ahead(U_WO[0] + j)
                if l == 0:
                    feed_forward()
                else:
                    route()
                    for a in range(2):
                        dve.wait_ge(tmp_full, a + 1)
                        dve.tensor_copy(rslot[:, a:a + 1], bank[6 + a][:, 0:1]).then_inc(tmp_free, 1)
                    for i in range(GATHERS):
                        dve.wait_ge(tmp_full, i + 3)
                        gathered(i, bank[6 + i % 2], i + 1)
                    ahead(U_WO[1] + 3)
                    gates()
                    run_turn(Turn("first"))
                    with dve.Fori(0, (NE - 2) // 2) as pair:
                        for half in range(2):
                            run_turn(Turn("loop", pair, half))
                    run_turn(Turn("last"))
                    run_turn(Turn("tail"))
                    with dve.If(dve.value_load(flag[0:1, 0:1], min_val=0, max_val=2 * T) > 0):
                        dve.wait_ge(o_std, 1)
                        dve.reciprocal(rstd[:, :], rstd[:, :]).then_inc(o_norm, 1)
                        dve.wait_ge(o_norm, 1)
                        for m in range(DC):
                            dve.tensor_tensor(hg[:, m, :], hg[:, m, :], rstd[:, :], ALU.mult).then_inc(o_norm, 1)
                        with dve.Fori(0, NE) as e:
                            over_expert(e)
                if l:
                    for m in range(DC):
                        finish(5, m)
                    ahead(U_PLE[1])
                else:
                    for m in range(DC):
                        ple_out(0, m)
                        finish(2, m)
                        if m == 3:
                            ahead(U_PLE[0])
                for j in range(4):
                    if j < 3:
                        ahead(U_PLE[l] + 1 + j)
                    for m in (2 * j, 2 * j + 1):
                        dve.wait_ge(ge_ready, DC * l + m + 1)
                        add_h(None, m, esb[l][:, m, :])
                    if l == 0:
                        for m in (2 * j, 2 * j + 1):
                            finish(3, m)
                ahead(U_PLE[l] + 4)
            side_step(DEPTH, "norm1")
            for m in range(DC):
                dve.scalar_tensor_tensor(out=h[:, m, :], in0=h[:, m, :], scalar=gains[:, 4, m:m + 1], in1=rstd[:, :],
                                         op0=ALU.mult, op1=ALU.mult).then_inc(y_ready, 1)

        @block.gpsimd
        def _(pool):
            steps = 0

            def step(ins):
                nonlocal steps
                steps += 1
                ins.then_inc(pool_step, 1)
                pool.wait_ge(pool_step, steps)

            def add_square(stage, m):
                n = SQUARES_AT[stage] + m
                pool.wait_ge(sq_ready, n + 1)
                if m == 0:
                    pool.tensor_copy(ssum[:, :], sq[:, n % 2, :]).then_inc(ss_added, 1)
                else:
                    pool.wait_ge(ss_added, n)
                    pool.tensor_tensor(ssum[:, :], ssum[:, :], sq[:, n % 2, :], ALU.add).then_inc(ss_added, 1)

            def square_sum(stage):
                for m in range(DC):
                    add_square(stage, m)

            def feed_forward():
                for half in range(2):
                    n = Count(half)
                    for f in range(EC):
                        pool.wait_ge(silu_f, n.hidden + (f + 1))
                        pool.tensor_tensor(tg[:, f % 2, :], tg[:, f % 2, :], rstd[:, :], ALU.mult).then_inc(scaled_f, 1)

            square_sum(0)
            for l in range(DEPTH):
                if l:
                    pool.wait_ge(acc_free, A_MIX[l])
                pool.dma_start(S[:, :, :, :], t["state_ret"][l].rearrange("s (c a) d e -> (a d) s c e", a=2)).then_inc(layer_in, 16)
                pool.dma_start(buf[:, :], t["state_pool"][l].rearrange("s r w -> (s r) w")).then_inc(layer_in, 16)
                pool.dma_start(wpool[:, :, :], t["w_pool"][l].rearrange("g c d -> c g d")).then_inc(layer_in, 16)
                pool.dma_start(selb[:, :, :], t["selb"]).then_inc(layer_in, 16)
                pool.dma_start(pin[:, :, :], t["p"][:, l, :, :]).then_inc(layer_in, 16)
                pool.dma_start(t["new_pool_sample"][l][:, 0:BUF - 1, :], t["state_pool"][l][:, 1:BUF, :]).then_inc(pool_kept, 16)
                pool.memset(upad[:, :, 0:PAD], 0.0).then_inc(zeroed, 1)
                pool.memset(sbd[:, :, :], 0.0).then_inc(zeroed, 1)
                pool.memset(vpad[:, :, :, 1, :], 0.0).then_inc(zeroed, 1)
                pool.memset(vs2[:, :, :], 0.0).then_inc(zeroed, 1)
                pool.memset(qm[:, :, :, :], 0.0).then_inc(zeroed, 1)
                pool.wait_ge(const_in, 64)
                for a, name in enumerate(("rq", "rk")):
                    for c in range(RC):
                        pool.wait_ge(side_full, SIDE[l, f"{name}{c}"] + 1)
                        pool.tensor_tensor(qk[:, a, c, :], qk[:, a, c, :], C("cos"), ALU.mult).then_inc(cosed, 1)
                pool.wait_ge(roped, 8 * l + 4)
                pool.wait_ge(zeroed, 5 * (l + 1))
                pool.wait_ge(cosed, 8 * (l + 1))
                for a in range(2):
                    rows = slice(a * HD, (a + 1) * HD)
                    pool.tensor_copy(qm[rows, :, :, a], qk[rows, 0, :, NP:T].rearrange("p c s -> p s c")).then_inc(qm_ready, 1)
                    pool.wait_ge(qm_ready, 2 * l + a + 1)
                pool.wait_ge(layer_in, 80 * (l + 1))
                pool.tensor_tensor(S[:, :, :, :], S[:, :, :, :],
                                   C("gamma").unsqueeze(1).unsqueeze(3).to_broadcast([P, NS, RC, HD]),
                                   ALU.mult).then_inc(s_decayed, 1)
                pool.wait_ge(s_decayed, l + 1)
                for i in range(4):
                    pool.wait_ge(side_free, SIDE[l, f"bc{i}"] + 1)
                    pool.tensor_tensor(S[:, 2 * i:2 * i + 2, :, :], S[:, 2 * i:2 * i + 2, :, :], kv[:, i % 2, :, :, :],
                                       ALU.add).then_inc(s_ready, 1)
                pool.wait_ge(side_full, SIDE[l, "vs"] + 1)
                wtmp = sq[:, :, :].rearrange("p a n -> p (a n)")
                pool.wait_ge(acc_free, A_MIX[l] + 16)
                for g in range(PC):
                    src, width = upad[:, g, :], 1
                    to_tmp = g % 2 == 1
                    while width < WINDOWS[g]:
                        dst = wtmp if to_tmp else wsum[:, g, :]
                        a = 2 * width - 1
                        ins = pool.tensor_tensor(dst[:, a:PAD + NP], src[:, a:PAD + NP], src[:, a - width:PAD + NP - width],
                                                 ALU.add)
                        width *= 2
                        if width == WINDOWS[g]:
                            ins.then_inc(wsummed, 1)
                            pool.wait_ge(wsummed, PC * l + g + 1)
                        else:
                            step(ins)
                        src, to_tmp = dst, not to_tmp
                pool.wait_ge(side_free, SIDE[l, "S2"] + 1)
                pool.dma_start(t["new_ret_prompt"][l, 0].rearrange("(c a) d e -> (a d) c e", a=2), s2[:, :, :]).then_inc(state_out, 16)
                pool.wait_ge(s_ready, 4 * (l + 1))
                pool.dma_start(t["new_ret_sample"][l].rearrange("s (c a) d e -> (a d) s c e", a=2), S[:, :, :, :]).then_inc(state_out, 16)
                pool.wait_ge(side_free, SIDE[l, "tail"] + 1)
                pool.dma_start(t["new_pool_prompt"][l, 0], utail[0:BUF, :]).then_inc(state_out, 16)
                pool.dma_start(t["new_pool_sample"][l][:, BUF - 1, :], utail[BUF:BUF + NS, :]).then_inc(state_out, 16)
                for c in range(RC):
                    pool.wait_ge(side_free, SIDE[l, f"mu{c}"] + 1)
                    pool.wait_ge(silu_g, RC * (l + 1))
                    pool.tensor_tensor(og[:, c, :], oc[:, c, :], sg[:, c, :], ALU.mult).then_inc(og_ready, 1)
                if l:
                    pool.wait_ge(state_out, 128)
                    pool.wait_ge(ple_lo, 2)
                    pool.memset(r["lg"][:, :, :], 0.0).then_inc(moe_zeroed, 1)
                    pool.memset(rs[:, :], 1.0).then_inc(moe_zeroed, 1)
                square_sum(4 if l else 1)
                if l == 0:
                    pool.wait_ge(side_free, SIDE[0, "norm2"] + 1)
                    feed_forward()
                for m in range(DC):
                    pool.wait_ge(acc_free, A_PLE[l] + m + 1)
                    pool.wait_ge(gate_ready, DC * l + m + 1)
                    pool.tensor_tensor(esb[l][:, m, :], esb[l][:, m, :], sgp[:, m % 2, :], ALU.mult).then_inc(ge_ready, 1)
                    if m % 2 and m > 1:
                        add_square(6 if l else 3, m - 3)
                        add_square(6 if l else 3, m - 2)
                add_square(6 if l else 3, DC - 2)
                add_square(6 if l else 3, DC - 1)
            pool.wait_ge(pool_kept, 32)
            pool.wait_ge(state_out, 128)


_OUTS = {"y": [P, DC, T], "new_pool_prompt": [DEPTH, 1, BUF, POOL_W],
         "new_ret_prompt": [DEPTH, 1, HEADS, HD, HD], "new_pool_sample": [DEPTH, NS, BUF, POOL_W],
         "new_ret_sample": [DEPTH, NS, HEADS, HD, HD]}


def kernel(**inputs):
    import concourse.bacc as bacc
    from concourse.bass_utils import run_bass_kernel_spmd

    a = {k: np.asarray(v) for k, v in inputs.items()}

    def columns(prompt, sample, width):
        x = np.concatenate([prompt.reshape(-1, width), sample.reshape(-1, width)])
        return np.ascontiguousarray(x.T.reshape(width // P, P, -1).transpose(1, 0, 2))

    def by_partition(rows):
        return np.ascontiguousarray(rows.reshape(rows.shape[0], -1, P).transpose(2, 0, 1))

    arrays = {
        "x": columns(a["x_prompt"], a["x_sample"], D),
        "p": np.ascontiguousarray(np.stack([columns(a["p_prompt"][l], a["p_sample"][l], PLE) for l in range(DEPTH)], 1)),
        "gains": by_partition(np.concatenate([a["norm1"], a["norm2"], a["final_norm"][None]])),
        "pscale": by_partition(a["pool_scale"]),
        "const": constants(),
        "selb": sample_rows(),
        "hrow": head_rows(),
    }
    for name in ("state_pool", "state_ret", "w_in", "w_pool", "w_o", "ffn_w_gate", "ffn_w_up", "ffn_w_down",
                 "moe_router", "moe_w_gate", "moe_w_up", "moe_w_down", "w_ple", "w_ple_gate"):
        arrays[name] = np.ascontiguousarray(a[name])
    nc = bacc.Bacc("TRN2", target_bir_lowering=False, num_devices=1)
    t = {k: nc.dram_tensor(f"in_{k}", list(x.shape), F32, kind="ExternalInput").ap() for k, x in arrays.items()}
    t |= {k: nc.dram_tensor(f"out_{k}", s, F32, kind="ExternalOutput").ap() for k, s in _OUTS.items()}
    program(nc, t)
    got = run_bass_kernel_spmd(nc, [{f"in_{k}": x for k, x in arrays.items()}], core_ids=[0]).results[0]
    y = got["out_y"].transpose(2, 1, 0).reshape(T, D)
    return (y[:NP].reshape(1, NP, D), y[NP:].reshape(NS, 1, D), got["out_new_pool_prompt"],
            got["out_new_ret_prompt"], got["out_new_pool_sample"], got["out_new_ret_sample"])
```
